# Optimizing a Trainium2 kernel written in Bass

```python
import math
import jax, jax.numpy as jnp
from jax import lax
import numpy as np

D_MODEL = 1024
BATCH = 1
SEQ = 256
DEPTH = 2
DEC_BATCH = 8
DEC_SEQ = 1
PAST_LEN = 2048
PAGE_SIZE = 128

N_HEADS = 16
HEAD_DIM = 64
WINDOWS = (128, 512, 2048)
DILATIONS = (1, 4, 16)
N_DGROUPS = 3
BAND = 128
N_BUCKETS = 32
MAX_DISTANCE = 2048
POOL_WINDOWS = (2, 4, 8, 16)
POOL_CH = D_MODEL // 4
POOL_STATE = max(POOL_WINDOWS) - 1
N_EGROUPS = 4
EXPERTS_PER_GROUP = 4
N_EXPERTS = N_EGROUPS * EXPERTS_PER_GROUP
TOP_K = 2
D_EXPERT = D_MODEL // 2
MOE_BLOCK = 1024
N_ATT = (DEPTH + 1) // 2
N_POOL = DEPTH // 2
RMS_EPS = 1e-6
NEG = -1e30

kernel_name = 'hybrid_dilated_pool_hmoe_step'

def rms_norm(x, g):
    xf = x.astype(jnp.float32)
    y = xf * lax.rsqrt(jnp.mean(xf * xf, axis=-1, keepdims=True) + RMS_EPS) * g.astype(jnp.float32)
    return y.astype(x.dtype)

def t5_bucket(dist):
    max_exact = N_BUCKETS // 2
    df = jnp.maximum(dist, max_exact).astype(jnp.float32)
    large = max_exact + (jnp.log(df / max_exact) / math.log(MAX_DISTANCE / max_exact)
                         * (N_BUCKETS - max_exact)).astype(jnp.int32)
    large = jnp.minimum(large, N_BUCKETS - 1)
    return jnp.where(dist < max_exact, dist, large)

def project_qkv(u, w_qkv, q_gain, k_gain):
    b, t, _ = u.shape
    z = jnp.einsum('btd,df->btf', u, w_qkv).reshape(b, t, N_DGROUPS, 3, N_HEADS, HEAD_DIM)
    q = rms_norm(z[:, :, :, 0], q_gain[:, None, :])
    k = rms_norm(z[:, :, :, 1], k_gain[:, None, :])
    return q, k, z[:, :, :, 2]

def softmax_parts(s, valid):
    s = jnp.where(valid, s, NEG)
    m = jnp.max(s, axis=-1, keepdims=True)
    p = jnp.exp(s - m)
    den = jnp.sum(p, axis=-1)
    return p, den, m[..., 0] + jnp.log(den)

def dilated_band(q, k, v, window, dilation, bias_tab):
    b, s_len, h, e = q.shape
    n_step = window // dilation
    n_sub = -(-s_len // dilation)
    nb = -(-n_sub // BAND)
    lp = nb * BAND
    pad = lp * dilation - s_len

    def to_sub(t):
        t = jnp.pad(t, ((0, 0), (0, pad), (0, 0), (0, 0)))
        return t.reshape(b, lp, dilation, h, e).transpose(0, 2, 1, 3, 4).reshape(b, dilation, nb, BAND, h, e)

    def with_prev(t):
        prev = jnp.pad(t[:, :, :-1], ((0, 0), (0, 0), (1, 0), (0, 0), (0, 0), (0, 0)))
        return jnp.concatenate([prev, t], axis=3)

    def from_sub(t):
        t = t.reshape((b, dilation, lp) + t.shape[4:])
        t = jnp.swapaxes(t, 1, 2)
        return t.reshape((b, lp * dilation) + t.shape[3:])[:, :s_len]

    qs = to_sub(q)
    ks = with_prev(to_sub(k))
    vs = with_prev(to_sub(v))
    qi = jnp.arange(BAND)[:, None]
    kj = jnp.arange(2 * BAND)[None, :]
    step = BAND + qi - kj
    blk = jnp.arange(nb)[:, None, None]
    valid = (step >= 0) & (step <= n_step) & ((blk > 0) | (kj >= BAND))
    bias = bias_tab.astype(jnp.float32)[t5_bucket(jnp.maximum(step, 0) * dilation)]
    sc = jnp.einsum('brnqhe,brnkhe->brnhqk', qs, ks, preferred_element_type=jnp.float32) * (HEAD_DIM ** -0.5)
    sc = sc + jnp.transpose(bias, (2, 0, 1))
    p, den, lse = softmax_parts(sc, valid[:, None])
    o = jnp.einsum('brnhqk,brnkhe->brnqhe', p, vs.astype(jnp.float32)) / jnp.moveaxis(den, 3, 4)[..., None]
    return from_sub(o), from_sub(jnp.moveaxis(lse, 3, 4))

def dilated_gather(q, k_ext, v_ext, buf_len, window, dilation, bias_tab):
    t_new = q.shape[1]
    n_step = window // dilation
    steps = jnp.arange(n_step + 1)
    idx = buf_len + jnp.arange(t_new)[:, None] - steps[None, :] * dilation
    valid = idx >= 0
    idx = jnp.maximum(idx, 0)
    kg = k_ext[:, idx]
    vg = v_ext[:, idx]
    bias = bias_tab.astype(jnp.float32)[t5_bucket(steps * dilation)].T
    sc = jnp.einsum('bthe,btmhe->bhtm', q, kg, preferred_element_type=jnp.float32) * (HEAD_DIM ** -0.5)
    sc = sc + bias[:, None, :]
    p, den, lse = softmax_parts(sc, valid)
    o = jnp.einsum('bhtm,btmhe->bthe', p, vg.astype(jnp.float32)) / jnp.swapaxes(den, 1, 2)[..., None]
    return o, jnp.swapaxes(lse, 1, 2)

def merge_groups(outs, lses):
    w = jax.nn.softmax(jnp.stack(lses), axis=0)
    return jnp.sum(w[..., None] * jnp.stack(outs), axis=0)

def attn_prompt(u, w_qkv, q_gain, k_gain, w_o, rel_bias):
    b, t, _ = u.shape
    q, k, v = project_qkv(u, w_qkv, q_gain, k_gain)
    outs, lses, new_kv = [], [], []
    for g, (win, dil) in enumerate(zip(WINDOWS, DILATIONS)):
        tab = rel_bias[:, g * N_HEADS:(g + 1) * N_HEADS]
        o, l = dilated_band(q[:, :, g], k[:, :, g], v[:, :, g], win, dil, tab)
        outs.append(o)
        lses.append(l)
        keep = min(win, t)
        new_kv.append(jnp.stack([k[:, t - keep:, g], v[:, t - keep:, g]], axis=2))
    o = merge_groups(outs, lses).reshape(b, t, N_HEADS * HEAD_DIM).astype(u.dtype)
    return jnp.einsum('btf,fd->btd', o, w_o), new_kv

def attn_sample(u, bufs, w_qkv, q_gain, k_gain, w_o, rel_bias):
    b, t, _ = u.shape
    q, k, v = project_qkv(u, w_qkv, q_gain, k_gain)
    outs, lses, new_kv = [], [], []
    for g, (win, dil) in enumerate(zip(WINDOWS, DILATIONS)):
        buf = bufs[g]
        buf_len = buf.shape[1]
        k_ext = jnp.concatenate([buf[:, :, 0], k[:, :, g].astype(buf.dtype)], axis=1)
        v_ext = jnp.concatenate([buf[:, :, 1], v[:, :, g].astype(buf.dtype)], axis=1)
        tab = rel_bias[:, g * N_HEADS:(g + 1) * N_HEADS]
        o, l = dilated_gather(q[:, :, g], k_ext, v_ext, buf_len, win, dil, tab)
        outs.append(o)
        lses.append(l)
        new_kv.append(jnp.stack([k_ext[:, -buf_len:], v_ext[:, -buf_len:]], axis=2))
    o = merge_groups(outs, lses).reshape(b, t, N_HEADS * HEAD_DIM).astype(u.dtype)
    return jnp.einsum('btf,fd->btd', o, w_o), new_kv

def pool_mix(u_ext, n_out, w, bias, scale):
    bsz, length, _ = u_ext.shape
    uf = u_ext.astype(jnp.float32)
    cs = jnp.concatenate([jnp.zeros_like(uf[:, :1]), jnp.cumsum(uf, axis=1)], axis=1)
    e = jnp.arange(length - n_out, length)
    parts = []
    for gi, win in enumerate(POOL_WINDOWS):
        sl = slice(gi * POOL_CH, (gi + 1) * POOL_CH)
        cg = cs[:, :, sl]
        total = cg[:, e + 1] - cg[:, jnp.maximum(e + 1 - win, 0)]
        cnt = jnp.minimum(win, e + 1).astype(jnp.float32)
        parts.append(total / cnt[None, :, None] - uf[:, length - n_out:, sl])
    z = jnp.stack(parts, axis=2)
    y = jnp.einsum('bngc,gcf->bngf', z, w.astype(jnp.float32)).reshape(bsz, n_out, D_MODEL)
    y = (y + bias.astype(jnp.float32)) * scale.astype(jnp.float32)
    return y.astype(u_ext.dtype)

def route(u, wgr, bgr, wer, ber):
    uf = u.astype(jnp.float32)
    pg = jax.nn.softmax(uf @ wgr.astype(jnp.float32) + bgr.astype(jnp.float32), axis=-1)
    gi = jnp.argmax(pg, axis=-1)
    gw = jnp.max(pg, axis=-1)
    le = (uf @ wer.astype(jnp.float32) + ber.astype(jnp.float32)).reshape(-1, N_EGROUPS, EXPERTS_PER_GROUP)
    le_sel = jnp.take_along_axis(le, gi[:, None, None], axis=1)[:, 0]
    tv, ti = lax.top_k(le_sel, TOP_K)
    pw = jax.nn.softmax(tv, axis=-1) * gw[:, None]
    eid = gi[:, None] * EXPERTS_PER_GROUP + ti
    return jnp.sum(jax.nn.one_hot(eid, N_EXPERTS, dtype=jnp.float32) * pw[..., None], axis=1)

def moe_ffn(h, g_norm, wgr, bgr, wer, ber, wg, wu, wd):
    b, t, d = h.shape
    n = b * t
    u = rms_norm(h, g_norm).reshape(n, d)
    gates = route(u, wgr, bgr, wer, ber).astype(u.dtype)

    def experts(args):
        ub, gb = args
        a = jnp.einsum('td,edf->tef', ub, wg)
        c = jnp.einsum('td,edf->tef', ub, wu)
        hh = jax.nn.silu(a) * c * gb[:, :, None]
        return jnp.einsum('tef,efd->td', hh, wd)

    if n > MOE_BLOCK and n % MOE_BLOCK == 0:
        out = lax.map(experts, (u.reshape(-1, MOE_BLOCK, d), gates.reshape(-1, MOE_BLOCK, N_EXPERTS))).reshape(n, d)
    else:
        out = experts((u, gates))
    return h + out.reshape(b, t, d).astype(h.dtype)

def setup_inputs(seed: int = 0) -> dict:
    key = jax.random.key(seed)
    ks = jax.random.split(key, 24)

    def nrm(k, shape, s=1.0):
        return s * jax.random.normal(k, shape, jnp.float32)

    def gain(k, shape):
        return 1.0 + 0.02 * jax.random.normal(k, shape, jnp.float32)

    qkv_cols = N_DGROUPS * 3 * N_HEADS * HEAD_DIM
    hd = N_HEADS * HEAD_DIM
    return {
        'x_prompt': nrm(ks[0], (BATCH, SEQ, D_MODEL)),
        'x_sample': nrm(ks[1], (DEC_BATCH, DEC_SEQ, D_MODEL)),
        'cache_kv_w128': nrm(ks[2], (N_ATT, DEC_BATCH, min(WINDOWS[0], PAST_LEN), 2, N_HEADS, HEAD_DIM)),
        'cache_kv_w512': nrm(ks[3], (N_ATT, DEC_BATCH, min(WINDOWS[1], PAST_LEN), 2, N_HEADS, HEAD_DIM)),
        'cache_kv_w2048': nrm(ks[4], (N_ATT, DEC_BATCH, min(WINDOWS[2], PAST_LEN), 2, N_HEADS, HEAD_DIM)),
        'state_pool': nrm(ks[5], (N_POOL, DEC_BATCH, POOL_STATE, D_MODEL)),
        'w_qkv': nrm(ks[6], (N_ATT, D_MODEL, qkv_cols), D_MODEL ** -0.5),
        'q_norm': gain(ks[7], (N_ATT, N_DGROUPS, HEAD_DIM)),
        'k_norm': gain(ks[8], (N_ATT, N_DGROUPS, HEAD_DIM)),
        'w_o': nrm(ks[9], (N_ATT, hd, D_MODEL), hd ** -0.5),
        'rel_bias': nrm(ks[10], (N_BUCKETS, N_DGROUPS * N_HEADS), 0.1),
        'attn_norm': gain(ks[11], (N_ATT, D_MODEL)),
        'pool_norm': gain(ks[12], (N_POOL, D_MODEL)),
        'pool_w': nrm(ks[13], (N_POOL, len(POOL_WINDOWS), POOL_CH, POOL_CH), POOL_CH ** -0.5),
        'pool_b': nrm(ks[14], (N_POOL, D_MODEL), 0.01),
        'pool_scale': gain(ks[15], (N_POOL, D_MODEL)),
        'ffn_norm': gain(ks[16], (DEPTH, D_MODEL)),
        'router_group_w': nrm(ks[17], (DEPTH, D_MODEL, N_EGROUPS), D_MODEL ** -0.5),
        'router_group_b': nrm(ks[18], (DEPTH, N_EGROUPS), 0.01),
        'router_expert_w': nrm(ks[19], (DEPTH, D_MODEL, N_EXPERTS), D_MODEL ** -0.5),
        'router_expert_b': nrm(ks[20], (DEPTH, N_EXPERTS), 0.01),
        'w_gate': nrm(ks[21], (DEPTH, N_EXPERTS, D_MODEL, D_EXPERT), D_MODEL ** -0.5),
        'w_up': nrm(ks[22], (DEPTH, N_EXPERTS, D_MODEL, D_EXPERT), D_MODEL ** -0.5),
        'w_down': nrm(ks[23], (DEPTH, N_EXPERTS, D_EXPERT, D_MODEL), D_EXPERT ** -0.5),
    }

def reference(x_prompt, x_sample, cache_kv_w128, cache_kv_w512, cache_kv_w2048, state_pool,
              w_qkv, q_norm, k_norm, w_o, rel_bias, attn_norm, pool_norm, pool_w, pool_b,
              pool_scale, ffn_norm, router_group_w, router_group_b, router_expert_w,
              router_expert_b, w_gate, w_up, w_down):
    hp, hs = x_prompt, x_sample
    kv_p = [[], [], []]
    kv_s = [[], [], []]
    pool_p, pool_s = [], []
    for i in range(DEPTH):
        if i % 2 == 0:
            a = i // 2
            up = rms_norm(hp, attn_norm[a])
            us = rms_norm(hs, attn_norm[a])
            yp, newp = attn_prompt(up, w_qkv[a], q_norm[a], k_norm[a], w_o[a], rel_bias)
            ys, news = attn_sample(us, (cache_kv_w128[a], cache_kv_w512[a], cache_kv_w2048[a]),
                                   w_qkv[a], q_norm[a], k_norm[a], w_o[a], rel_bias)
            for g in range(N_DGROUPS):
                kv_p[g].append(newp[g])
                kv_s[g].append(news[g])
        else:
            p = i // 2
            up = rms_norm(hp, pool_norm[p])
            us = rms_norm(hs, pool_norm[p])
            yp = pool_mix(up, up.shape[1], pool_w[p], pool_b[p], pool_scale[p])
            pool_p.append(up[:, -POOL_STATE:])
            u_ext = jnp.concatenate([state_pool[p].astype(us.dtype), us], axis=1)
            ys = pool_mix(u_ext, us.shape[1], pool_w[p], pool_b[p], pool_scale[p])
            pool_s.append(u_ext[:, -POOL_STATE:])
        hp = hp + yp
        hs = hs + ys
        hp = moe_ffn(hp, ffn_norm[i], router_group_w[i], router_group_b[i], router_expert_w[i],
                     router_expert_b[i], w_gate[i], w_up[i], w_down[i])
        hs = moe_ffn(hs, ffn_norm[i], router_group_w[i], router_group_b[i], router_expert_w[i],
                     router_expert_b[i], w_gate[i], w_up[i], w_down[i])
    new_kv_w128_prompt = jnp.stack(kv_p[0])
    new_kv_w512_prompt = jnp.stack(kv_p[1])
    new_kv_w2048_prompt = jnp.stack(kv_p[2])
    new_pool_prompt = jnp.stack(pool_p)
    new_kv_w128_sample = jnp.stack(kv_s[0])
    new_kv_w512_sample = jnp.stack(kv_s[1])
    new_kv_w2048_sample = jnp.stack(kv_s[2])
    new_pool_sample = jnp.stack(pool_s)
    return (hp, hs, new_kv_w128_prompt, new_kv_w512_prompt, new_kv_w2048_prompt, new_pool_prompt,
            new_kv_w128_sample, new_kv_w512_sample, new_kv_w2048_sample, new_pool_sample)


_drawn_inputs = setup_inputs


def setup_inputs(seed=0):
    import zlib

    import numpy as np

    out = dict(_drawn_inputs(seed))
    spreads = {}
    factors = {'q_norm': 3.537,
     'k_norm': 3.595,
     'attn_norm': 2.818,
     'pool_b': 4.857,
     'pool_scale': 11.793,
     'router_expert_b': 19.989,
     'pool_norm': 2.909,
     'ffn_norm': 5.045,
     'router_group_b': 8.0}
    for name, (base, spread) in spreads.items():
        noise = np.random.default_rng([zlib.crc32(name.encode()), seed]).standard_normal(out[name].shape)
        drawn = base * np.exp(spread * noise) if base else spread * noise
        out[name] = __import__('jax').numpy.asarray(drawn.astype(out[name].dtype))
    for name, factor in factors.items():
        out[name] = (out[name] * factor).astype(out[name].dtype)
    return out
```

```python
from contextlib import ExitStack

import concourse.bass as bass
from concourse import mybir

ALU = mybir.AluOpType
ACT = mybir.ActivationFunctionType
F32 = mybir.dt.float32
AX_X = mybir.AxisListType.X
ds = bass.ds

P = 128
DILATIONS = (1, 4, 16)
WINDOWS = (128, 512, 2048)
POOL_WINDOWS = (2, 4, 8, 16)
NEG = -1e30
RMS_EPS = 1e-6


class Chain:

    def __init__(self, eng, sem):
        self.eng, self.sem, self.base, self.k, self.i, self.per = eng, sem, 0, 0, 0, 0

    def __call__(self, instruction):
        instruction.then_inc(self.sem, 1)
        self.k += 1
        self.eng.wait_ge(self.sem, self.i * self.per + (self.base + self.k))

    def enter(self, i, per, first=0):
        self.base += self.k - first * per
        self.k, self.i, self.per = 0, i, per

    def leave(self, end):
        assert self.k == self.per, (self.k, self.per)
        self.base += end * self.per
        self.k, self.i, self.per = 0, 0, 0


def build(nc, x_prompt, x_sample, cache_w128, cache_w512, cache_w2048, state_pool, w_qkv, q_norm,
          k_norm, w_o, rel_bias, attn_norm, pool_norm, pool_w, pool_b, pool_scale, ffn_norm,
          router_group_w, router_group_b, router_expert_w, router_expert_b, w_gate, w_up, w_down,
          c_ident, c_bucket_prompt, c_bucket_sample, c_same_batch, c_rank, c_inv_count, c_state_sum,
          y_prompt, y_sample, kv128_p, kv512_p, kv2048_p, pool_p, kv128_s, kv512_s, kv2048_s, pool_s):
    _, SEQ, D = x_prompt.shape
    NS = x_sample.shape[0]
    T = SEQ + NS
    KT = D // P
    G = len(WINDOWS)
    NB, GH = rel_bias.shape
    H = GH // G
    HD = D // H
    PAIRS = H // 2
    BH = NS * H
    NE = w_gate.shape[1]
    FT = w_gate.shape[3] // P
    NG = router_group_w.shape[2]
    EPG = NE // NG
    NR = NG + NE
    LAYERS = w_gate.shape[0]
    STATE = state_pool.shape[2]
    BV = 3 * P
    CW = 512
    SLOT = KT * CW
    TPC = CW // P
    NZ = 3 * KT
    NQK = 2 * KT
    CHUNKS = G * NZ // TPC
    caches = (cache_w128, cache_w512, cache_w2048)
    kv_p, kv_s = (kv128_p, kv512_p, kv2048_p), (kv128_s, kv512_s, kv2048_s)
    HALF = NS // 2
    assert SEQ == 2 * P and BH == P and KT * P == D and LAYERS == 2 and NZ // TPC == 6

    qkvs_dram = nc.dram_tensor("qkv_of_samples", [NS, G, 3, D], F32, kind="Internal").ap()
    bias_dram = nc.dram_tensor("bias_by_distance", [H, G, BV], F32, kind="Internal").ap()

    with ExitStack() as ctx:
        def sb(name, shape):
            return ctx.enter_context(nc.sbuf_tensor(name, shape, F32))

        def sem(name):
            return ctx.enter_context(nc.semaphore(name))

        ring_lo = sb("ring_lo", [P, 4 * SLOT])
        hT = sb("hT", [P, KT, T])
        uT = sb("uT", [P, KT, T])
        oT = uT
        region_a = sb("region_a", [P, G * 2 * KT * T + 2 * G * D])
        scratch = sb("scratch", [P, 10752])
        ident = sb("ident", [P, P])
        ones = sb("ones", [P, P])
        blockones = sb("blockones", [P, P])
        epsc = sb("epsc", [P, 1])
        NVEC = 6 * KT + 2 * G
        vec_rows = sb("vec_rows", [NVEC, P])
        vecs = sb("vecs", [P, NVEC])
        gains = sb("gains", [P, 2])
        bucket_s = sb("bucket_s", [NB, G, P + 1])
        tab = sb("tab", [NB + 1, GH])
        tabrep = sb("tabrep", [NB, G, NS, H])
        same_batch = sb("same_batch", [BH, NS])
        rank = sb("rank", [P, NE])
        wr = sb("wr", [P, LAYERS, KT, NR])
        brow = sb("brow", [1, LAYERS, NR])
        rstd = sb("rstd", [P, 2, T])
        small = sb("small", [P, 64])

        def slot(s):
            if s < 4:
                return ring_lo[:, s * SLOT:(s + 1) * SLOT]
            return region_a[:, (s - 4) * SLOT:(s - 3) * SLOT]

        qk = region_a[:, 0:G * 2 * KT * T].rearrange("p (g w k t) -> p g w k t", g=G, w=2, k=KT)
        v_tok = region_a[:, G * 2 * KT * T:].rearrange("p (b g c) -> p b g c", b=2, g=G)

        def cut(start, shape, region=scratch):
            n = 1
            for s in shape:
                n *= s
            assert start + n <= region.shape[1], (start, n)
            names = "abcd"[:len(shape)]
            v = region[:, start:start + n]
            if len(shape) > 1:
                v = v.rearrange(f"p ({' '.join(names)}) -> p {' '.join(names)}",
                                **{c: s for c, s in zip(names, shape)})
            return v

        x_tok = cut(0, (3, D))
        sq = cut(4352, (KT, T))
        bucket_p = cut(6528, (G, BV))
        bias_rows = cut(7680, (G, BV))
        zn = cut(0, (4, T))
        zsq = cut(4 * T, (2, T))
        zr = cut(6 * T, (2, T))
        zri = cut(8 * T, (2, T))
        k_tok = cut(8832, (D,)), cut(3072, (D,))
        qkv_s = cut(4352, (3, D))
        q_rep = cut(0, (3, D))
        prod = cut(3072, (2, D))
        s_keys = cut(5120, (G, BH))
        s_rows = cut(5504, (G, P + 1))
        p_keys = cut(5904, (G, BH))
        qk_new = cut(6288, (2, G, HD))
        qk_prod = cut(6672, (G, HD))
        p_newm = cut(6864, (G, NS))
        p_newT = cut(6888, (G, BH))
        v_new = cut(7296, (G, D))
        o_new = cut(10368, (KT, NS, 2))
        q_st = cut(0, (2, G, SEQ))
        k_st = cut(1536, (2, G, SEQ))
        v_st = cut(3072, (2, 2, G * P))
        bias_t = cut(4608, (2, G, SEQ))
        probs = cut(6144, (2, 9 * P))
        probsT = cut(8448, (2, 9 * P))
        silu = cut(0, (2, T))
        act = cut(2 * T, (2, T))
        hid = cut(4 * T, (FT, T))
        gate_bc = cut(8 * T, (T,))
        gatesT = cut(9 * T, (T,))
        gate_one = cut(10 * T, (T,))
        logits = cut(11 * T, (3, NR))
        rt = cut(11 * T + 64, (16, 3, NE))
        y_tok = cut(0, (3, D))
        PAD = POOL_WINDOWS[-1]
        A0 = 2 * SLOT
        pw = cut(A0, (KT, D // 4), region_a)
        inv_count = cut(A0 + 2048, (4, SEQ), region_a)
        state = cut(A0 + 3072, (D,), region_a)
        state_sum = cut(A0 + 4096, (4, NS), region_a)
        ext = cut(A0 + 4128, (2, 2, PAD + SEQ), region_a)
        pool_z = cut(A0 + 5216, (KT, T), region_a)
        pool_tok = cut(A0 + 7328, (D,), region_a)
        ybuf = cut(A0 + 8352, (2, T), region_a)
        zs_tmp = cut(A0 + 8880, (2, NS), region_a)

        bank = [ctx.enter_context(nc.psum_tensor(f"bank{n}", [P, 512], F32)) for n in range(8)]

        x_landed, consts_landed, vecs_landed = sem("x_landed"), sem("consts_landed"), sem("vecs_landed")
        cache_copied = sem("cache_copied")
        ring_full = [sem(f"ring_full{n}") for n in range(6)]
        dve_own, act_own = sem("dve_own"), sem("act_own")
        setup_done, vecs_turned, bias_made = sem("setup_done"), sem("vecs_turned"), sem("bias_made")
        bias_copied, bias_stored = sem("bias_copied"), sem("bias_stored")
        x_turned, h_filled = sem("x_turned"), sem("h_filled")
        squares_ready, sums_ready = sem("squares_ready"), sem("sums_ready")
        root_ready, u_ready = sem("root_ready"), sem("u_ready")
        z_ready, zsq_ready, zsum_ready = sem("z_ready"), sem("zsq_ready"), sem("zsum_ready")
        zroot_ready, zn_ready, zn_kept = sem("zroot_ready"), sem("zn_ready"), sem("zn_kept")
        z_turned, z_stored, tokens_sent = sem("z_turned"), sem("z_stored"), sem("tokens_sent")
        q_rep_landed = [sem(f"q_rep_landed{n}") for n in range(3)]
        qk_new_landed, v_new_landed = sem("qk_new_landed"), sem("v_new_landed")
        prod_ready, s_keys_ready, s_turned = sem("prod_ready"), sem("s_keys_ready"), sem("s_turned")
        s_rows_ready, s_exp_ready, p_ready = sem("s_rows_ready"), sem("s_exp_ready"), sem("p_ready")
        p_turned, p_keys_ready = sem("p_turned"), sem("p_keys_ready")
        pv_s_ready, sample_done = sem("pv_s_ready"), sem("sample_done")
        staged = sem("staged")
        bias_landed = [sem(f"bias_landed{n}") for n in range(2)]
        scores_ready, biased, exps_ready = sem("scores_ready"), sem("biased"), sem("exps_ready")
        inv_ready, probs_ready, pt_ready = sem("inv_ready"), sem("probs_ready"), sem("pt_ready")
        pt_copied_dve, pt_copied_act = sem("pt_copied_dve"), sem("pt_copied_act")
        pv_ready, o_copied = sem("pv_ready"), sem("o_copied")
        wo_ready, wo_added = sem("wo_ready"), sem("wo_added")
        logits_made, router_arg, router_exp = sem("logits_made"), sem("router_arg"), sem("router_exp")
        gates_ready, gates_turned, gate_one_ready = sem("gates_ready"), sem("gates_turned"), sem("gate_one_ready")
        gate_bc_made, gate_bc_ready = sem("gate_bc_made"), sem("gate_bc_ready")
        up_ready, silu_ready, act_ready = sem("up_ready"), sem("silu_ready"), sem("act_ready")
        hid_ready, down_ready, down_added = sem("hid_ready"), sem("down_ready"), sem("down_added")
        pool_landed, state_summed, pooled = sem("pool_landed"), sem("state_summed"), sem("pooled")
        pool_y_ready, pool_y_added = sem("pool_y_ready"), sem("pool_y_added")
        pool_turned, pool_tok_ready, pool_sent = sem("pool_turned"), sem("pool_tok_ready"), sem("pool_sent")
        y_turned, y_ready, y_sent = sem("y_turned"), sem("y_ready"), sem("y_sent")
        block = ctx.enter_context(nc.Block())

        ATTN_G, POOL_G, FFN_G, POOL_B, POOL_S = 0, KT, (2 * KT, 3 * KT), 4 * KT, 5 * KT
        QK_G = 6 * KT
        N_CONSTS = 11
        N_VECS = 5 + 4 * G
        SENT_PER_G = 4
        RING_KV = CHUNKS // 3
        RING_WO = RING_KV + 4

        qkv_chunks = w_qkv[0].rearrange("(k p) (c n) -> c p k n", p=P, n=CW)
        kv_strided = [c[0].rearrange("(x b) (s d) w h e -> x w s b d (h e)", b=HALF, d=d)[:, :, :, :, 0, :]
                      for c, d in zip(caches, DILATIONS)]
        expert_w = (w_gate.rearrange("l e (k p) f -> (l e) p k f", p=P),
                    w_up.rearrange("l e (k p) f -> (l e) p k f", p=P),
                    w_down.rearrange("l e (k p) f -> (l e) p k f", p=P))
        SLOTS = ((2, 3, 4), (5, 0, 1))
        FIRST_USES = (RING_WO + 1, RING_WO + 1, RING_WO, 0, 0, 0)

        def norm_sums(pe, n):
            pe.wait_ge(squares_ready, n + 1)
            for k in range(KT):
                last = nc.tensor.matmul(bank[7][:, 0:T], ones[:], sq[:, k, :], start=(k == 0), stop=(k == KT - 1))
            last.then_inc(sums_ready, 1)

        def norm_root(act_e, n, h_done, count):
            act_e.wait_ge(h_done, count)
            nc.scalar.activation(sq[:, :, :], hT[:], ACT.Square).then_inc(squares_ready, 1)
            act_e.wait_ge(sums_ready, n + 1)
            nc.scalar.activation(rstd[:, 0, :], bank[7][:, 0:T], ACT.Sqrt, bias=epsc[:, 0:1], scale=1.0 / D).then_inc(root_ready, 1)

        def norm_apply(dve, chain, n, gain):
            dve.wait_ge(root_ready, n + 1)
            chain(nc.vector.reciprocal(rstd[:, 1, :], rstd[:, 0, :]))
            for k in range(KT):
                last = nc.vector.scalar_tensor_tensor(out=uT[:, k, :], in0=hT[:, k, :], scalar=vecs[:, gain + k:gain + k + 1],
                                                      in1=rstd[:, 1, :], op0=ALU.mult, op1=ALU.mult)
            last.then_inc(u_ready, 1)

        @block.sync
        def _(sp):
            sp.dma_start(x_tok[:, 0:2, :], x_prompt[0].rearrange("(b p) c -> p b c", p=P)).then_inc(x_landed, 16)
            sp.dma_start(x_tok[0:NS, 2, :], x_sample[:, 0, :]).then_inc(x_landed, 16)
            for c in range(3):
                sp.dma_start(slot(c).rearrange("p (k n) -> p k n", k=KT), qkv_chunks[c]).then_inc(ring_full[c], 16)
            with sp.Fori(1, CHUNKS // 3) as r:
                for c in range(3):
                    sp.wait_ge(z_ready, r * (3 * TPC) + (c - 2) * TPC)
                    sp.dma_start(slot(c).rearrange("p (k n) -> p k n", k=KT),
                                 qkv_chunks[ds(r * 3 + c, 1)].rearrange("a p k n -> p (a k) n")).then_inc(ring_full[c], 16)
            for w in range(2):
                for half in range(2):
                    for g in range(G):
                        if w == 0 and half == 0:
                            sp.wait_ge(z_ready, G * NZ)
                        elif (w, half) < (1, 1):
                            sp.wait_ge(prod_ready, ((w * 2 + half - 1) * G + g + 1) * HALF)
                        else:
                            sp.wait_ge(pv_s_ready, 1)
                        sp.dma_start(slot(g).rearrange("p (b c) -> p b c", b=HALF), kv_strided[g][half, w]).then_inc(ring_full[g], 16)
            sp.wait_ge(pv_s_ready, 2)
            for s in range(2):
                sp.dma_start(slot(s).rearrange("p (k n) -> p k n", k=KT // 2),
                             w_o[0].rearrange("(s k p) n -> s p k n", p=P, s=2)[s]).then_inc(ring_full[s], 16)

            def expert(e, odd, what):
                s = SLOTS[odd][what]
                src = expert_w[what]
                src = src[e] if isinstance(e, int) else src[ds(e, 1)].rearrange("a p k f -> p (a k) f")
                sp.dma_start(slot(s).rearrange("p (k f) -> p k f", k=FT if what == 2 else KT), src).then_inc(ring_full[s], 16)

            expert(0, 0, 0)
            expert(0, 0, 1)
            sp.wait_ge(bias_stored, 16)
            sp.wait_ge(sample_done, 1)

            def bias_load(h, b):
                sp.dma_start(bias_t[:, b], bass.AP(tensor=bias_dram.tensor, offset=h * (G * BV),
                                                   ap=[[1, P], [BV, G], [1, SEQ]])).then_inc(bias_landed[b], 16)

            for b in range(2):
                bias_load(b, b)
            with sp.Fori(1, PAIRS) as r:
                for b in range(2):
                    sp.wait_ge(biased, r * 2 + b - 1)
                    bias_load(r * 2 + b, b)
            sp.wait_ge(staged, 3 * PAIRS)
            expert(0, 0, 2)
            expert(1, 1, 0)
            sp.wait_ge(wo_ready, KT)
            expert(1, 1, 1)
            expert(1, 1, 2)
            with sp.Fori(1, LAYERS * NE // 2) as r:
                for odd in range(2):
                    for what in range(3):
                        if what < 2:
                            sp.wait_ge(up_ready, r * (2 * FT) + (odd - 1) * FT)
                        else:
                            sp.wait_ge(down_ready, r * (2 * KT) + (odd - 1) * KT)
                        expert(r * 2 + odd, odd, what)
            for b in range(3):
                sp.wait_ge(y_ready, 2 * (b + 1))
                if b < 2:
                    sp.dma_start(y_prompt[0, b * P:(b + 1) * P, :], y_tok[:, b, :]).then_inc(y_sent, 16)
                else:
                    sp.dma_start(y_sample[:, 0, :], y_tok[0:NS, b, :]).then_inc(y_sent, 16)
            sp.wait_ge(y_sent, 48)

        @block.gpsimd
        def _(pool):
            n_copies = 0
            for src, dst in zip(caches, kv_s):
                row = 2 * D
                m = (src.shape[2] - 1) * row
                a = src[0].rearrange("b l w h e -> b (l w h e)")
                o = dst[0].rearrange("b l w h e -> b (l w h e)")
                for b in range(NS):
                    pool.dma_start(o[b, 0:m].rearrange("(x y) -> x y", x=16),
                                   a[b, row:row + m].rearrange("(x y) -> x y", x=16)).then_inc(cache_copied, 16)
                    n_copies += 1
            pool.dma_start(pool_s[0, :, 0:STATE - 1, :].rearrange("b s c -> b (s c)"),
                           state_pool[0, :, 1:STATE, :].rearrange("b s c -> b (s c)")).then_inc(cache_copied, 16)
            n_copies += 1

            for g in range(G):
                for n in range(NQK):
                    pool.wait_ge(zn_ready, g * NZ + n + 1)
                    nc.gpsimd.tensor_copy(qk[:, g, n // KT, n % KT, :], zn[:, n % 4, :]).then_inc(zn_kept, 1)
                pool.wait_ge(z_stored, (g + 1) * NZ)
                dst = kv_p[g][0, 0].rearrange("t w h e -> t w (h e)")
                if g == 0:
                    pool.dma_start(dst[:, 0, :], k_tok[1]).then_inc(tokens_sent, 16)
                    for a in range(2):
                        pool.dma_start(dst[a * HD:(a + 1) * HD, 1, :], v_tok[a * HD:(a + 1) * HD, 1, g, :]).then_inc(tokens_sent, 16)
                else:
                    for b in range(2):
                        pool.dma_start(dst[b * P:(b + 1) * P, 0, :], k_tok[b]).then_inc(tokens_sent, 16)
                    pool.dma_start(dst[:, 1, :].rearrange("(b p) c -> p b c", p=P), v_tok[:, :, g, :]).then_inc(tokens_sent, 16)
                pool.dma_start(qkvs_dram[:, g], qkv_s[0:NS, :, :]).then_inc(tokens_sent, 16)
                pool.dma_start(kv_s[g][0, :, kv_s[g].shape[2] - 1].rearrange("b w h e -> b w (h e)"),
                               qkv_s[0:NS, 1:3, :]).then_inc(tokens_sent, 16)

            def stage(pair, u):
                one = ds(pair, 1)
                for blk in range(2):
                    nc.gpsimd.tensor_copy(q_st[:, u, :, blk * P:(blk + 1) * P][:, :, ::-1],
                                          qk[:, :, 0, one, blk * P:(blk + 1) * P].rearrange("p g a t -> p (g a) t"))
                nc.gpsimd.tensor_copy(k_st[:, u], qk[:, :, 1, one, 0:SEQ].rearrange("p g a t -> p (g a) t")).then_inc(staged, 2)
                nc.gpsimd.tensor_copy(v_st[:, u].rearrange("p b (g c) -> p b g c", g=G),
                                      v_tok[:, :, :, ds(pair * P, P)]).then_inc(staged, 1)

            def step(i, s, stages):
                h = i * 4 + s
                b = s % 2
                pool.wait_ge(inv_ready, h + 1)
                nc.gpsimd.tensor_tensor(probs[:, b, 0:G * P], probs[:, b, 0:G * P],
                                        small[:, 8 * b + 7:8 * b + 8].to_broadcast([P, G * P]), ALU.mult)
                nc.gpsimd.tensor_tensor(probs[:, b, G * P:], probs[:, b, G * P:],
                                        small[:, 8 * b + 6:8 * b + 7].to_broadcast([P, 2 * G * P]), ALU.mult).then_inc(probs_ready, 1)
                if stages:
                    pool.wait_ge(pv_ready, h)
                    stage(i * 2 + s // 2 + 1, (s // 2 + 1) % 2)

            pool.wait_ge(tokens_sent, 16 * 5 * G)
            pool.wait_ge(sample_done, 1)
            stage(0, 0)
            stage(1, 1)
            for s in range(4):
                step(0, s, s == 2)
            with pool.Fori(1, H // 4 - 1) as i:
                for s in range(4):
                    step(i, s, s % 2 == 0)
            for s in range(4):
                step(H // 4 - 1, s, s == 0)

            with pool.Fori(0, LAYERS * NE) as e:
                pool.wait_ge(gate_bc_ready, e + 1)
                for j in range(FT):
                    pool.wait_ge(act_ready, e * FT + (j + 1))
                    nc.gpsimd.tensor_tensor(hid[:, j, :], act[:, j % 2, :], gate_bc, ALU.mult).then_inc(hid_ready, 1)
            pool.wait_ge(cache_copied, 16 * n_copies)

        @block.scalar
        def _(ac):
            dma = ac.dma_start
            dma(ident[:], c_ident).then_inc(consts_landed, 16)
            dma(bucket_p[0:NB + 1, :, :], c_bucket_prompt).then_inc(consts_landed, 16)
            dma(bucket_s[:], c_bucket_sample.rearrange("g n k -> n g k")).then_inc(consts_landed, 16)
            dma(tab[0:NB, :], rel_bias).then_inc(consts_landed, 16)
            dma(same_batch[:], c_same_batch).then_inc(consts_landed, 16)
            dma(rank[:], c_rank).then_inc(consts_landed, 16)
            for at, v in ((ATTN_G, attn_norm[0]), (POOL_G, pool_norm[0]), (POOL_B, pool_b[0]), (POOL_S, pool_scale[0])):
                dma(vec_rows[at:at + KT, :], v.rearrange("(k p) -> k p", p=P)).then_inc(vecs_landed, 16)
            dma(vec_rows[FFN_G[0]:FFN_G[0] + 2 * KT, :], ffn_norm.rearrange("l (k p) -> (l k) p", p=P)).then_inc(vecs_landed, 16)
            for w, v in enumerate((q_norm, k_norm)):
                for g in range(G):
                    for t in range(2):
                        dma(vec_rows[QK_G + 2 * g + w:QK_G + 2 * g + w + 1, t * HD:(t + 1) * HD], v[0, g:g + 1, :]).then_inc(vecs_landed, 16)
            for layer in range(LAYERS):
                dma(wr[:, layer, :, 0:NG], router_group_w[layer].rearrange("(k p) g -> p k g", p=P)).then_inc(consts_landed, 16)
                dma(wr[:, layer, :, NG:], router_expert_w[layer].rearrange("(k p) g -> p k g", p=P)).then_inc(consts_landed, 16)
            dma(brow[:, :, 0:NG], router_group_b.rearrange("(a l) g -> a l g", a=1)).then_inc(consts_landed, 16)
            dma(brow[:, :, NG:], router_expert_b.rearrange("(a l) g -> a l g", a=1)).then_inc(consts_landed, 16)

            ac.wait_ge(setup_done, 1)
            norm_root(ac, 0, h_filled, KT)
            ac.wait_ge(bias_copied, 1)
            dma(bias_dram.rearrange("h g d -> h g d"), bias_rows[0:H, :, :]).then_inc(bias_stored, 16)
            ac.wait_ge(bias_stored, 16)

            with ac.Fori(0, G) as g:
                for s in range(NZ + 4):
                    if s < NQK:
                        ac.wait_ge(z_ready, g * NZ + (s + 1))
                        nc.scalar.activation(zsq[:, s % 2, :], bank[s % 2][:, 0:T], ACT.Square).then_inc(zsq_ready, 1)
                    if 1 <= s <= NQK:
                        n = s - 1
                        ac.wait_ge(zsum_ready, g * NQK + (n + 1))
                        if n >= 2:
                            ac.wait_ge(zn_ready, g * NZ + (n - 1))
                        nc.scalar.activation(zr[:, n % 2, :], bank[2 + n % 2][:, 0:T], ACT.Sqrt, bias=epsc[:, 0:1],
                                             scale=1.0 / HD).then_inc(zroot_ready, 1)
                    if s >= 4:
                        n = s - 4
                        what, k = n // KT, n % KT
                        at = slice(k * P, (k + 1) * P)
                        src = bank[4 + n % 2]
                        ac.wait_ge(z_turned, g * NZ + (n + 1))
                        if what == 1:
                            for b in range(2):
                                nc.scalar.activation(k_tok[b][:, at], src[:, b * P:(b + 1) * P], ACT.Copy)
                        if what == 2:
                            nc.scalar.activation(v_tok[:, :, ds(g, 1), at].rearrange("p b a c -> p (b a) c"),
                                                 src[:, 0:2 * P].rearrange("p (b c) -> p b c", b=2), ACT.Copy)
                        nc.scalar.activation(qkv_s[0:NS, what, at], src[0:NS, 2 * P:3 * P], ACT.Copy).then_inc(z_stored, 1)
                ac.wait_ge(tokens_sent, g * (16 * 5) + 16 * 5)

            ac.wait_ge(tokens_sent, 16 * 5 * G)
            ac.wait_ge(zn_kept, G * NQK)
            ac.wait_ge(z_turned, G * NZ)
            for b in range(NS):
                for w in range(2):
                    dma(qk_new[b * H:(b + 1) * H, w, :, :],
                        qkvs_dram[b, :, w, :].rearrange("g (h e) -> h g e", e=HD)).then_inc(qk_new_landed, 16)
            dma(v_new[0:NS, :, :], qkvs_dram[:, :, 2, :]).then_inc(v_new_landed, 16)
            for m in range(NS * G):
                half, g, b = m // (G * HALF), m // HALF % G, m % HALF
                if m >= 3:
                    ac.wait_ge(prod_ready, m - 2)
                dma(q_rep[:, m % 3, :], qkvs_dram[half * HALF + b, g, 0:1, :].to_broadcast([P, D])).then_inc(q_rep_landed[m % 3], 16)
            ac.wait_ge(s_rows_ready, 1)
            nc.scalar.activation(s_rows[:, :, :], s_rows[:, :, :], ACT.Exp, bias=small[:, 36:37],
                                 accum_out=small[:, 37:38]).then_inc(s_exp_ready, 1)

            def step(i, s, live, behind):
                h = i * 4 + s
                if live:
                    b = s % 2
                    ac.wait_ge(biased, h + 1)
                    nc.scalar.activation(probs[:, b, 0:G * P], probs[:, b, 0:G * P], ACT.Exp,
                                         bias=small[:, 8 * b + 3:8 * b + 4], accum_out=small[:, 8 * b + 5:8 * b + 6])
                    nc.scalar.activation(probs[:, b, G * P:], probs[:, b, G * P:], ACT.Exp,
                                         bias=small[:, 8 * b + 2:8 * b + 3], accum_out=small[:, 8 * b + 4:8 * b + 5]).then_inc(exps_ready, 1)
                if s % 2 == 1 and behind >= 3:
                    pair, u = i * 2 + (s - 3) // 2, (s - 3) // 2 % 2
                    ac.wait_ge(pv_ready, h - 1)
                    for blk in range(2):
                        last = nc.scalar.activation(oT[:, ds(pair, 1), blk * P:(blk + 1) * P],
                                                    bank[6 + u][:, blk * P:(blk + 1) * P][:, ::-1].rearrange("p (a t) -> p a t", a=1), ACT.Copy)
                    last.then_inc(o_copied, 1)
                if 1 <= behind <= H:
                    b = (s - 1) % 2
                    ac.wait_ge(pt_ready, h)
                    nc.scalar.activation(probsT[:, b, 4 * P:8 * P], bank[4][:, :], ACT.Copy)
                    nc.scalar.activation(probsT[:, b, 8 * P:], bank[5][:, 0:P], ACT.Copy).then_inc(pt_copied_act, 1)

            for s in range(4):
                step(0, s, True, s)
            with ac.Fori(1, H // 4) as i:
                for s in range(4):
                    step(i, s, True, 4)
            step(H // 4, 0, False, H)
            step(H // 4, 1, False, H + 1)

            ac.wait_ge(staged, 3 * PAIRS)
            dma(pw, pool_w[0].rearrange("g (k p) f -> p (g k) f", p=P)).then_inc(pool_landed, 16)
            for gi in range(4):
                dma(inv_count[:, gi, :], c_inv_count[gi:gi + 1, :].to_broadcast([P, SEQ])).then_inc(pool_landed, 16)
            dma(state[0:NS * STATE], state_pool[0].rearrange("b s c -> (b s) c")).then_inc(pool_landed, 16)
            dma(state_sum[0:NS * STATE], c_state_sum).then_inc(pool_landed, 16)

            for layer in range(LAYERS):
                if layer:
                    norm_root(ac, 2, down_added, NE * KT)
                    ac.wait_ge(pool_tok_ready, 1)
                    dma(pool_p[0, 0], pool_tok[0:STATE]).then_inc(pool_sent, 16)
                    dma(pool_s[0, :, STATE - 1, :], pool_tok[STATE:STATE + NS]).then_inc(pool_sent, 16)
                    norm_root(ac, 3, pool_y_added, KT)
                else:
                    norm_root(ac, 1, wo_added, KT)
                for which in range(2):
                    ac.wait_ge(router_arg, 2 * layer + which + 1)
                    v = rt[:, 1, :, 0:NG] if which == 0 else rt[:, 12, :, 0:1]
                    nc.scalar.activation(v, v, ACT.Exp).then_inc(router_exp, 1)
                with ac.Fori(layer * NE, (layer + 1) * NE) as e:
                    ac.wait_ge(gate_bc_made, e + 1)
                    nc.scalar.activation(gate_bc, bank[6][:, 0:T], ACT.Copy).then_inc(gate_bc_ready, 1)
                    for j in range(FT):
                        ac.wait_ge(up_ready, e * FT + (j + 1))
                        nc.scalar.activation(silu[:, j % 2, :], bank[j % 2][:, 0:T], ACT.Silu).then_inc(silu_ready, 1)
            ac.wait_ge(pool_sent, 32)

        @block.vector
        def _(dve):
            chain = Chain(dve, dve_own)
            vec = nc.vector
            vec.memset(ones[:], 1.0)
            vec.memset(epsc[:], RMS_EPS)
            vec.memset(small[:], 0.0)
            vec.memset(tab[NB:NB + 1, :], NEG)
            for a in range(2):
                for b in range(2):
                    last = vec.memset(blockones[a * HD:(a + 1) * HD, b * HD:(b + 1) * HD], float(a == b))
            last.then_inc(setup_done, 1)

            dve.wait_ge(vecs_turned, 1)
            chain(vec.tensor_copy(vecs[:], bank[7][:, 0:NVEC]))
            for g in range(G):
                c = QK_G + 2 * g
                last = vec.tensor_scalar(vecs[:, c:c + 1], vecs[:, c:c + 1], float(HD) ** -0.5, None, ALU.mult)
            chain(last)
            for k in range(KT):
                dve.wait_ge(x_turned, k + 1)
                vec.tensor_copy(hT[:, k, :], bank[k % 4][:, 0:T]).then_inc(h_filled, 1)
            dve.wait_ge(bias_made, 1)
            for g in range(G):
                last = vec.tensor_copy(bias_rows[0:H, g, :], bank[4 + g][0:H, 0:BV])
            last.then_inc(bias_copied, 1)
            dve.wait_ge(consts_landed, 16 * 12)
            for g in range(G):
                chain(vec.tensor_copy(tabrep[:, g, :, :], tab[0:NB, g * H:(g + 1) * H].rearrange("p (a h) -> p a h", a=1).to_broadcast([NB, NS, H])))
            norm_apply(dve, chain, 0, ATTN_G)

            with dve.Fori(0, G) as g:
                chain.enter(g, NQK + 1)
                chain(vec.tensor_copy(gains[:], vecs[:, ds(g * 2 + QK_G, 2)]))
                for n in range(NZ):
                    if n >= 4:
                        dve.wait_ge(z_turned, g * NZ + (n - 3))
                        if n - 4 < NQK:
                            dve.wait_ge(zn_kept, g * NQK + (n - 3))
                    if n < NQK:
                        dve.wait_ge(zroot_ready, g * NQK + (n + 1))
                        chain(vec.reciprocal(zri[:, n % 2, :], zr[:, n % 2, :]))
                        vec.scalar_tensor_tensor(out=zn[:, n % 4, :], in0=bank[n % 2][:, 0:T], scalar=gains[:, n // KT:n // KT + 1],
                                                 in1=zri[:, n % 2, :], op0=ALU.mult, op1=ALU.mult).then_inc(zn_ready, 1)
                    else:
                        dve.wait_ge(z_ready, g * NZ + (n + 1))
                        vec.tensor_copy(zn[:, n % 4, :], bank[n % 2][:, 0:T]).then_inc(zn_ready, 1)
                dve.wait_ge(z_turned, g * NZ + NZ)
                dve.wait_ge(zn_kept, g * NQK + NQK)
            chain.leave(G)

            dve.wait_ge(tokens_sent, 16 * 5 * G)
            for m in range(NS * G):
                half, g, b = m // (G * HALF), m // HALF % G, m % HALF
                dve.wait_ge(q_rep_landed[m % 3], 16 * (m // 3 + 1))
                if b == 0:
                    dve.wait_ge(ring_full[g], 16 * (RING_KV + half + 1))
                vec.tensor_tensor(prod[:, m % 2, :], slot(g)[:, b * D:(b + 1) * D], q_rep[:, m % 3, :], ALU.mult).then_inc(prod_ready, 1)
                dve.wait_ge(prod_ready, m + 1)
                at = (half * HALF + b) * H
                last = vec.tensor_reduce(out=s_keys[:, g, at:at + H], in_=prod[:, m % 2, :].rearrange("p (h e) -> p h e", e=HD),
                                         axis=AX_X, op=ALU.add)
            last.then_inc(s_keys_ready, 1)
            dve.wait_ge(qk_new_landed, 16 * 2 * NS)
            chain(vec.tensor_tensor(qk_prod, qk_new[:, 0], qk_new[:, 1], ALU.mult))
            chain(vec.tensor_reduce(out=small[:, 32:32 + G], in_=qk_prod, axis=AX_X, op=ALU.add))
            dve.wait_ge(s_turned, 1)
            chain(vec.tensor_copy(s_rows, bank[0][:, 0:G * (P + 1)].rearrange("p (g k) -> p g k", g=G)))
            chain(vec.tensor_tensor(s_rows[:, :, P], s_rows[:, :, P], small[:, 32:32 + G], ALU.add))
            chain(vec.tensor_reduce(out=small[:, 35:36], in_=s_rows.rearrange("p g k -> p (g k)"), axis=AX_X, op=ALU.max))
            vec.tensor_scalar(small[:, 36:37], small[:, 35:36], -1.0, None, ALU.mult).then_inc(s_rows_ready, 1)
            dve.wait_ge(s_exp_ready, 1)
            chain(vec.reciprocal(small[:, 38:39], small[:, 37:38]))
            chain(vec.tensor_scalar(s_rows, s_rows, small[:, 38:39], None, ALU.mult))
            for g in range(G):
                last = vec.tensor_scalar(p_newm[:, g, :], same_batch[:], s_rows[:, g, P:P + 1], None, ALU.mult)
            last.then_inc(p_ready, 1)
            dve.wait_ge(p_turned, 1)
            vec.tensor_copy(p_keys, bank[1][:, 0:G * BH].rearrange("p (g k) -> p g k", g=G))
            vec.tensor_copy(p_newT[0:NS], bank[2][0:NS, 0:G * BH].rearrange("p (g k) -> p g k", g=G)).then_inc(p_keys_ready, 1)
            dve.wait_ge(pv_s_ready, 2)
            chain(vec.tensor_copy(o_new, bank[3][:, 0:KT * NS * 2].rearrange("p (k b t) -> p k b t", k=KT, t=2)))
            for t in range(2):
                rows = slice(t * HD, (t + 1) * HD)
                last = vec.tensor_tensor(oT[rows, :, SEQ:], bank[4][rows, 0:KT * NS * 2].rearrange("p (k b t) -> p k b t", k=KT, t=2)[:, :, :, t],
                                         o_new[rows, :, :, t], ALU.add)
            last.then_inc(sample_done, 1)

            def step(i, s, live, behind):
                h = i * 4 + s
                b = s % 2
                if live:
                    dve.wait_ge(scores_ready, h + 1)
                    dve.wait_ge(bias_landed[b], (i * 2 + s // 2 + 1) * 16)
                    c = 8 * b
                    vec.memset(small[:, 60:61], 0.0)
                    vec.tensor_tensor_reduce(out=probs[:, b, 0:G * P].rearrange("p (g k) -> p g k", g=G), in0=bank[0][:, 0:G * P].rearrange("p (g k) -> p g k", g=G),
                                             in1=bias_t[:, b, :, P:], scale=1.0, scalar=NEG, op0=ALU.add, op1=ALU.max,
                                             accum_out=small[:, 16 + c:17 + c])
                    vec.tensor_tensor_reduce(out=probs[:, b, 3 * P:7 * P], in0=bank[1][:, :], in1=bias_t[:, b, 0:2, :].rearrange("p g k -> p (g k)"),
                                             scale=1.0, scalar=NEG, op0=ALU.add, op1=ALU.max, accum_out=small[:, 17 + c:18 + c])
                    chain(vec.tensor_tensor_reduce(out=probs[:, b, 7 * P:], in0=bank[2][:, 0:SEQ], in1=bias_t[:, b, 2, :],
                                                   scale=1.0, scalar=NEG, op0=ALU.add, op1=ALU.max, accum_out=small[:, 18 + c:19 + c]))
                    vec.tensor_scalar(small[:, c + 3:c + 4], small[:, 16 + c:17 + c], -1.0, None, ALU.mult)
                    vec.tensor_scalar(small[:, c + 2:c + 3], small[:, 17 + c:18 + c], small[:, 18 + c:19 + c], -1.0,
                                      ALU.max, ALU.mult).then_inc(biased, 1)
                if 1 <= behind <= H:
                    dve.wait_ge(pt_ready, h)
                    vec.tensor_copy(probsT[:, 1 - b, 0:4 * P], bank[3][:, :]).then_inc(pt_copied_dve, 1)
                if live:
                    dve.wait_ge(exps_ready, h + 1)
                    vec.reciprocal(small[:, 8 * b + 6:8 * b + 8], small[:, 8 * b + 4:8 * b + 6]).then_inc(inv_ready, 1)

            for s in range(4):
                step(0, s, True, s)
            with dve.Fori(1, H // 4) as i:
                chain.enter(i, 4, 1)
                for s in range(4):
                    step(i, s, True, 4)
            chain.leave(H // 4)
            step(H // 4, 0, False, H)

            for m in range(KT):
                dve.wait_ge(wo_ready, m + 1)
                vec.tensor_tensor(hT[:, m, :], bank[m % 2][:, 0:T], hT[:, m, :], ALU.add).then_inc(wo_added, 1)

            def wide(v, n):
                return v.to_broadcast([P, 3, n])

            def router(layer):
                lg, le = logits[:, :, 0:NG], logits[:, :, NG:]
                r = [rt[:, n] for n in range(16)]
                chain(vec.memset(logits[:, 2, :], 0.0))
                dve.wait_ge(logits_made, layer + 1)
                vec.tensor_copy(logits[:, 0:2, :], bank[6][:, 0:2 * NR].rearrange("p (t n) -> p t n", t=2))
                chain(vec.tensor_copy(logits[0:NS, 2, :], bank[6][0:NS, 2 * NR:3 * NR]))
                gmax = r[0][:, :, 0:1]
                chain(vec.tensor_reduce(out=gmax, in_=lg, axis=AX_X, op=ALU.max))
                vec.tensor_tensor(r[1][:, :, 0:NG], lg, wide(gmax, NG), ALU.subtract).then_inc(router_arg, 1)
                chain(vec.tensor_tensor(r[2][:, :, 0:NG], lg, wide(gmax, NG), ALU.is_equal))
                rk = rank[:, :].rearrange("p (a n) -> p a n", a=1)
                chain(vec.tensor_tensor(r[2][:, :, 0:NG], r[2][:, :, 0:NG], rk[:, :, 0:NG].to_broadcast([P, 3, NG]), ALU.mult))
                chain(vec.tensor_reduce(out=r[3][:, :, 0:1], in_=r[2][:, :, 0:NG], axis=AX_X, op=ALU.max))
                chain(vec.tensor_tensor(r[2][:, :, 0:NG], r[2][:, :, 0:NG], wide(r[3][:, :, 0:1], NG), ALU.is_equal))
                for g in range(NG):
                    last = vec.tensor_copy(r[4][:, :, g * EPG:(g + 1) * EPG], wide(r[2][:, :, g:g + 1], EPG))
                chain(last)
                chain(vec.tensor_tensor(r[5], le, r[4], ALU.mult))
                chain(vec.tensor_scalar(r[4], r[4], -1.0, -NEG, ALU.add, ALU.mult))
                chain(vec.tensor_tensor(r[5], r[5], r[4], ALU.add))

                def first_of_largest(src, top, out):
                    chain(vec.tensor_reduce(out=top, in_=src, axis=AX_X, op=ALU.max))
                    chain(vec.tensor_tensor(out, src, wide(top, NE), ALU.is_equal))
                    chain(vec.tensor_tensor(out, out, rk.to_broadcast([P, 3, NE]), ALU.mult))
                    chain(vec.tensor_reduce(out=r[3][:, :, 0:1], in_=out, axis=AX_X, op=ALU.max))
                    chain(vec.tensor_tensor(out, out, wide(r[3][:, :, 0:1], NE), ALU.is_equal))

                first_of_largest(r[5], r[6][:, :, 0:1], r[7])
                chain(vec.tensor_scalar(r[8], r[7], 2 * NEG, None, ALU.mult))
                chain(vec.tensor_tensor(r[8], r[8], r[5], ALU.add))
                first_of_largest(r[8], r[9][:, :, 0:1], r[10])
                vec.tensor_tensor(r[12][:, :, 0:1], r[9][:, :, 0:1], r[6][:, :, 0:1], ALU.subtract).then_inc(router_arg, 1)
                dve.wait_ge(router_exp, 2 * layer + 2)
                chain(vec.tensor_reduce(out=r[11][:, :, 0:1], in_=r[1][:, :, 0:NG], axis=AX_X, op=ALU.add))
                chain(vec.tensor_scalar(r[13][:, :, 0:1], r[12][:, :, 0:1], 1.0, None, ALU.add))
                chain(vec.tensor_tensor(r[13][:, :, 0:1], r[13][:, :, 0:1], r[11][:, :, 0:1], ALU.mult))
                chain(vec.reciprocal(r[14][:, :, 0:1], r[13][:, :, 0:1]))
                chain(vec.tensor_tensor(r[15][:, :, 0:1], r[14][:, :, 0:1], r[12][:, :, 0:1], ALU.mult))
                chain(vec.tensor_tensor(r[7], r[7], wide(r[14][:, :, 0:1], NE), ALU.mult))
                chain(vec.tensor_tensor(r[10], r[10], wide(r[15][:, :, 0:1], NE), ALU.mult))
                vec.tensor_tensor(r[7], r[7], r[10], ALU.add).then_inc(gates_ready, 1)
                dve.wait_ge(gates_turned, layer + 1)
                chain(vec.tensor_copy(gatesT[0:NE], bank[5][0:NE, 0:T]))

            def experts(layer):
                with dve.Fori(layer * NE, (layer + 1) * NE) as e:
                    vec.tensor_scalar(gate_one[0:NE], gatesT[0:NE], ident[0:NE, ds(e - layer * NE, 1)], None, ALU.mult).then_inc(gate_one_ready, 1)
                    for j in range(FT):
                        dve.wait_ge(silu_ready, e * FT + (j + 1))
                        if j >= 2:
                            dve.wait_ge(hid_ready, e * FT + (j - 1))
                        vec.tensor_tensor(act[:, j % 2, :], bank[2 + j % 2][:, 0:T], silu[:, j % 2, :], ALU.mult).then_inc(act_ready, 1)
                    for m in range(KT):
                        dve.wait_ge(down_ready, e * KT + (m + 1))
                        vec.tensor_tensor(hT[:, m, :], bank[4 + m % 2][:, 0:T], hT[:, m, :], ALU.add).then_inc(down_added, 1)

            norm_apply(dve, chain, 1, FFN_G[0])
            router(0)
            experts(0)

            norm_apply(dve, chain, 2, POOL_G)
            dve.wait_ge(u_ready, 3)
            dve.wait_ge(pool_landed, 16 * 7)
            chain(vec.memset(ext[:, :, :, 0:PAD], 0.0))
            for gi, win in enumerate(POOL_WINDOWS):
                u2 = uT[:, 2 * gi:2 * gi + 2, 0:SEQ]
                chain(vec.tensor_copy(ext[:, 0, :, PAD:], u2))
                at, sh = 0, 1
                while sh < win:
                    chain(vec.tensor_tensor(ext[:, 1 - at, :, PAD:], ext[:, at, :, PAD:], ext[:, at, :, PAD - sh:PAD + SEQ - sh], ALU.add))
                    at, sh = 1 - at, sh * 2
                chain(vec.tensor_tensor(ext[:, 1 - at, :, PAD:], ext[:, at, :, PAD:], inv_count[:, gi:gi + 1, :].to_broadcast([P, 2, SEQ]), ALU.mult))
                chain(vec.tensor_tensor(pool_z[:, 2 * gi:2 * gi + 2, 0:SEQ], ext[:, 1 - at, :, PAD:], u2, ALU.subtract))
                if gi == 0:
                    dve.wait_ge(state_summed, 1)
                us = uT[:, 2 * gi:2 * gi + 2, SEQ:]
                chain(vec.tensor_tensor(zs_tmp, bank[0][:, 2 * gi * NS:(2 * gi + 2) * NS].rearrange("p (k b) -> p k b", k=2), us, ALU.add))
                vec.scalar_tensor_tensor(out=pool_z[:, 2 * gi:2 * gi + 2, SEQ:], in0=zs_tmp, scalar=1.0 / win, in1=us,
                                         op0=ALU.mult, op1=ALU.subtract).then_inc(pooled, 1)
                dve.wait_ge(pooled, gi + 1)
            for a in range(2):
                dve.wait_ge(pool_turned, a + 1)
                last = vec.tensor_copy(pool_tok[0:STATE + NS, a * 512:(a + 1) * 512], bank[3 + a][0:STATE + NS, :])
            last.then_inc(pool_tok_ready, 1)
            for m in range(KT):
                dve.wait_ge(pool_y_ready, m + 1)
                chain(vec.tensor_scalar(ybuf[:, m % 2, :], bank[1 + m % 2][:, 0:T], vecs[:, POOL_B + m:POOL_B + m + 1],
                                        vecs[:, POOL_S + m:POOL_S + m + 1], ALU.add, ALU.mult))
                vec.tensor_tensor(hT[:, m, :], hT[:, m, :], ybuf[:, m % 2, :], ALU.add).then_inc(pool_y_added, 1)

            norm_apply(dve, chain, 3, FFN_G[1])
            router(1)
            experts(1)

            for b in range(3):
                n = P if b < 2 else NS
                for a in range(2):
                    dve.wait_ge(y_turned, 2 * b + a + 1)
                    vec.tensor_copy(y_tok[0:n, b, a * 512:(a + 1) * 512], bank[2 * b + a][0:n, :]).then_inc(y_ready, 1)

        @block.tensor
        def _(pe):
            mm = nc.tensor.matmul
            pe.wait_ge(consts_landed, 16 * 12)
            pe.wait_ge(setup_done, 1)
            pe.wait_ge(vecs_landed, 16 * (5 + 4 * G))
            nc.tensor.transpose(bank[7][:, 0:NVEC], vec_rows[:], ident[0:NVEC, 0:NVEC]).then_inc(vecs_turned, 1)
            pe.wait_ge(x_landed, 32)
            for k in range(KT):
                if k >= 4:
                    pe.wait_ge(h_filled, k - 3)
                for b in range(2):
                    nc.tensor.transpose(bank[k % 4][:, b * P:(b + 1) * P], x_tok[:, b, k * P:(k + 1) * P], ident[:])
                nc.tensor.transpose(bank[k % 4][:, SEQ:T], x_tok[0:NS, 2, k * P:(k + 1) * P], ident[0:NS, 0:NS]).then_inc(x_turned, 1)
            for g in range(G):
                last = mm(bank[4 + g][0:H, 0:BV], tab[:, g * H:(g + 1) * H], bucket_p[0:NB + 1, g, :], start=True, stop=True)
            last.then_inc(bias_made, 1)
            norm_sums(pe, 0)
            pe.wait_ge(u_ready, 1)
            pe.wait_ge(bias_copied, 1)

            with pe.Fori(0, G) as g:
                for s in range(NZ + 3):
                    if s < NZ:
                        c = s // TPC
                        if s % TPC == 0:
                            pe.wait_ge(ring_full[c % 3], g * 32 + 16 * (c // 3 + 1))
                        if s >= 2:
                            pe.wait_ge(zn_ready, g * NZ + (s - 1))
                        w = slot(c % 3).rearrange("p (k n) -> p k n", k=KT)
                        at = s % TPC * P
                        for k in range(KT):
                            last = mm(bank[s % 2][:, 0:T], w[:, k, at:at + P], uT[:, k, :], start=(k == 0), stop=(k == KT - 1))
                        last.then_inc(z_ready, 1)
                    if 1 <= s <= NQK:
                        n = s - 1
                        pe.wait_ge(zsq_ready, g * NQK + (n + 1))
                        if n >= 2:
                            pe.wait_ge(zroot_ready, g * NQK + (n - 1))
                        mm(bank[2 + n % 2][:, 0:T], blockones[:], zsq[:, n % 2, :], start=True, stop=True).then_inc(zsum_ready, 1)
                    if s >= 3:
                        n = s - 3
                        pe.wait_ge(zn_ready, g * NZ + (n + 1))
                        if n >= 2:
                            pe.wait_ge(z_stored, g * NZ + (n - 1))
                        dst = bank[4 + n % 2]
                        if n >= KT:
                            for b in range(2):
                                nc.tensor.transpose(dst[:, b * P:(b + 1) * P], zn[:, n % 4, b * P:(b + 1) * P], ident[:])
                        nc.tensor.transpose(dst[0:NS, 2 * P:3 * P], zn[:, n % 4, SEQ:T], ident[:]).then_inc(z_turned, 1)
                pe.wait_ge(z_stored, g * NZ + NZ)

            pe.wait_ge(s_keys_ready, 1)
            for g in range(G):
                at = g * (P + 1)
                mm(bank[0][:, at:at + P + 1], tabrep[:, g, :, :].rearrange("p b h -> p (b h)"), bucket_s[:, g, :], start=True, stop=False)
                last = mm(bank[0][:, at:at + P], s_keys[:, g, :], ident[:], start=False, stop=True)
            last.then_inc(s_turned, 1)
            pe.wait_ge(p_ready, 1)
            for g in range(G):
                nc.tensor.transpose(bank[1][:, g * BH:(g + 1) * BH], s_rows[:, g, 0:P], ident[:])
                last = nc.tensor.transpose(bank[2][0:NS, g * BH:(g + 1) * BH], p_newm[:, g, :], ident[:])
            last.then_inc(p_turned, 1)
            pe.wait_ge(p_keys_ready, 1)
            pe.wait_ge(v_new_landed, 16)
            for j in range(KT):
                for g in range(G):
                    mm(bank[3][:, j * 2 * NS:(j + 1) * 2 * NS], v_new[0:NS, g, j * P:(j + 1) * P],
                       p_newT[0:NS, g, :].rearrange("p (b h) -> p b h", b=NS)[:, :, 2 * j:2 * j + 2], start=(g == 0), stop=(g == G - 1))
            for half in range(2):
                for g in range(G):
                    pe.wait_ge(ring_full[g], 16 * (RING_KV + 2 + half + 1))
                for b4 in range(HALF):
                    b = half * HALF + b4
                    for j in range(KT):
                        at = (j * NS + b) * 2
                        for g in range(G):
                            last = mm(bank[4][:, at:at + 2], slot(g)[:, b4 * D + j * P:b4 * D + (j + 1) * P],
                                      p_keys[:, g, b * H + 2 * j:b * H + 2 * j + 2], start=(g == 0), stop=(g == G - 1))
                last.then_inc(pv_s_ready, 1)

            def step(i, s, live, behind):
                h = i * 4 + s
                if live:
                    u, t = s // 2 % 2, s % 2
                    rows = slice(t * HD, (t + 1) * HD)
                    pe.wait_ge(staged, (i * 2 + s // 2 + 1) * 3)
                    pe.wait_ge(biased, h)
                    for g in range(G):
                        mm(bank[0][:, g * P:(g + 1) * P], q_st[rows, u, g, 0:P], k_st[rows, u, g, 0:P], start=True, stop=True)
                    for g in range(G):
                        at = g % 2 * SEQ
                        last = mm(bank[1 + g // 2][:, at:at + SEQ], q_st[rows, u, g, P:], k_st[rows, u, g, :], start=True, stop=True)
                    last.then_inc(scores_ready, 1)
                if 1 <= behind <= H:
                    u, t = (s - 1) // 2 % 2, (s - 1) % 2
                    rows = slice(t * HD, (t + 1) * HD)
                    pe.wait_ge(probs_ready, h)
                    for n in range(3 * G):
                        last = nc.tensor.transpose(bank[3 + n // 4][:, n % 4 * P:(n % 4 + 1) * P], probs[:, t, n * P:(n + 1) * P], ident[:])
                    last.then_inc(pt_ready, 1)
                    pe.wait_ge(pt_copied_dve, h)
                    pe.wait_ge(pt_copied_act, h)
                    for g in range(G):
                        mm(bank[6 + u][rows, 0:P], v_st[:, u, 0, g * P + t * HD:g * P + (t + 1) * HD],
                           probsT[:, t, g * P:(g + 1) * P], start=(g == 0), stop=(g == G - 1))
                    for g in range(G):
                        for kb in range(2):
                            n = G + 2 * g + kb
                            last = mm(bank[6 + u][rows, P:2 * P], v_st[:, u, kb, g * P + t * HD:g * P + (t + 1) * HD],
                                      probsT[:, t, n * P:(n + 1) * P], start=(n == G), stop=(n == 3 * G - 1))
                    last.then_inc(pv_ready, 1)

            pe.wait_ge(sample_done, 1)
            for s in range(4):
                step(0, s, True, s)
            with pe.Fori(1, H // 4) as i:
                for s in range(4):
                    step(i, s, True, 4)
            step(H // 4, 0, False, H)

            pe.wait_ge(o_copied, PAIRS)
            for s in range(2):
                pe.wait_ge(ring_full[s], 16 * (RING_WO + 1))
            for m in range(KT):
                if m >= 2:
                    pe.wait_ge(wo_added, m - 1)
                for f in range(KT):
                    w = slot(f // 4).rearrange("p (k n) -> p k n", k=4)
                    last = mm(bank[m % 2][:, 0:T], w[:, f % 4, m * P:(m + 1) * P], oT[:, f, :], start=(f == 0), stop=(f == KT - 1))
                last.then_inc(wo_ready, 1)

            def router(layer, n_norm):
                pe.wait_ge(u_ready, n_norm + 1)
                for b in range(3):
                    n = P if b < 2 else NS
                    out = bank[6][0:n, b * NR:(b + 1) * NR]
                    for k in range(KT):
                        mm(out, uT[:, k, b * P:b * P + n], wr[:, layer, k, :], start=(k == 0), stop=False)
                    last = mm(out, ones[0:1, 0:n], brow[:, layer, :], start=False, stop=True)
                last.then_inc(logits_made, 1)
                pe.wait_ge(gates_ready, layer + 1)
                for b in range(3):
                    n = P if b < 2 else NS
                    last = nc.tensor.transpose(bank[5][0:NE, b * P:b * P + n], rt[0:n, 7, b, :], ident[0:n, 0:n])
                last.then_inc(gates_turned, 1)

            def experts(layer):
                with pe.Fori(layer * NE // 2, (layer + 1) * NE // 2) as r:
                    for odd in range(2):
                        e = r * 2 + odd
                        wg, wu, wd = (slot(s) for s in SLOTS[odd])
                        wg = wg.rearrange("p (k f) -> p k f", k=KT)
                        wu = wu.rearrange("p (k f) -> p k f", k=KT)
                        wd = wd.rearrange("p (k f) -> p k f", k=FT)
                        for what in range(2):
                            s = SLOTS[odd][what]
                            pe.wait_ge(ring_full[s], r * 16 + 16 * (FIRST_USES[s] + 1))
                        for j in range(FT):
                            if j >= 2:
                                pe.wait_ge(act_ready, e * FT + (j - 1))
                            for w, bk in ((wg, bank[j % 2]), (wu, bank[2 + j % 2])):
                                for k in range(KT):
                                    last = mm(bk[:, 0:T], w[:, k, j * P:(j + 1) * P], uT[:, k, :], start=(k == 0), stop=(k == KT - 1))
                            last.then_inc(up_ready, 1)
                            if j == 0:
                                pe.wait_ge(gate_one_ready, e + 1)
                                mm(bank[6][:, 0:T], ones[0:NE, :], gate_one[0:NE], start=True, stop=True).then_inc(gate_bc_made, 1)
                        pe.wait_ge(ring_full[SLOTS[odd][2]], r * 16 + 16 * (FIRST_USES[SLOTS[odd][2]] + 1))
                        pe.wait_ge(hid_ready, e * FT + FT)
                        for m in range(KT):
                            if m >= 2:
                                pe.wait_ge(down_added, e * KT + (m - 1))
                            for f in range(FT):
                                last = mm(bank[4 + m % 2][:, 0:T], wd[:, f, m * P:(m + 1) * P], hid[:, f, :], start=(f == 0), stop=(f == FT - 1))
                            last.then_inc(down_ready, 1)

            norm_sums(pe, 1)
            router(0, 1)
            experts(0)

            norm_sums(pe, 2)
            pe.wait_ge(pool_landed, 16 * 7)
            for k in range(KT):
                last = mm(bank[0][:, k * NS:(k + 1) * NS], state[0:NS * STATE, k * P:(k + 1) * P], state_sum[0:NS * STATE, k // 2, :], start=True, stop=True)
            last.then_inc(state_summed, 1)
            pe.wait_ge(u_ready, 3)
            for k in range(KT):
                last = nc.tensor.transpose(bank[3 + k // 4][0:STATE + NS, k % 4 * P:(k % 4 + 1) * P], uT[:, k, SEQ - STATE:T], ident[:])
                if k % 4 == 3:
                    last.then_inc(pool_turned, 1)
            for m in range(KT):
                gi, ft = m // 2, m % 2
                pe.wait_ge(pooled, gi + 1)
                if m >= 2:
                    pe.wait_ge(pool_y_added, m - 1)
                for ct in range(2):
                    last = mm(bank[1 + m % 2][:, 0:T], pw[:, 2 * gi + ct, ft * P:(ft + 1) * P], pool_z[:, 2 * gi + ct, :], start=(ct == 0), stop=(ct == 1))
                last.then_inc(pool_y_ready, 1)

            norm_sums(pe, 3)
            router(1, 3)
            experts(1)

            pe.wait_ge(down_added, LAYERS * NE * KT)
            for b in range(3):
                n = P if b < 2 else NS
                for k in range(KT):
                    last = nc.tensor.transpose(bank[2 * b + k // 4][0:n, k % 4 * P:(k % 4 + 1) * P], hT[:, k, b * P:b * P + n], ident[:])
                    if k % 4 == 3:
                        last.then_inc(y_turned, 1)


def constants():
    import math

    import numpy as np

    n_buckets, max_distance, seq, ns = 32, 2048, 256, 8
    exact = n_buckets // 2

    def bucket(dist):
        df = np.maximum(dist, exact).astype(np.float32)
        large = exact + (np.log(df / np.float32(exact)) / np.float32(math.log(max_distance / exact))
                         * np.float32(n_buckets - exact)).astype(np.int32)
        return np.where(dist < exact, dist, np.minimum(large, n_buckets - 1))

    one = np.float32(1)
    dist = 2 * P - 1 - np.arange(3 * P)
    bp = np.zeros((n_buckets + 1, 3, 3 * P), np.float32)
    for g, (w, d) in enumerate(zip(WINDOWS, DILATIONS)):
        ok = (dist >= 0) & (dist <= w) & (dist % d == 0)
        bp[bucket(np.maximum(dist, 0))[ok], g, np.nonzero(ok)[0]] = one
        bp[n_buckets, g, ~ok] = one
    bs = np.zeros((3, n_buckets, P + 1), np.float32)
    for g, d in enumerate(DILATIONS):
        bs[g, bucket((P - np.arange(P + 1)) * d), np.arange(P + 1)] = one
    same = np.repeat(np.eye(ns, dtype=np.float32), P // ns, axis=0)
    rank = np.tile(16 - np.arange(16, dtype=np.float32), (P, 1))
    inv = np.stack([one / np.minimum(w, np.arange(seq) + 1).astype(np.float32) for w in POOL_WINDOWS]).astype(np.float32)
    n_state = POOL_WINDOWS[-1] - 1
    ssum = np.zeros((ns, n_state, 4, ns), np.float32)
    for gi, w in enumerate(POOL_WINDOWS):
        for b in range(ns):
            ssum[b, n_state - (w - 1):, gi, b] = one
    return {"c_ident": np.eye(P, dtype=np.float32), "c_bucket_prompt": bp, "c_bucket_sample": bs, "c_same_batch": same,
            "c_rank": rank, "c_inv_count": inv, "c_state_sum": ssum.reshape(ns * n_state, 4, ns)}


_INS = ['x_prompt', 'x_sample', 'cache_kv_w128', 'cache_kv_w512', 'cache_kv_w2048', 'state_pool', 'w_qkv', 'q_norm',
        'k_norm', 'w_o', 'rel_bias', 'attn_norm', 'pool_norm', 'pool_w', 'pool_b', 'pool_scale', 'ffn_norm',
        'router_group_w', 'router_group_b', 'router_expert_w', 'router_expert_b', 'w_gate', 'w_up', 'w_down']
_OUTS = [(1, 256, 1024), (8, 1, 1024), (1, 1, 128, 2, 16, 64), (1, 1, 256, 2, 16, 64), (1, 1, 256, 2, 16, 64),
         (1, 1, 15, 1024), (1, 8, 128, 2, 16, 64), (1, 8, 512, 2, 16, 64), (1, 8, 2048, 2, 16, 64), (1, 8, 15, 1024)]


def kernel(**inputs):
    import numpy as _np
    import concourse.bacc as _bacc
    from concourse import mybir as _mybir
    from concourse.bass_utils import run_bass_kernel_spmd as _run

    nc = _bacc.Bacc("TRN2", target_bir_lowering=False, num_devices=1)
    arrays, args = {}, []
    given = [(n, _np.ascontiguousarray(inputs[n])) for n in _INS] + list(constants().items())
    for name, a in given:
        arrays[f"in_{name}_dram"] = a
        args.append(nc.dram_tensor(f"in_{name}_dram", a.shape, _mybir.dt.from_np(a.dtype), kind="ExternalInput").ap())
    for i, shape in enumerate(_OUTS):
        args.append(nc.dram_tensor(f"out_{i}_dram", shape, _mybir.dt.float32, kind="ExternalOutput").ap())
    build(nc, *args)
    r = _run(nc, [arrays], core_ids=[0])
    return tuple(r.results[0][f"out_{i}_dram"] for i in range(len(_OUTS)))
```

```python
from contextlib import ExitStack

import concourse.bass as bass
from concourse import mybir

ALU = mybir.AluOpType
ACT = mybir.ActivationFunctionType
F32 = mybir.dt.float32
I32 = mybir.dt.int32
AX_X = mybir.AxisListType.X
ds = bass.ds

P = 128
DILATIONS = (1, 4, 16)
WINDOWS = (128, 512, 2048)
POOL_WINDOWS = (2, 4, 8, 16)
NEG = -1e30
RMS_EPS = 1e-6


class Chain:

    def __init__(self, eng, sem):
        self.eng, self.sem, self.base, self.k, self.i, self.per = eng, sem, 0, 0, 0, 0

    def __call__(self, instruction):
        instruction.then_inc(self.sem, 1)
        self.k += 1
        self.eng.wait_ge(self.sem, self.i * self.per + (self.base + self.k))

    def enter(self, i, per, first=0):
        self.base += self.k - first * per
        self.k, self.i, self.per = 0, i, per

    def leave(self, end):
        assert self.k == self.per, (self.k, self.per)
        self.base += end * self.per
        self.k, self.i, self.per = 0, 0, 0


def build(nc, x_prompt, x_sample, cache_w128, cache_w512, cache_w2048, state_pool, w_qkv, q_norm,
          k_norm, w_o, rel_bias, attn_norm, pool_norm, pool_w, pool_b, pool_scale, ffn_norm,
          router_group_w, router_group_b, router_expert_w, router_expert_b, w_gate, w_up, w_down,
          c_ident, c_bucket_prompt, c_bucket_sample, c_same_batch, c_rank, c_inv_count, c_state_sum, c_tri,
          y_prompt, y_sample, kv128_p, kv512_p, kv2048_p, pool_p, kv128_s, kv512_s, kv2048_s, pool_s):
    _, SEQ, D = x_prompt.shape
    NS = x_sample.shape[0]
    T = SEQ + NS
    KT = D // P
    G = len(WINDOWS)
    NB, GH = rel_bias.shape
    H = GH // G
    HD = D // H
    PAIRS = H // 2
    BH = NS * H
    NE = w_gate.shape[1]
    FT = w_gate.shape[3] // P
    NG = router_group_w.shape[2]
    EPG = NE // NG
    NR = NG + NE
    LAYERS = w_gate.shape[0]
    STATE = state_pool.shape[2]
    BV = 3 * P
    CW = 512
    SLOT = KT * CW
    TPC = CW // P
    NZ = 3 * KT
    NQK = 2 * KT
    CHUNKS = G * NZ // TPC
    caches = (cache_w128, cache_w512, cache_w2048)
    kv_p, kv_s = (kv128_p, kv512_p, kv2048_p), (kv128_s, kv512_s, kv2048_s)
    HALF = NS // 2
    CAP = 64
    NP = NE // 2
    MAX_ROUNDS = LAYERS * NP * -(-T // CAP)
    assert SEQ == 2 * P and BH == P and KT * P == D and LAYERS == 2 and NZ // TPC == 6

    qkvs_dram = nc.dram_tensor("qkv_of_samples", [NS, G, 3, D], F32, kind="Internal").ap()
    bias_dram = nc.dram_tensor("bias_by_distance", [H, G, BV], F32, kind="Internal").ap()

    with ExitStack() as ctx:
        def sb(name, shape):
            return ctx.enter_context(nc.sbuf_tensor(name, shape, F32))

        def sem(name):
            return ctx.enter_context(nc.semaphore(name))

        ring_lo = sb("ring_lo", [P, 4 * SLOT])
        hT = sb("hT", [P, KT, T])
        uT = sb("uT", [P, KT, T])
        oT = uT
        region_a = sb("region_a", [P, G * 2 * KT * T + 2 * G * D])
        scratch = sb("scratch", [P, 10752])
        ident = sb("ident", [P, P])
        ones = sb("ones", [P, P])
        blockones = sb("blockones", [P, P])
        epsc = sb("epsc", [P, 1])
        NVEC = 6 * KT + 2 * G
        vec_rows = sb("vec_rows", [NVEC, P])
        vecs = sb("vecs", [P, NVEC])
        gains = sb("gains", [P, 2])
        bucket_s = sb("bucket_s", [NB, G, P + 1])
        tab = sb("tab", [NB + 1, GH])
        tabrep = sb("tabrep", [NB, G, NS, H])
        same_batch = sb("same_batch", [BH, NS])
        rank = sb("rank", [P, NE])
        wr = sb("wr", [P, LAYERS, KT, NR])
        brow = sb("brow", [1, LAYERS, NR])
        rstd = sb("rstd", [P, 2, T])
        small = sb("small", [P, 64])
        tri = sb("tri", [P, P])
        slot_no = sb("slot_no", [P, CAP])
        rounds_f = sb("rounds_f", [P, LAYERS, NP + 1])
        rounds_i = ctx.enter_context(nc.sbuf_tensor("rounds_i", [1, LAYERS * (NP + 1)], I32))

        def slot(s):
            if s < 4:
                return ring_lo[:, s * SLOT:(s + 1) * SLOT]
            return region_a[:, (s - 4) * SLOT:(s - 3) * SLOT]

        qk = region_a[:, 0:G * 2 * KT * T].rearrange("p (g w k t) -> p g w k t", g=G, w=2, k=KT)
        v_tok = region_a[:, G * 2 * KT * T:].rearrange("p (b g c) -> p b g c", b=2, g=G)

        def cut(start, shape, region=scratch):
            n = 1
            for s in shape:
                n *= s
            assert start + n <= region.shape[1], (start, n)
            names = "abcd"[:len(shape)]
            v = region[:, start:start + n]
            if len(shape) > 1:
                v = v.rearrange(f"p ({' '.join(names)}) -> p {' '.join(names)}",
                                **{c: s for c, s in zip(names, shape)})
            return v

        x_tok = cut(0, (3, D))
        sq = cut(4352, (KT, T))
        bucket_p = cut(6528, (G, BV))
        bias_rows = cut(7680, (G, BV))
        zn = cut(0, (4, T))
        zsq = cut(4 * T, (2, T))
        zr = cut(6 * T, (2, T))
        zri = cut(8 * T, (2, T))
        k_tok = cut(8832, (D,)), cut(3072, (D,))
        qkv_s = cut(4352, (3, D))
        q_rep = cut(0, (3, D))
        prod = cut(3072, (2, D))
        s_keys = cut(5120, (G, BH))
        s_rows = cut(5504, (G, P + 1))
        p_keys = cut(5904, (G, BH))
        qk_new = cut(6288, (2, G, HD))
        qk_prod = cut(6672, (G, HD))
        p_newm = cut(6864, (G, NS))
        p_newT = cut(6888, (G, BH))
        v_new = cut(7296, (G, D))
        o_new = cut(10368, (KT, NS, 2))
        q_st = cut(0, (2, G, SEQ))
        k_st = cut(1536, (2, G, SEQ))
        v_st = cut(3072, (2, 2, G * P))
        bias_t = cut(4608, (2, G, SEQ))
        probs = cut(6144, (2, 9 * P))
        probsT = cut(8448, (2, 9 * P))
        u_tok = cut(0, (3, D))
        u_slots = cut(3072, (KT, P))
        silu = cut(4096, (FT * P,))
        hid = cut(4608, (FT, 2, CAP))
        y_pair = cut(5120, (D,))
        pick = cut(6144, (3, P))
        pick_gate = cut(6528, (3, P))
        place = cut(6912, (T,))
        logits = cut(7200, (3, NR))
        rt = cut(7264, (16, 3, NE))
        chosen = cut(8032, (3, NE))
        gates = cut(8080, (3, NE))
        position = cut(8128, (3, NE))
        pair_at = cut(8176, (2, 3, 2))
        hid_rows = cut(8208, (FT * P,))
        pair_max = cut(8192, (NP,))
        pair_rounds = cut(8200, (NP,))
        y_tok = cut(0, (3, D))
        PAD = POOL_WINDOWS[-1]
        A0 = 2 * SLOT
        pw = cut(A0, (KT, D // 4), region_a)
        inv_count = cut(A0 + 2048, (4, SEQ), region_a)
        state = cut(A0 + 3072, (D,), region_a)
        state_sum = cut(A0 + 4096, (4, NS), region_a)
        ext = cut(A0 + 4128, (2, 2, PAD + SEQ), region_a)
        pool_z = cut(A0 + 5216, (KT, T), region_a)
        pool_tok = cut(A0 + 7328, (D,), region_a)
        ybuf = cut(A0 + 8352, (2, T), region_a)
        zs_tmp = cut(A0 + 8880, (2, NS), region_a)

        bank = [ctx.enter_context(nc.psum_tensor(f"bank{n}", [P, 512], F32)) for n in range(8)]

        z_bank = [bank[n] for n in (0, 1, 6, 7)]

        x_landed, consts_landed, vecs_landed = sem("x_landed"), sem("consts_landed"), sem("vecs_landed")
        cache_copied = sem("cache_copied")
        ring_full = [sem(f"ring_full{n}") for n in range(6)]
        dve_own, act_own = sem("dve_own"), sem("act_own")
        setup_done, vecs_turned, bias_made = sem("setup_done"), sem("vecs_turned"), sem("bias_made")
        bias_copied, bias_stored = sem("bias_copied"), sem("bias_stored")
        x_turned, h_filled = sem("x_turned"), sem("h_filled")
        squares_ready, sums_ready = sem("squares_ready"), sem("sums_ready")
        root_ready, u_ready = sem("root_ready"), sem("u_ready")
        z_ready, zsq_ready, zsum_ready = sem("z_ready"), sem("zsq_ready"), sem("zsum_ready")
        zroot_ready, zn_ready, zn_kept = sem("zroot_ready"), sem("zn_ready"), sem("zn_kept")
        z_turned, z_stored, tokens_sent = sem("z_turned"), sem("z_stored"), sem("tokens_sent")
        q_rep_landed = [sem(f"q_rep_landed{n}") for n in range(3)]
        qk_new_landed, v_new_landed = sem("qk_new_landed"), sem("v_new_landed")
        prod_ready, s_keys_ready, s_turned = sem("prod_ready"), sem("s_keys_ready"), sem("s_turned")
        s_rows_ready, s_exp_ready, p_ready = sem("s_rows_ready"), sem("s_exp_ready"), sem("p_ready")
        p_turned, p_keys_ready = sem("p_turned"), sem("p_keys_ready")
        pv_s_ready, sample_done = sem("pv_s_ready"), sem("sample_done")
        staged = sem("staged")
        bias_landed = [sem(f"bias_landed{n}") for n in range(2)]
        scores_ready, biased, exps_ready = sem("scores_ready"), sem("biased"), sem("exps_ready")
        inv_ready, probs_ready, pt_ready = sem("inv_ready"), sem("probs_ready"), sem("pt_ready")
        pt_copied_dve, pt_copied_act = sem("pt_copied_dve"), sem("pt_copied_act")
        pv_ready, o_copied = sem("pv_ready"), sem("o_copied")
        wo_ready, wo_added = sem("wo_ready"), sem("wo_added")
        u_turned, u_tok_dve, u_tok_act = sem("u_turned"), sem("u_tok_dve"), sem("u_tok_act")
        rounds_ready, pick_ready, shifted = sem("rounds_ready"), sem("pick_ready"), sem("shifted")
        gathered, slots_dve, slots_act = sem("gathered"), sem("slots_dve"), sem("slots_act")
        place_made, place_ready, y_half, y_copied = sem("place_made"), sem("place_ready"), sem("y_half"), sem("y_copied")
        spread, spread_added, layer_added = sem("spread"), sem("spread_added"), sem("layer_added")
        logits_made, router_arg, router_exp = sem("logits_made"), sem("router_arg"), sem("router_exp")
        chosen_ready, positions_made = sem("chosen_ready"), sem("positions_made")
        up_ready = [sem("up_ready_even"), sem("up_ready_odd")]
        silu_ready, hid_rows_ready = sem("silu_ready"), sem("hid_rows_ready")
        hid_turned, hid_ready = sem("hid_turned"), sem("hid_ready")
        down_even_done = sem("down_even_done")
        pool_landed, state_summed, pooled = sem("pool_landed"), sem("state_summed"), sem("pooled")
        pool_y_ready, pool_y_added = sem("pool_y_ready"), sem("pool_y_added")
        pool_turned, pool_tok_ready, pool_sent = sem("pool_turned"), sem("pool_tok_ready"), sem("pool_sent")
        y_turned, y_ready, y_sent = sem("y_turned"), sem("y_ready"), sem("y_sent")
        block = ctx.enter_context(nc.Block())

        ATTN_G, POOL_G, FFN_G, POOL_B, POOL_S = 0, KT, (2 * KT, 3 * KT), 4 * KT, 5 * KT
        QK_G = 6 * KT
        N_CONSTS = 11
        N_VECS = 5 + 4 * G
        SENT_PER_G = 4
        RING_KV = CHUNKS // 3
        RING_WO = RING_KV + 4

        qkv_chunks = w_qkv[0].rearrange("(k p) (c n) -> c p k n", p=P, n=CW)
        kv_strided = [c[0].rearrange("(x b) (s d) w h e -> x w s b d (h e)", b=HALF, d=d)[:, :, :, :, 0, :]
                      for c, d in zip(caches, DILATIONS)]
        expert_w = (w_gate.rearrange("l e (k p) f -> (l e) p k f", p=P),
                    w_up.rearrange("l e (k p) f -> (l e) p k f", p=P),
                    w_down.rearrange("l e (k p) f -> (l e) p k f", p=P))
        SLOTS = ((2, 3, 4), (5, 0, 1))
        FIRST_USES = (RING_WO + 1, RING_WO + 1, RING_WO, 0, 0, 0)

        def norm_sums(pe, n):
            pe.wait_ge(squares_ready, n + 1)
            for k in range(KT):
                last = nc.tensor.matmul(bank[7][:, 0:T], ones[:], sq[:, k, :], start=(k == 0), stop=(k == KT - 1))
            last.then_inc(sums_ready, 1)

        def norm_root(act_e, n, h_done, count):
            act_e.wait_ge(h_done, count)
            nc.scalar.activation(sq[:, :, :], hT[:], ACT.Square).then_inc(squares_ready, 1)
            act_e.wait_ge(sums_ready, n + 1)
            nc.scalar.activation(rstd[:, 0, :], bank[7][:, 0:T], ACT.Sqrt, bias=epsc[:, 0:1], scale=1.0 / D).then_inc(root_ready, 1)

        def norm_apply(dve, chain, n, gain):
            dve.wait_ge(root_ready, n + 1)
            chain(nc.vector.reciprocal(rstd[:, 1, :], rstd[:, 0, :]))
            for k in range(KT):
                last = nc.vector.scalar_tensor_tensor(out=uT[:, k, :], in0=hT[:, k, :], scalar=vecs[:, gain + k:gain + k + 1],
                                                      in1=rstd[:, 1, :], op0=ALU.mult, op1=ALU.mult)
            last.then_inc(u_ready, 1)

        def all_rounds(eng, layer, one_round, pair_start=None, chain=None):
            eng.wait_ge(rounds_ready, layer + 1)
            with eng.Fori(0, NP) as p:
                first, end = (eng.value_load(rounds_i[0:1, ds(p + (layer * (NP + 1) + n), 1)], min_val=n, max_val=MAX_ROUNDS)
                              for n in range(2))
                if pair_start is not None:
                    chain.enter(p, 2)
                    pair_start(layer, p)
                with eng.Fori(first, end) as q:
                    one_round(q, p)
            if chain is not None:
                chain.leave(NP)

        @block.sync
        def _(sp):
            sp.dma_start(x_tok[:, 0:2, :], x_prompt[0].rearrange("(b p) c -> p b c", p=P)).then_inc(x_landed, 16)
            sp.dma_start(x_tok[0:NS, 2, :], x_sample[:, 0, :]).then_inc(x_landed, 16)

            PIECES = (1, 4, 16)
            moved = []
            for src, out, n in zip(caches, kv_s, PIECES):
                m = (src.shape[2] - 1) * 2 * D
                moved.append([v[0].rearrange("b l w h e -> b (l w h e)")[:, at:at + m].rearrange("b (n x y) -> b n x y", n=n, x=16)
                              for v, at in ((out, 0), (src, 2 * D))])

            def move(g, b, n):
                views = []
                for v in moved[g]:
                    v = v[b] if isinstance(b, int) else v[ds(b, 1)].rearrange("a n x y -> (a n) x y")
                    views.append(v[n] if isinstance(n, int) else v[ds(n, 1)].rearrange("a x y -> (a x) y"))
                sp.dma_start(views[0], views[1]).then_inc(cache_copied, 16)

            N_PIECES = NS * sum(PIECES)
            for c in range(3):
                sp.dma_start(slot(c).rearrange("p (k n) -> p k n", k=KT), qkv_chunks[c]).then_inc(ring_full[c], 16)
            with sp.Fori(1, CHUNKS // 3) as r:
                for c in range(3):
                    sp.wait_ge(z_ready, r * (3 * TPC) + (c - 2) * TPC)
                    sp.dma_start(slot(c).rearrange("p (k n) -> p k n", k=KT),
                                 qkv_chunks[ds(r * 3 + c, 1)].rearrange("a p k n -> p (a k) n")).then_inc(ring_full[c], 16)
                    for n in range(3 * c, min(3 * c + 3, 8)):
                        move(2, r, n)
            for w in range(2):
                for half in range(2):
                    for g in range(G):
                        if w == 0 and half == 0:
                            sp.wait_ge(z_ready, G * NZ)
                        elif (w, half) < (1, 1):
                            sp.wait_ge(prod_ready, ((w * 2 + half - 1) * G + g + 1) * HALF)
                        else:
                            sp.wait_ge(pv_s_ready, 1)
                        sp.dma_start(slot(g).rearrange("p (b c) -> p b c", b=HALF), kv_strided[g][half, w]).then_inc(ring_full[g], 16)
            for b in range(NS):
                move(0, b, 0)
            sp.wait_ge(pv_s_ready, 2)
            for s in range(2):
                sp.dma_start(slot(s).rearrange("p (k n) -> p k n", k=KT // 2),
                             w_o[0].rearrange("(s k p) n -> s p k n", p=P, s=2)[s]).then_inc(ring_full[s], 16)

            def expert(e, odd, what):
                s = SLOTS[odd][what]
                src = expert_w[what]
                src = src[e] if isinstance(e, int) else src[ds(e, 1)].rearrange("a p k f -> p (a k) f")
                sp.dma_start(slot(s).rearrange("p (k f) -> p k f", k=FT if what == 2 else KT), src).then_inc(ring_full[s], 16)

            expert(0, 0, 0)
            expert(0, 0, 1)
            sp.wait_ge(bias_stored, 16)
            sp.wait_ge(sample_done, 1)

            def bias_load(h, b):
                sp.dma_start(bias_t[:, b], bass.AP(tensor=bias_dram.tensor, offset=h * (G * BV),
                                                   ap=[[1, P], [BV, G], [1, SEQ]])).then_inc(bias_landed[b], 16)

            for b in range(2):
                bias_load(b, b)
            with sp.Fori(1, PAIRS) as r:
                for b in range(2):
                    move(2, 0, r * 2 + b - 2)
                    sp.wait_ge(biased, r * 2 + b - 1)
                    bias_load(r * 2 + b, b)
            for n in range(2 * PAIRS - 2, 16):
                move(2, 0, n)
            sp.wait_ge(staged, 3 * PAIRS)
            expert(0, 0, 2)
            expert(1, 1, 0)
            sp.wait_ge(wo_ready, KT)
            expert(1, 1, 1)
            expert(1, 1, 2)

            def next_pair(r, rounds, moves):
                for odd in range(2):
                    for what in range(2):
                        sp.wait_ge(up_ready[odd], rounds)
                        expert(r * 2 + odd, odd, what)
                    for move_args in moves[odd::3]:
                        move(*move_args)
                for odd in range(2):
                    if odd:
                        sp.wait_ge(y_half, rounds * 2)
                        for move_args in moves[2::3]:
                            move(*move_args)
                    else:
                        sp.wait_ge(down_even_done, rounds)
                    expert(r * 2 + odd, odd, 2)

            def rounds_at(layer, p):
                return sp.value_load(rounds_i[0:1, ds(p + layer * (NP + 1), 1)], min_val=1, max_val=MAX_ROUNDS)

            sp.wait_ge(rounds_ready, 1)
            with sp.Fori(1, NP + 1) as p:
                next_pair(p, rounds_at(0, p), [(1, p - 1, n) for n in range(PIECES[1])]
                          + [(2, b, p + (8 * n - 1)) for b in (6, 7) for n in range(2)])
            for b in range(1, 6):
                move(2, b, 15)
            sp.wait_ge(rounds_ready, 2)
            with sp.Fori(1, NP) as p:
                next_pair(p + NP, rounds_at(1, p), [(2, b, p + 7) for b in range(1, 6)])
            for b in range(3):
                sp.wait_ge(y_ready, 2 * (b + 1))
                if b < 2:
                    sp.dma_start(y_prompt[0, b * P:(b + 1) * P, :], y_tok[:, b, :]).then_inc(y_sent, 16)
                else:
                    sp.dma_start(y_sample[:, 0, :], y_tok[0:NS, b, :]).then_inc(y_sent, 16)
            sp.wait_ge(y_sent, 48)
            sp.wait_ge(cache_copied, 16 * N_PIECES)

        @block.gpsimd
        def _(pool):
            pool.dma_start(pool_s[0, :, 0:STATE - 1, :].rearrange("b s c -> b (s c)"),
                           state_pool[0, :, 1:STATE, :].rearrange("b s c -> b (s c)")).then_inc(tokens_sent, 16)
            for g in range(G):
                for n in range(NQK):
                    pool.wait_ge(zn_ready, g * NZ + n + 1)
                    nc.gpsimd.tensor_copy(qk[:, g, n // KT, n % KT, :], zn[:, n % 4, :]).then_inc(zn_kept, 1)
                pool.wait_ge(z_stored, (g + 1) * NZ)
                dst = kv_p[g][0, 0].rearrange("t w h e -> t w (h e)")
                if g == 0:
                    pool.dma_start(dst[:, 0, :], k_tok[1]).then_inc(tokens_sent, 16)
                    for a in range(2):
                        pool.dma_start(dst[a * HD:(a + 1) * HD, 1, :], v_tok[a * HD:(a + 1) * HD, 1, g, :]).then_inc(tokens_sent, 16)
                else:
                    for b in range(2):
                        pool.dma_start(dst[b * P:(b + 1) * P, 0, :], k_tok[b]).then_inc(tokens_sent, 16)
                    pool.dma_start(dst[:, 1, :].rearrange("(b p) c -> p b c", p=P), v_tok[:, :, g, :]).then_inc(tokens_sent, 16)
                pool.dma_start(qkvs_dram[:, g], qkv_s[0:NS, :, :]).then_inc(tokens_sent, 16)
                pool.dma_start(kv_s[g][0, :, kv_s[g].shape[2] - 1].rearrange("b w h e -> b w (h e)"),
                               qkv_s[0:NS, 1:3, :]).then_inc(tokens_sent, 16)

            def stage(pair, u):
                one = ds(pair, 1)
                for blk in range(2):
                    nc.gpsimd.tensor_copy(q_st[:, u, :, blk * P:(blk + 1) * P][:, :, ::-1],
                                          qk[:, :, 0, one, blk * P:(blk + 1) * P].rearrange("p g a t -> p (g a) t"))
                nc.gpsimd.tensor_copy(k_st[:, u], qk[:, :, 1, one, 0:SEQ].rearrange("p g a t -> p (g a) t")).then_inc(staged, 2)
                nc.gpsimd.tensor_copy(v_st[:, u].rearrange("p b (g c) -> p b g c", g=G),
                                      v_tok[:, :, :, ds(pair * P, P)]).then_inc(staged, 1)

            def step(i, s, stages):
                h = i * 4 + s
                b = s % 2
                pool.wait_ge(inv_ready, h + 1)
                nc.gpsimd.tensor_tensor(probs[:, b, 0:G * P], probs[:, b, 0:G * P],
                                        small[:, 8 * b + 7:8 * b + 8].to_broadcast([P, G * P]), ALU.mult)
                nc.gpsimd.tensor_tensor(probs[:, b, G * P:], probs[:, b, G * P:],
                                        small[:, 8 * b + 6:8 * b + 7].to_broadcast([P, 2 * G * P]), ALU.mult).then_inc(probs_ready, 1)
                if stages:
                    pool.wait_ge(pv_ready, h)
                    stage(i * 2 + s // 2 + 1, (s // 2 + 1) % 2)

            pool.wait_ge(tokens_sent, 16 * 5 * G + 16)
            pool.wait_ge(sample_done, 1)
            stage(0, 0)
            stage(1, 1)
            for s in range(4):
                step(0, s, s == 2)
            with pool.Fori(1, H // 4 - 1) as i:
                for s in range(4):
                    step(i, s, s % 2 == 0)
            for s in range(4):
                step(H // 4 - 1, s, s == 0)

        @block.scalar
        def _(ac):
            dma = ac.dma_start
            dma(ident[:], c_ident).then_inc(consts_landed, 16)
            dma(bucket_p[0:NB + 1, :, :], c_bucket_prompt).then_inc(consts_landed, 16)
            dma(bucket_s[:], c_bucket_sample.rearrange("g n k -> n g k")).then_inc(consts_landed, 16)
            dma(tab[0:NB, :], rel_bias).then_inc(consts_landed, 16)
            dma(same_batch[:], c_same_batch).then_inc(consts_landed, 16)
            dma(rank[:], c_rank[:, 0:NE]).then_inc(consts_landed, 16)
            dma(slot_no[:], c_rank[:, NE:]).then_inc(consts_landed, 16)
            dma(tri[:], c_tri).then_inc(consts_landed, 16)
            for at, v in ((ATTN_G, attn_norm[0]), (POOL_G, pool_norm[0]), (POOL_B, pool_b[0]), (POOL_S, pool_scale[0])):
                dma(vec_rows[at:at + KT, :], v.rearrange("(k p) -> k p", p=P)).then_inc(vecs_landed, 16)
            dma(vec_rows[FFN_G[0]:FFN_G[0] + 2 * KT, :], ffn_norm.rearrange("l (k p) -> (l k) p", p=P)).then_inc(vecs_landed, 16)
            for w, v in enumerate((q_norm, k_norm)):
                for g in range(G):
                    for t in range(2):
                        dma(vec_rows[QK_G + 2 * g + w:QK_G + 2 * g + w + 1, t * HD:(t + 1) * HD], v[0, g:g + 1, :]).then_inc(vecs_landed, 16)
            for layer in range(LAYERS):
                dma(wr[:, layer, :, 0:NG], router_group_w[layer].rearrange("(k p) g -> p k g", p=P)).then_inc(consts_landed, 16)
                dma(wr[:, layer, :, NG:], router_expert_w[layer].rearrange("(k p) g -> p k g", p=P)).then_inc(consts_landed, 16)
            dma(brow[:, :, 0:NG], router_group_b.rearrange("(a l) g -> a l g", a=1)).then_inc(consts_landed, 16)
            dma(brow[:, :, NG:], router_expert_b.rearrange("(a l) g -> a l g", a=1)).then_inc(consts_landed, 16)

            ac.wait_ge(setup_done, 1)
            norm_root(ac, 0, h_filled, KT)
            ac.wait_ge(bias_copied, 1)
            dma(bias_dram.rearrange("h g d -> h g d"), bias_rows[0:H, :, :]).then_inc(bias_stored, 16)
            ac.wait_ge(bias_stored, 16)

            with ac.Fori(0, G) as g:
                for s in range(NZ + 4):
                    if s < NQK:
                        ac.wait_ge(z_ready, g * NZ + (s + 1))
                        nc.scalar.activation(zsq[:, s % 2, :], z_bank[s % 4][:, 0:T], ACT.Square).then_inc(zsq_ready, 1)
                    if 1 <= s <= NQK:
                        n = s - 1
                        ac.wait_ge(zsum_ready, g * NQK + (n + 1))
                        if n >= 2:
                            ac.wait_ge(zn_ready, g * NZ + (n - 1))
                        nc.scalar.activation(zr[:, n % 2, :], bank[2 + n % 2][:, 0:T], ACT.Sqrt, bias=epsc[:, 0:1],
                                             scale=1.0 / HD).then_inc(zroot_ready, 1)
                    if s >= 4:
                        n = s - 4
                        what, k = n // KT, n % KT
                        at = slice(k * P, (k + 1) * P)
                        src = bank[4 + n % 2]
                        if n == 0:
                            ac.wait_ge(tokens_sent, g * (16 * 5) + 16)
                        ac.wait_ge(z_turned, g * NZ + (n + 1))
                        if what == 1:
                            for b in range(2):
                                nc.scalar.activation(k_tok[b][:, at], src[:, b * P:(b + 1) * P], ACT.Copy)
                        if what == 2:
                            nc.scalar.activation(v_tok[:, :, ds(g, 1), at].rearrange("p b a c -> p (b a) c"),
                                                 src[:, 0:2 * P].rearrange("p (b c) -> p b c", b=2), ACT.Copy)
                        nc.scalar.activation(qkv_s[0:NS, what, at], src[0:NS, 2 * P:3 * P], ACT.Copy).then_inc(z_stored, 1)

            ac.wait_ge(tokens_sent, 16 * 5 * G + 16)
            ac.wait_ge(zn_kept, G * NQK)
            ac.wait_ge(z_turned, G * NZ)
            for b in range(NS):
                for w in range(2):
                    dma(qk_new[b * H:(b + 1) * H, w, :, :],
                        qkvs_dram[b, :, w, :].rearrange("g (h e) -> h g e", e=HD)).then_inc(qk_new_landed, 16)
            dma(v_new[0:NS, :, :], qkvs_dram[:, :, 2, :]).then_inc(v_new_landed, 16)
            for m in range(NS * G):
                half, g, b = m // (G * HALF), m // HALF % G, m % HALF
                if m >= 3:
                    ac.wait_ge(prod_ready, m - 2)
                dma(q_rep[:, m % 3, :], qkvs_dram[half * HALF + b, g, 0:1, :].to_broadcast([P, D])).then_inc(q_rep_landed[m % 3], 16)
            ac.wait_ge(s_rows_ready, 1)
            nc.scalar.activation(s_rows[:, :, :], s_rows[:, :, :], ACT.Exp, bias=small[:, 36:37],
                                 accum_out=small[:, 37:38]).then_inc(s_exp_ready, 1)

            def step(i, s, live, behind):
                h = i * 4 + s
                if live:
                    b = s % 2
                    ac.wait_ge(biased, h + 1)
                    nc.scalar.activation(probs[:, b, 0:G * P], probs[:, b, 0:G * P], ACT.Exp,
                                         bias=small[:, 8 * b + 3:8 * b + 4], accum_out=small[:, 8 * b + 5:8 * b + 6])
                    nc.scalar.activation(probs[:, b, G * P:], probs[:, b, G * P:], ACT.Exp,
                                         bias=small[:, 8 * b + 2:8 * b + 3], accum_out=small[:, 8 * b + 4:8 * b + 5]).then_inc(exps_ready, 1)
                if s % 2 == 1 and behind >= 3:
                    pair, u = i * 2 + (s - 3) // 2, (s - 3) // 2 % 2
                    ac.wait_ge(pv_ready, h - 1)
                    for blk in range(2):
                        last = nc.scalar.activation(oT[:, ds(pair, 1), blk * P:(blk + 1) * P],
                                                    bank[6 + u][:, blk * P:(blk + 1) * P][:, ::-1].rearrange("p (a t) -> p a t", a=1), ACT.Copy)
                    last.then_inc(o_copied, 1)
                if 1 <= behind <= H:
                    b = (s - 1) % 2
                    ac.wait_ge(pt_ready, h)
                    nc.scalar.activation(probsT[:, b, 4 * P:8 * P], bank[4][:, :], ACT.Copy)
                    nc.scalar.activation(probsT[:, b, 8 * P:], bank[5][:, 0:P], ACT.Copy).then_inc(pt_copied_act, 1)

            for s in range(4):
                step(0, s, True, s)
            with ac.Fori(1, H // 4) as i:
                for s in range(4):
                    step(i, s, True, 4)
            step(H // 4, 0, False, H)
            step(H // 4, 1, False, H + 1)

            ac.wait_ge(staged, 3 * PAIRS)
            dma(pw, pool_w[0].rearrange("g (k p) f -> p (g k) f", p=P)).then_inc(pool_landed, 16)
            for gi in range(4):
                dma(inv_count[:, gi, :], c_inv_count[gi:gi + 1, :].to_broadcast([P, SEQ])).then_inc(pool_landed, 16)
            dma(state[0:NS * STATE], state_pool[0].rearrange("b s c -> (b s) c")).then_inc(pool_landed, 16)
            dma(state_sum[0:NS * STATE], c_state_sum).then_inc(pool_landed, 16)

            for layer in range(LAYERS):
                if layer:
                    norm_root(ac, 2, layer_added, 1)
                    ac.wait_ge(pool_tok_ready, 1)
                    dma(pool_p[0, 0], pool_tok[0:STATE]).then_inc(pool_sent, 16)
                    dma(pool_s[0, :, STATE - 1, :], pool_tok[STATE:STATE + NS]).then_inc(pool_sent, 16)
                    norm_root(ac, 3, pool_y_added, KT)
                else:
                    norm_root(ac, 1, wo_added, KT)
                for b in range(3):
                    n = P if b < 2 else NS
                    ac.wait_ge(u_turned, 6 * layer + 2 * b + 2)
                    nc.scalar.activation(u_tok[0:n, b, D // 2:], bank[2 * b + 1][0:n, :], ACT.Copy).then_inc(u_tok_act, 1)
                for which in range(2):
                    ac.wait_ge(router_arg, 2 * layer + which + 1)
                    v = rt[:, 1, :, 0:NG] if which == 0 else rt[:, 12, :, 0:1]
                    nc.scalar.activation(v, v, ACT.Exp).then_inc(router_exp, 1)

                def one_round(q, p):
                    ac.wait_ge(place_made, q + 1)
                    nc.scalar.activation(place, bank[6][:, 0:T], ACT.Copy).then_inc(place_ready, 1)
                    ac.wait_ge(gathered, q * 2 + 2)
                    nc.scalar.activation(u_slots[:, KT // 2:, :], bank[1].rearrange("p (k n) -> p k n", n=P), ACT.Copy).then_inc(slots_act, 1)
                    for e in range(2):
                        rows = slice(e * CAP, (e + 1) * CAP)
                        ac.wait_ge(up_ready[e], q + 1)
                        nc.scalar.activation(silu[rows], bank[2][rows, :], ACT.Silu).then_inc(silu_ready, 1)
                    for a in range(2):
                        ac.wait_ge(y_half, q * 2 + (a + 1))
                        nc.scalar.activation(y_pair[:, a * 512:(a + 1) * 512], bank[4 + a][:, :], ACT.Copy).then_inc(y_copied, 1)

                all_rounds(ac, layer, one_round)
            ac.wait_ge(pool_sent, 32)

        @block.vector
        def _(dve):
            chain = Chain(dve, dve_own)
            vec = nc.vector
            vec.memset(ones[:], 1.0)
            vec.memset(epsc[:], RMS_EPS)
            vec.memset(small[:], 0.0)
            vec.memset(tab[NB:NB + 1, :], NEG)
            for a in range(2):
                for b in range(2):
                    last = vec.memset(blockones[a * HD:(a + 1) * HD, b * HD:(b + 1) * HD], float(a == b))
            last.then_inc(setup_done, 1)

            dve.wait_ge(vecs_turned, 1)
            chain(vec.tensor_copy(vecs[:], bank[7][:, 0:NVEC]))
            for g in range(G):
                c = QK_G + 2 * g
                last = vec.tensor_scalar(vecs[:, c:c + 1], vecs[:, c:c + 1], float(HD) ** -0.5, None, ALU.mult)
            chain(last)
            for k in range(KT):
                dve.wait_ge(x_turned, k + 1)
                vec.tensor_copy(hT[:, k, :], bank[k % 4][:, 0:T]).then_inc(h_filled, 1)
            dve.wait_ge(bias_made, 1)
            for g in range(G):
                last = vec.tensor_copy(bias_rows[0:H, g, :], bank[4 + g][0:H, 0:BV])
            last.then_inc(bias_copied, 1)
            dve.wait_ge(consts_landed, 16 * 14)
            for g in range(G):
                chain(vec.tensor_copy(tabrep[:, g, :, :], tab[0:NB, g * H:(g + 1) * H].rearrange("p (a h) -> p a h", a=1).to_broadcast([NB, NS, H])))
            norm_apply(dve, chain, 0, ATTN_G)

            with dve.Fori(0, G) as g:
                chain.enter(g, NQK + 1)
                chain(vec.tensor_copy(gains[:], vecs[:, ds(g * 2 + QK_G, 2)]))
                for n in range(NZ):
                    if n >= 4:
                        dve.wait_ge(z_turned, g * NZ + (n - 3))
                        if n - 4 < NQK:
                            dve.wait_ge(zn_kept, g * NQK + (n - 3))
                    if n < NQK:
                        dve.wait_ge(zroot_ready, g * NQK + (n + 1))
                        chain(vec.reciprocal(zri[:, n % 2, :], zr[:, n % 2, :]))
                        vec.scalar_tensor_tensor(out=zn[:, n % 4, :], in0=z_bank[n % 4][:, 0:T], scalar=gains[:, n // KT:n // KT + 1],
                                                 in1=zri[:, n % 2, :], op0=ALU.mult, op1=ALU.mult).then_inc(zn_ready, 1)
                    else:
                        dve.wait_ge(z_ready, g * NZ + (n + 1))
                        vec.tensor_copy(zn[:, n % 4, :], z_bank[n % 4][:, 0:T]).then_inc(zn_ready, 1)
                dve.wait_ge(z_turned, g * NZ + NZ)
                dve.wait_ge(zn_kept, g * NQK + NQK)
            chain.leave(G)

            dve.wait_ge(tokens_sent, 16 * 5 * G + 16)
            for m in range(NS * G):
                half, g, b = m // (G * HALF), m // HALF % G, m % HALF
                dve.wait_ge(q_rep_landed[m % 3], 16 * (m // 3 + 1))
                if b == 0:
                    dve.wait_ge(ring_full[g], 16 * (RING_KV + half + 1))
                vec.tensor_tensor(prod[:, m % 2, :], slot(g)[:, b * D:(b + 1) * D], q_rep[:, m % 3, :], ALU.mult).then_inc(prod_ready, 1)
                dve.wait_ge(prod_ready, m + 1)
                at = (half * HALF + b) * H
                last = vec.tensor_reduce(out=s_keys[:, g, at:at + H], in_=prod[:, m % 2, :].rearrange("p (h e) -> p h e", e=HD),
                                         axis=AX_X, op=ALU.add)
            last.then_inc(s_keys_ready, 1)
            dve.wait_ge(qk_new_landed, 16 * 2 * NS)
            chain(vec.tensor_tensor(qk_prod, qk_new[:, 0], qk_new[:, 1], ALU.mult))
            chain(vec.tensor_reduce(out=small[:, 32:32 + G], in_=qk_prod, axis=AX_X, op=ALU.add))
            dve.wait_ge(s_turned, 1)
            chain(vec.tensor_copy(s_rows, bank[0][:, 0:G * (P + 1)].rearrange("p (g k) -> p g k", g=G)))
            chain(vec.tensor_tensor(s_rows[:, :, P], s_rows[:, :, P], small[:, 32:32 + G], ALU.add))
            chain(vec.tensor_reduce(out=small[:, 35:36], in_=s_rows.rearrange("p g k -> p (g k)"), axis=AX_X, op=ALU.max))
            vec.tensor_scalar(small[:, 36:37], small[:, 35:36], -1.0, None, ALU.mult).then_inc(s_rows_ready, 1)
            dve.wait_ge(s_exp_ready, 1)
            chain(vec.reciprocal(small[:, 38:39], small[:, 37:38]))
            chain(vec.tensor_scalar(s_rows, s_rows, small[:, 38:39], None, ALU.mult))
            for g in range(G):
                last = vec.tensor_scalar(p_newm[:, g, :], same_batch[:], s_rows[:, g, P:P + 1], None, ALU.mult)
            last.then_inc(p_ready, 1)
            dve.wait_ge(p_turned, 1)
            vec.tensor_copy(p_keys, bank[1][:, 0:G * BH].rearrange("p (g k) -> p g k", g=G))
            vec.tensor_copy(p_newT[0:NS], bank[2][0:NS, 0:G * BH].rearrange("p (g k) -> p g k", g=G)).then_inc(p_keys_ready, 1)
            dve.wait_ge(pv_s_ready, 2)
            chain(vec.tensor_copy(o_new, bank[3][:, 0:KT * NS * 2].rearrange("p (k b t) -> p k b t", k=KT, t=2)))
            for t in range(2):
                rows = slice(t * HD, (t + 1) * HD)
                last = vec.tensor_tensor(oT[rows, :, SEQ:], bank[4][rows, 0:KT * NS * 2].rearrange("p (k b t) -> p k b t", k=KT, t=2)[:, :, :, t],
                                         o_new[rows, :, :, t], ALU.add)
            last.then_inc(sample_done, 1)

            def step(i, s, live, behind):
                h = i * 4 + s
                b = s % 2
                if live:
                    dve.wait_ge(scores_ready, h + 1)
                    dve.wait_ge(bias_landed[b], (i * 2 + s // 2 + 1) * 16)
                    c = 8 * b
                    vec.memset(small[:, 60:61], 0.0)
                    vec.tensor_tensor_reduce(out=probs[:, b, 0:G * P].rearrange("p (g k) -> p g k", g=G), in0=bank[0][:, 0:G * P].rearrange("p (g k) -> p g k", g=G),
                                             in1=bias_t[:, b, :, P:], scale=1.0, scalar=NEG, op0=ALU.add, op1=ALU.max,
                                             accum_out=small[:, 16 + c:17 + c])
                    vec.tensor_tensor_reduce(out=probs[:, b, 3 * P:7 * P], in0=bank[1][:, :], in1=bias_t[:, b, 0:2, :].rearrange("p g k -> p (g k)"),
                                             scale=1.0, scalar=NEG, op0=ALU.add, op1=ALU.max, accum_out=small[:, 17 + c:18 + c])
                    chain(vec.tensor_tensor_reduce(out=probs[:, b, 7 * P:], in0=bank[2][:, 0:SEQ], in1=bias_t[:, b, 2, :],
                                                   scale=1.0, scalar=NEG, op0=ALU.add, op1=ALU.max, accum_out=small[:, 18 + c:19 + c]))
                    vec.tensor_scalar(small[:, c + 3:c + 4], small[:, 16 + c:17 + c], -1.0, None, ALU.mult)
                    vec.tensor_scalar(small[:, c + 2:c + 3], small[:, 17 + c:18 + c], small[:, 18 + c:19 + c], -1.0,
                                      ALU.max, ALU.mult).then_inc(biased, 1)
                if 1 <= behind <= H:
                    dve.wait_ge(pt_ready, h)
                    vec.tensor_copy(probsT[:, 1 - b, 0:4 * P], bank[3][:, :]).then_inc(pt_copied_dve, 1)
                if live:
                    dve.wait_ge(exps_ready, h + 1)
                    vec.reciprocal(small[:, 8 * b + 6:8 * b + 8], small[:, 8 * b + 4:8 * b + 6]).then_inc(inv_ready, 1)

            for s in range(4):
                step(0, s, True, s)
            with dve.Fori(1, H // 4) as i:
                chain.enter(i, 4, 1)
                for s in range(4):
                    step(i, s, True, 4)
            chain.leave(H // 4)
            step(H // 4, 0, False, H)

            for m in range(KT):
                dve.wait_ge(wo_ready, m + 1)
                vec.tensor_tensor(hT[:, m, :], bank[m % 2][:, 0:T], hT[:, m, :], ALU.add).then_inc(wo_added, 1)

            def wide(v, n):
                return v.to_broadcast([P, 3, n])

            def router(layer):
                lg, le = logits[:, :, 0:NG], logits[:, :, NG:]
                r = [rt[:, n] for n in range(16)]
                for b in range(3):
                    n = P if b < 2 else NS
                    dve.wait_ge(u_turned, 6 * layer + 2 * b + 1)
                    vec.tensor_copy(u_tok[0:n, b, 0:D // 2], bank[2 * b][0:n, :]).then_inc(u_tok_dve, 1)
                chain(vec.memset(logits[:, 2, :], 0.0))
                dve.wait_ge(logits_made, layer + 1)
                vec.tensor_copy(logits[:, 0:2, :], bank[6][:, 0:2 * NR].rearrange("p (t n) -> p t n", t=2))
                chain(vec.tensor_copy(logits[0:NS, 2, :], bank[6][0:NS, 2 * NR:3 * NR]))
                gmax = r[0][:, :, 0:1]
                chain(vec.tensor_reduce(out=gmax, in_=lg, axis=AX_X, op=ALU.max))
                vec.tensor_tensor(r[1][:, :, 0:NG], lg, wide(gmax, NG), ALU.subtract).then_inc(router_arg, 1)
                chain(vec.tensor_tensor(r[2][:, :, 0:NG], lg, wide(gmax, NG), ALU.is_equal))
                rk = rank[:, :].rearrange("p (a n) -> p a n", a=1)
                chain(vec.tensor_tensor(r[2][:, :, 0:NG], r[2][:, :, 0:NG], rk[:, :, 0:NG].to_broadcast([P, 3, NG]), ALU.mult))
                chain(vec.tensor_reduce(out=r[3][:, :, 0:1], in_=r[2][:, :, 0:NG], axis=AX_X, op=ALU.max))
                chain(vec.tensor_tensor(r[2][:, :, 0:NG], r[2][:, :, 0:NG], wide(r[3][:, :, 0:1], NG), ALU.is_equal))
                for g in range(NG):
                    last = vec.tensor_copy(r[4][:, :, g * EPG:(g + 1) * EPG], wide(r[2][:, :, g:g + 1], EPG))
                chain(last)
                chain(vec.tensor_tensor(r[5], le, r[4], ALU.mult))
                chain(vec.tensor_scalar(r[4], r[4], -1.0, -NEG, ALU.add, ALU.mult))
                chain(vec.tensor_tensor(r[5], r[5], r[4], ALU.add))

                def first_of_largest(src, top, out):
                    chain(vec.tensor_reduce(out=top, in_=src, axis=AX_X, op=ALU.max))
                    chain(vec.tensor_tensor(out, src, wide(top, NE), ALU.is_equal))
                    chain(vec.tensor_tensor(out, out, rk.to_broadcast([P, 3, NE]), ALU.mult))
                    chain(vec.tensor_reduce(out=r[3][:, :, 0:1], in_=out, axis=AX_X, op=ALU.max))
                    chain(vec.tensor_tensor(out, out, wide(r[3][:, :, 0:1], NE), ALU.is_equal))

                first_of_largest(r[5], r[6][:, :, 0:1], r[7])
                chain(vec.tensor_scalar(r[8], r[7], 2 * NEG, None, ALU.mult))
                chain(vec.tensor_tensor(r[8], r[8], r[5], ALU.add))
                first_of_largest(r[8], r[9][:, :, 0:1], r[10])
                vec.tensor_tensor(r[12][:, :, 0:1], r[9][:, :, 0:1], r[6][:, :, 0:1], ALU.subtract).then_inc(router_arg, 1)
                dve.wait_ge(router_exp, 2 * layer + 2)
                chain(vec.tensor_reduce(out=r[11][:, :, 0:1], in_=r[1][:, :, 0:NG], axis=AX_X, op=ALU.add))
                chain(vec.tensor_scalar(r[13][:, :, 0:1], r[12][:, :, 0:1], 1.0, None, ALU.add))
                chain(vec.tensor_tensor(r[13][:, :, 0:1], r[13][:, :, 0:1], r[11][:, :, 0:1], ALU.mult))
                chain(vec.reciprocal(r[14][:, :, 0:1], r[13][:, :, 0:1]))
                chain(vec.tensor_tensor(r[15][:, :, 0:1], r[14][:, :, 0:1], r[12][:, :, 0:1], ALU.mult))
                vec.tensor_tensor(chosen, r[7], r[10], ALU.add).then_inc(chosen_ready, 1)
                chain(vec.tensor_tensor(r[7], r[7], wide(r[14][:, :, 0:1], NE), ALU.mult))
                chain(vec.tensor_tensor(r[10], r[10], wide(r[15][:, :, 0:1], NE), ALU.mult))
                chain(vec.tensor_tensor(gates, r[7], r[10], ALU.add))
                dve.wait_ge(positions_made, layer + 1)
                chain(vec.memset(position[:, 2, :], 0.0))
                vec.tensor_tensor(position[:, 0:2, :], bank[6][:, 64:64 + 2 * NE].rearrange("p (b e) -> p b e", b=2), chosen[:, 0:2, :], ALU.mult)
                chain(vec.tensor_tensor(position[0:NS, 2, :], bank[6][0:NS, 64 + 2 * NE:64 + 3 * NE], chosen[0:NS, 2, :], ALU.mult))
                chain(vec.tensor_scalar(position, position, -1.0, None, ALU.add))
                chain(vec.tensor_reduce(out=pair_max, in_=bank[6][:, 128:128 + NE].rearrange("p (n a) -> p n a", a=2), axis=AX_X, op=ALU.max))
                chain(vec.tensor_scalar(pair_rounds, pair_max, float(CAP), 1.0, ALU.is_gt, ALU.add))
                for full in range(2 * CAP, T, CAP):
                    chain(vec.scalar_tensor_tensor(out=pair_rounds, in0=pair_max, scalar=float(full), in1=pair_rounds, op0=ALU.is_gt, op1=ALU.add))
                rf = rounds_f[:, layer, :]
                chain(vec.tensor_copy(rf[:, 0:1], rounds_f[:, 0, NP:]) if layer else vec.memset(rf[:, 0:1], 0.0))
                for p in range(NP):
                    chain(vec.tensor_tensor(rf[:, p + 1:p + 2], rf[:, p:p + 1], pair_rounds[:, p:p + 1], ALU.add))
                vec.tensor_copy(rounds_i[0:1, layer * (NP + 1):(layer + 1) * (NP + 1)], rounds_f[0:1, layer, :]).then_inc(rounds_ready, 1)

            def pair_start(layer, p):
                e = p * 2
                chain(vec.tensor_copy(pair_at[:, 0], position[:, :, ds(e, 2)]))
                chain(vec.tensor_copy(pair_at[:, 1], gates[:, :, ds(e, 2)]))
                vec.memset(small[:, 62:63], 0.0)

            def one_round(q, p):
                for b in range(3):
                    n = P if b < 2 else NS
                    for e in range(2):
                        at = slice(e * CAP, (e + 1) * CAP)
                        vec.tensor_scalar(pick_gate[0:n, b, at], slot_no[0:n, :], pair_at[0:n, 0, b, e:e + 1], pair_at[0:n, 1, b, e:e + 1],
                                          ALU.is_equal, ALU.mult)
                        last = vec.tensor_scalar(pick[0:n, b, at], slot_no[0:n, :], pair_at[0:n, 0, b, e:e + 1], None, ALU.is_equal)
                last.then_inc(pick_ready, 1)
                dve.wait_ge(pick_ready, q + 1)
                vec.tensor_scalar(pair_at[:, 0], pair_at[:, 0], -float(CAP), None, ALU.add).then_inc(shifted, 1)
                dve.wait_ge(shifted, q + 1)
                dve.wait_ge(gathered, q * 2 + 1)
                vec.tensor_copy(u_slots[:, 0:KT // 2, :], bank[0].rearrange("p (k n) -> p k n", n=P)).then_inc(slots_dve, 1)
                for e in range(2):
                    rows = slice(e * CAP, (e + 1) * CAP)
                    dve.wait_ge(silu_ready, q * 2 + (e + 1))
                    vec.tensor_tensor(hid_rows[rows], bank[3][rows, :], silu[rows], ALU.mult).then_inc(hid_rows_ready, 1)
                    dve.wait_ge(hid_turned, q * 2 + (e + 1))
                    vec.tensor_copy(hid[:, :, e, :], bank[0][:, e * FT * CAP:(e + 1) * FT * CAP].rearrange("p (f n) -> p f n", f=FT)).then_inc(hid_ready, 1)
                for m in range(KT):
                    dve.wait_ge(spread, q * KT + (m + 1))
                    vec.tensor_tensor(hT[:, m, :], bank[6 + m % 2][:, 0:T], hT[:, m, :], ALU.add).then_inc(spread_added, 1)

            def experts(layer):
                dve.wait_ge(rounds_ready, layer + 1)
                all_rounds(dve, layer, one_round, pair_start, chain)
                vec.memset(small[:, 61:62], 0.0).then_inc(layer_added, 1)

            norm_apply(dve, chain, 1, FFN_G[0])
            router(0)
            experts(0)

            norm_apply(dve, chain, 2, POOL_G)
            dve.wait_ge(u_ready, 3)
            dve.wait_ge(pool_landed, 16 * 7)
            chain(vec.memset(ext[:, :, :, 0:PAD], 0.0))
            for gi, win in enumerate(POOL_WINDOWS):
                u2 = uT[:, 2 * gi:2 * gi + 2, 0:SEQ]
                chain(vec.tensor_copy(ext[:, 0, :, PAD:], u2))
                at, sh = 0, 1
                while sh < win:
                    chain(vec.tensor_tensor(ext[:, 1 - at, :, PAD:], ext[:, at, :, PAD:], ext[:, at, :, PAD - sh:PAD + SEQ - sh], ALU.add))
                    at, sh = 1 - at, sh * 2
                chain(vec.tensor_tensor(ext[:, 1 - at, :, PAD:], ext[:, at, :, PAD:], inv_count[:, gi:gi + 1, :].to_broadcast([P, 2, SEQ]), ALU.mult))
                chain(vec.tensor_tensor(pool_z[:, 2 * gi:2 * gi + 2, 0:SEQ], ext[:, 1 - at, :, PAD:], u2, ALU.subtract))
                if gi == 0:
                    dve.wait_ge(state_summed, 1)
                us = uT[:, 2 * gi:2 * gi + 2, SEQ:]
                chain(vec.tensor_tensor(zs_tmp, bank[0][:, 2 * gi * NS:(2 * gi + 2) * NS].rearrange("p (k b) -> p k b", k=2), us, ALU.add))
                vec.scalar_tensor_tensor(out=pool_z[:, 2 * gi:2 * gi + 2, SEQ:], in0=zs_tmp, scalar=1.0 / win, in1=us,
                                         op0=ALU.mult, op1=ALU.subtract).then_inc(pooled, 1)
                dve.wait_ge(pooled, gi + 1)
            for a in range(2):
                dve.wait_ge(pool_turned, a + 1)
                last = vec.tensor_copy(pool_tok[0:STATE + NS, a * 512:(a + 1) * 512], bank[3 + a][0:STATE + NS, :])
            last.then_inc(pool_tok_ready, 1)
            for m in range(KT):
                dve.wait_ge(pool_y_ready, m + 1)
                chain(vec.tensor_scalar(ybuf[:, m % 2, :], bank[1 + m % 2][:, 0:T], vecs[:, POOL_B + m:POOL_B + m + 1],
                                        vecs[:, POOL_S + m:POOL_S + m + 1], ALU.add, ALU.mult))
                vec.tensor_tensor(hT[:, m, :], hT[:, m, :], ybuf[:, m % 2, :], ALU.add).then_inc(pool_y_added, 1)

            norm_apply(dve, chain, 3, FFN_G[1])
            router(1)
            experts(1)

            for b in range(3):
                n = P if b < 2 else NS
                for a in range(2):
                    dve.wait_ge(y_turned, 2 * b + a + 1)
                    vec.tensor_copy(y_tok[0:n, b, a * 512:(a + 1) * 512], bank[2 * b + a][0:n, :]).then_inc(y_ready, 1)

        @block.tensor
        def _(pe):
            mm = nc.tensor.matmul
            pe.wait_ge(consts_landed, 16 * 14)
            pe.wait_ge(setup_done, 1)
            pe.wait_ge(vecs_landed, 16 * (5 + 4 * G))
            nc.tensor.transpose(bank[7][:, 0:NVEC], vec_rows[:], ident[0:NVEC, 0:NVEC]).then_inc(vecs_turned, 1)
            pe.wait_ge(x_landed, 32)
            for k in range(KT):
                if k >= 4:
                    pe.wait_ge(h_filled, k - 3)
                for b in range(2):
                    nc.tensor.transpose(bank[k % 4][:, b * P:(b + 1) * P], x_tok[:, b, k * P:(k + 1) * P], ident[:])
                nc.tensor.transpose(bank[k % 4][:, SEQ:T], x_tok[0:NS, 2, k * P:(k + 1) * P], ident[0:NS, 0:NS]).then_inc(x_turned, 1)
            for g in range(G):
                last = mm(bank[4 + g][0:H, 0:BV], tab[:, g * H:(g + 1) * H], bucket_p[0:NB + 1, g, :], start=True, stop=True)
            last.then_inc(bias_made, 1)
            norm_sums(pe, 0)
            pe.wait_ge(u_ready, 1)
            pe.wait_ge(bias_copied, 1)

            with pe.Fori(0, G) as g:
                for s in range(NZ + 3):
                    if s < NZ:
                        c = s // TPC
                        if s % TPC == 0:
                            pe.wait_ge(ring_full[c % 3], g * 32 + 16 * (c // 3 + 1))
                        if s >= 4:
                            pe.wait_ge(zn_ready, g * NZ + (s - 3))
                        w = slot(c % 3).rearrange("p (k n) -> p k n", k=KT)
                        at = s % TPC * P
                        for k in range(KT):
                            last = mm(z_bank[s % 4][:, 0:T], w[:, k, at:at + P], uT[:, k, :], start=(k == 0), stop=(k == KT - 1))
                        last.then_inc(z_ready, 1)
                    if 1 <= s <= NQK:
                        n = s - 1
                        pe.wait_ge(zsq_ready, g * NQK + (n + 1))
                        if n >= 2:
                            pe.wait_ge(zroot_ready, g * NQK + (n - 1))
                        mm(bank[2 + n % 2][:, 0:T], blockones[:], zsq[:, n % 2, :], start=True, stop=True).then_inc(zsum_ready, 1)
                    if s >= 3:
                        n = s - 3
                        pe.wait_ge(zn_ready, g * NZ + (n + 1))
                        if n >= 2:
                            pe.wait_ge(z_stored, g * NZ + (n - 1))
                        dst = bank[4 + n % 2]
                        if n >= KT:
                            for b in range(2):
                                nc.tensor.transpose(dst[:, b * P:(b + 1) * P], zn[:, n % 4, b * P:(b + 1) * P], ident[:])
                        nc.tensor.transpose(dst[0:NS, 2 * P:3 * P], zn[:, n % 4, SEQ:T], ident[:]).then_inc(z_turned, 1)
                pe.wait_ge(z_stored, g * NZ + NZ)

            pe.wait_ge(s_keys_ready, 1)
            for g in range(G):
                at = g * (P + 1)
                mm(bank[0][:, at:at + P + 1], tabrep[:, g, :, :].rearrange("p b h -> p (b h)"), bucket_s[:, g, :], start=True, stop=False)
                last = mm(bank[0][:, at:at + P], s_keys[:, g, :], ident[:], start=False, stop=True)
            last.then_inc(s_turned, 1)
            pe.wait_ge(p_ready, 1)
            for g in range(G):
                nc.tensor.transpose(bank[1][:, g * BH:(g + 1) * BH], s_rows[:, g, 0:P], ident[:])
                last = nc.tensor.transpose(bank[2][0:NS, g * BH:(g + 1) * BH], p_newm[:, g, :], ident[:])
            last.then_inc(p_turned, 1)
            pe.wait_ge(p_keys_ready, 1)
            pe.wait_ge(v_new_landed, 16)
            for j in range(KT):
                for g in range(G):
                    mm(bank[3][:, j * 2 * NS:(j + 1) * 2 * NS], v_new[0:NS, g, j * P:(j + 1) * P],
                       p_newT[0:NS, g, :].rearrange("p (b h) -> p b h", b=NS)[:, :, 2 * j:2 * j + 2], start=(g == 0), stop=(g == G - 1))
            for half in range(2):
                for g in range(G):
                    pe.wait_ge(ring_full[g], 16 * (RING_KV + 2 + half + 1))
                for b4 in range(HALF):
                    b = half * HALF + b4
                    for j in range(KT):
                        at = (j * NS + b) * 2
                        for g in range(G):
                            last = mm(bank[4][:, at:at + 2], slot(g)[:, b4 * D + j * P:b4 * D + (j + 1) * P],
                                      p_keys[:, g, b * H + 2 * j:b * H + 2 * j + 2], start=(g == 0), stop=(g == G - 1))
                last.then_inc(pv_s_ready, 1)

            def step(i, s, live, behind):
                h = i * 4 + s
                if live:
                    u, t = s // 2 % 2, s % 2
                    rows = slice(t * HD, (t + 1) * HD)
                    pe.wait_ge(staged, (i * 2 + s // 2 + 1) * 3)
                    pe.wait_ge(biased, h)
                    for g in range(G):
                        mm(bank[0][:, g * P:(g + 1) * P], q_st[rows, u, g, 0:P], k_st[rows, u, g, 0:P], start=True, stop=True)
                    for g in range(G):
                        at = g % 2 * SEQ
                        last = mm(bank[1 + g // 2][:, at:at + SEQ], q_st[rows, u, g, P:], k_st[rows, u, g, :], start=True, stop=True)
                    last.then_inc(scores_ready, 1)
                if 1 <= behind <= H:
                    u, t = (s - 1) // 2 % 2, (s - 1) % 2
                    rows = slice(t * HD, (t + 1) * HD)
                    pe.wait_ge(probs_ready, h)
                    for n in range(3 * G):
                        last = nc.tensor.transpose(bank[3 + n // 4][:, n % 4 * P:(n % 4 + 1) * P], probs[:, t, n * P:(n + 1) * P], ident[:])
                    last.then_inc(pt_ready, 1)
                    pe.wait_ge(pt_copied_dve, h)
                    pe.wait_ge(pt_copied_act, h)
                    for g in range(G):
                        mm(bank[6 + u][rows, 0:P], v_st[:, u, 0, g * P + t * HD:g * P + (t + 1) * HD],
                           probsT[:, t, g * P:(g + 1) * P], start=(g == 0), stop=(g == G - 1))
                    for g in range(G):
                        for kb in range(2):
                            n = G + 2 * g + kb
                            last = mm(bank[6 + u][rows, P:2 * P], v_st[:, u, kb, g * P + t * HD:g * P + (t + 1) * HD],
                                      probsT[:, t, n * P:(n + 1) * P], start=(n == G), stop=(n == 3 * G - 1))
                    last.then_inc(pv_ready, 1)

            pe.wait_ge(sample_done, 1)
            for s in range(4):
                step(0, s, True, s)
            with pe.Fori(1, H // 4) as i:
                for s in range(4):
                    step(i, s, True, 4)
            step(H // 4, 0, False, H)

            pe.wait_ge(o_copied, PAIRS)
            for s in range(2):
                pe.wait_ge(ring_full[s], 16 * (RING_WO + 1))
            for m in range(KT):
                if m >= 2:
                    pe.wait_ge(wo_added, m - 1)
                for f in range(KT):
                    w = slot(f // 4).rearrange("p (k n) -> p k n", k=4)
                    last = mm(bank[m % 2][:, 0:T], w[:, f % 4, m * P:(m + 1) * P], oT[:, f, :], start=(f == 0), stop=(f == KT - 1))
                last.then_inc(wo_ready, 1)

            def router(layer, n_norm):
                pe.wait_ge(u_ready, n_norm + 1)
                for b in range(3):
                    n = P if b < 2 else NS
                    out = bank[6][0:n, b * NR:(b + 1) * NR]
                    for k in range(KT):
                        mm(out, uT[:, k, b * P:b * P + n], wr[:, layer, k, :], start=(k == 0), stop=False)
                    last = mm(out, ones[0:1, 0:n], brow[:, layer, :], start=False, stop=True)
                last.then_inc(logits_made, 1)
                for b in range(3):
                    n = P if b < 2 else NS
                    for k in range(KT):
                        last = nc.tensor.transpose(bank[2 * b + k // 4][0:n, k % 4 * P:(k % 4 + 1) * P], uT[:, k, b * P:b * P + n], ident[:])
                        if k % 4 == 3:
                            last.then_inc(u_turned, 1)
                pe.wait_ge(chosen_ready, layer + 1)
                sizes = (P, P, NS)
                for b in range(3):
                    out = bank[6][0:sizes[b], 64 + b * NE:64 + (b + 1) * NE]
                    for a in range(b + 1):
                        w = tri if a == b else ones
                        mm(out, w[0:sizes[a], 0:sizes[b]], chosen[0:sizes[a], a, :], start=(a == 0), stop=(a == b))
                for a in range(3):
                    last = mm(bank[6][:, 128:128 + NE], ones[0:sizes[a], :], chosen[0:sizes[a], a, :], start=(a == 0), stop=(a == 2))
                last.then_inc(positions_made, 1)
                pe.wait_ge(u_tok_dve, 3 * layer + 3)
                pe.wait_ge(u_tok_act, 3 * layer + 3)

            weights = [(slot(a).rearrange("p (k f) -> p k f", k=KT), slot(b).rearrange("p (k f) -> p k f", k=KT),
                        slot(c).rearrange("p (k f) -> p k f", k=FT)) for a, b, c in SLOTS]

            def one_round(q, p, layer):
                def weights_there(s):
                    pe.wait_ge(ring_full[s], p * 16 + 16 * (layer * NP + FIRST_USES[s] + 1))

                pe.wait_ge(pick_ready, q + 1)
                sizes = (P, P, NS)
                for m in range(KT):
                    for b in range(3):
                        last = mm(bank[m // 4][:, m % 4 * P:(m % 4 + 1) * P], u_tok[0:sizes[b], b, m * P:(m + 1) * P],
                                  pick[0:sizes[b], b, :], start=(b == 0), stop=(b == 2))
                    if m % 4 == 3:
                        last.then_inc(gathered, 1)
                for b in range(3):
                    last = nc.tensor.transpose(bank[6][:, b * P:b * P + sizes[b]], pick_gate[0:sizes[b], b, :], ident[0:sizes[b], 0:sizes[b]])
                last.then_inc(place_made, 1)
                pe.wait_ge(slots_dve, q + 1)
                pe.wait_ge(slots_act, q + 1)

                def turn_hidden(e):
                    rows = slice(e * CAP, (e + 1) * CAP)
                    pe.wait_ge(hid_rows_ready, q * 2 + (e + 1))
                    for f in range(FT):
                        at = (e * FT + f) * CAP
                        if f == 0:
                            mm(bank[0][:, at:at + CAP], hid_rows[rows, f * P:(f + 1) * P], ident[rows, rows], start=True, stop=True)
                        else:
                            last = nc.tensor.transpose(bank[0][:, at:at + CAP], hid_rows[rows, f * P:(f + 1) * P], ident[rows, rows])
                    last.then_inc(hid_turned, 1)

                def down(e, a):
                    weights_there(SLOTS[e][2])
                    pe.wait_ge(hid_ready, q * 2 + (e + 1))
                    for f in range(FT):
                        last = mm(bank[4 + a][e * CAP:(e + 1) * CAP, :], hid[:, f, e, :], weights[e][2][:, f, a * 512:(a + 1) * 512],
                                  start=(f == 0), stop=(f == FT - 1))
                    return last

                for e in range(2):
                    rows = slice(e * CAP, (e + 1) * CAP)
                    for w in range(2):
                        weights_there(SLOTS[e][w])
                        for k in range(KT):
                            last = mm(bank[2 + w][rows, :], u_slots[:, k, rows], weights[e][w][:, k, :], start=(k == 0), stop=(k == KT - 1))
                        if e == 1 and w == 0:
                            turn_hidden(0)
                    last.then_inc(up_ready[e], 1)
                down(0, 0)
                turn_hidden(1)
                down(0, 1).then_inc(down_even_done, 1)
                down(1, 0).then_inc(y_half, 1)
                down(1, 1).then_inc(y_half, 1)
                pe.wait_ge(place_ready, q + 1)
                for m in range(KT):
                    if m % 4 == 0:
                        pe.wait_ge(y_copied, q * 2 + (m // 4 + 1))
                    if m >= 2:
                        pe.wait_ge(spread_added, q * KT + (m - 1))
                    mm(bank[6 + m % 2][:, 0:T], y_pair[:, m * P:(m + 1) * P], place, start=True, stop=True).then_inc(spread, 1)

            def experts(layer):
                all_rounds(pe, layer, lambda q, p: one_round(q, p, layer))

            norm_sums(pe, 1)
            router(0, 1)
            experts(0)

            norm_sums(pe, 2)
            pe.wait_ge(pool_landed, 16 * 7)
            for k in range(KT):
                last = mm(bank[0][:, k * NS:(k + 1) * NS], state[0:NS * STATE, k * P:(k + 1) * P], state_sum[0:NS * STATE, k // 2, :], start=True, stop=True)
            last.then_inc(state_summed, 1)
            pe.wait_ge(u_ready, 3)
            for k in range(KT):
                last = nc.tensor.transpose(bank[3 + k // 4][0:STATE + NS, k % 4 * P:(k % 4 + 1) * P], uT[:, k, SEQ - STATE:T], ident[:])
                if k % 4 == 3:
                    last.then_inc(pool_turned, 1)
            for m in range(KT):
                gi, ft = m // 2, m % 2
                pe.wait_ge(pooled, gi + 1)
                if m >= 2:
                    pe.wait_ge(pool_y_added, m - 1)
                for ct in range(2):
                    last = mm(bank[1 + m % 2][:, 0:T], pw[:, 2 * gi + ct, ft * P:(ft + 1) * P], pool_z[:, 2 * gi + ct, :], start=(ct == 0), stop=(ct == 1))
                last.then_inc(pool_y_ready, 1)

            norm_sums(pe, 3)
            router(1, 3)
            experts(1)

            pe.wait_ge(layer_added, LAYERS)
            for b in range(3):
                n = P if b < 2 else NS
                for k in range(KT):
                    last = nc.tensor.transpose(bank[2 * b + k // 4][0:n, k % 4 * P:(k % 4 + 1) * P], hT[:, k, b * P:b * P + n], ident[:])
                    if k % 4 == 3:
                        last.then_inc(y_turned, 1)


def constants():
    import math

    import numpy as np

    n_buckets, max_distance, seq, ns = 32, 2048, 256, 8
    exact = n_buckets // 2

    def bucket(dist):
        df = np.maximum(dist, exact).astype(np.float32)
        large = exact + (np.log(df / np.float32(exact)) / np.float32(math.log(max_distance / exact))
                         * np.float32(n_buckets - exact)).astype(np.int32)
        return np.where(dist < exact, dist, np.minimum(large, n_buckets - 1))

    one = np.float32(1)
    dist = 2 * P - 1 - np.arange(3 * P)
    bp = np.zeros((n_buckets + 1, 3, 3 * P), np.float32)
    for g, (w, d) in enumerate(zip(WINDOWS, DILATIONS)):
        ok = (dist >= 0) & (dist <= w) & (dist % d == 0)
        bp[bucket(np.maximum(dist, 0))[ok], g, np.nonzero(ok)[0]] = one
        bp[n_buckets, g, ~ok] = one
    bs = np.zeros((3, n_buckets, P + 1), np.float32)
    for g, d in enumerate(DILATIONS):
        bs[g, bucket((P - np.arange(P + 1)) * d), np.arange(P + 1)] = one
    same = np.repeat(np.eye(ns, dtype=np.float32), P // ns, axis=0)
    rank = np.tile(np.concatenate([16 - np.arange(16), np.arange(64)]).astype(np.float32), (P, 1))
    inv = np.stack([one / np.minimum(w, np.arange(seq) + 1).astype(np.float32) for w in POOL_WINDOWS]).astype(np.float32)
    n_state = POOL_WINDOWS[-1] - 1
    ssum = np.zeros((ns, n_state, 4, ns), np.float32)
    for gi, w in enumerate(POOL_WINDOWS):
        for b in range(ns):
            ssum[b, n_state - (w - 1):, gi, b] = one
    return {"c_ident": np.eye(P, dtype=np.float32), "c_bucket_prompt": bp, "c_bucket_sample": bs, "c_same_batch": same,
            "c_rank": rank, "c_inv_count": inv, "c_state_sum": ssum.reshape(ns * n_state, 4, ns),
            "c_tri": np.triu(np.ones((P, P), np.float32))}


_INS = ['x_prompt', 'x_sample', 'cache_kv_w128', 'cache_kv_w512', 'cache_kv_w2048', 'state_pool', 'w_qkv', 'q_norm',
        'k_norm', 'w_o', 'rel_bias', 'attn_norm', 'pool_norm', 'pool_w', 'pool_b', 'pool_scale', 'ffn_norm',
        'router_group_w', 'router_group_b', 'router_expert_w', 'router_expert_b', 'w_gate', 'w_up', 'w_down']
_OUTS = [(1, 256, 1024), (8, 1, 1024), (1, 1, 128, 2, 16, 64), (1, 1, 256, 2, 16, 64), (1, 1, 256, 2, 16, 64),
         (1, 1, 15, 1024), (1, 8, 128, 2, 16, 64), (1, 8, 512, 2, 16, 64), (1, 8, 2048, 2, 16, 64), (1, 8, 15, 1024)]


def kernel(**inputs):
    import numpy as _np
    import concourse.bacc as _bacc
    from concourse import mybir as _mybir
    from concourse.bass_utils import run_bass_kernel_spmd as _run

    nc = _bacc.Bacc("TRN2", target_bir_lowering=False, num_devices=1)
    arrays, args = {}, []
    given = [(n, _np.ascontiguousarray(inputs[n])) for n in _INS] + list(constants().items())
    for name, a in given:
        arrays[f"in_{name}_dram"] = a
        args.append(nc.dram_tensor(f"in_{name}_dram", a.shape, _mybir.dt.from_np(a.dtype), kind="ExternalInput").ap())
    for i, shape in enumerate(_OUTS):
        args.append(nc.dram_tensor(f"out_{i}_dram", shape, _mybir.dt.float32, kind="ExternalOutput").ap())
    build(nc, *args)
    r = _run(nc, [arrays], core_ids=[0])
    return tuple(r.results[0][f"out_{i}_dram"] for i in range(len(_OUTS)))
```

```python
from contextlib import ExitStack

import concourse.bass as bass
from concourse import mybir

ALU = mybir.AluOpType
ACT = mybir.ActivationFunctionType
F32 = mybir.dt.float32
I32 = mybir.dt.int32
AX_X = mybir.AxisListType.X
ds = bass.ds

P = 128
DILATIONS = (1, 4, 16)
WINDOWS = (128, 512, 2048)
POOL_WINDOWS = (2, 4, 8, 16)
NEG = -1e30
RMS_EPS = 1e-6


class Chain:

    def __init__(self, eng, sem):
        self.eng, self.sem, self.base, self.k, self.i, self.per = eng, sem, 0, 0, 0, 0

    def __call__(self, instruction):
        instruction.then_inc(self.sem, 1)
        self.k += 1
        self.eng.wait_ge(self.sem, self.i * self.per + (self.base + self.k))

    def enter(self, i, per, first=0):
        self.base += self.k - first * per
        self.k, self.i, self.per = 0, i, per

    def leave(self, end):
        assert self.k == self.per, (self.k, self.per)
        self.base += end * self.per
        self.k, self.i, self.per = 0, 0, 0


def build(nc, x_prompt, x_sample, cache_w128, cache_w512, cache_w2048, state_pool, w_qkv, q_norm,
          k_norm, w_o, rel_bias, attn_norm, pool_norm, pool_w, pool_b, pool_scale, ffn_norm,
          router_group_w, router_group_b, router_expert_w, router_expert_b, w_gate, w_up, w_down,
          c_ident, c_bucket_prompt, c_bucket_sample, c_same_batch, c_rank, c_inv_count, c_state_sum, c_tri,
          y_prompt, y_sample, kv128_p, kv512_p, kv2048_p, pool_p, kv128_s, kv512_s, kv2048_s, pool_s):
    _, SEQ, D = x_prompt.shape
    NS = x_sample.shape[0]
    T = SEQ + NS
    KT = D // P
    G = len(WINDOWS)
    NB, GH = rel_bias.shape
    H = GH // G
    HD = D // H
    PAIRS = H // 2
    BH = NS * H
    NE = w_gate.shape[1]
    FT = w_gate.shape[3] // P
    NG = router_group_w.shape[2]
    EPG = NE // NG
    NR = NG + NE
    LAYERS = w_gate.shape[0]
    STATE = state_pool.shape[2]
    BV = 3 * P
    CW = 512
    SLOT = KT * CW
    TPC = CW // P
    NZ = 3 * KT
    NQK = 2 * KT
    CHUNKS = G * NZ // TPC
    caches = (cache_w128, cache_w512, cache_w2048)
    kv_p, kv_s = (kv128_p, kv512_p, kv2048_p), (kv128_s, kv512_s, kv2048_s)
    HALF = NS // 2
    CAP = 64
    NP = NE // 2
    MAX_ROUNDS = LAYERS * NP * -(-T // CAP)
    assert SEQ == 2 * P and BH == P and KT * P == D and LAYERS == 2 and NZ // TPC == 6

    qkvs_dram = nc.dram_tensor("qkv_of_samples", [NS, 3, G, D], F32, kind="Internal").ap()
    bias_dram = nc.dram_tensor("bias_by_distance", [H, G, BV], F32, kind="Internal").ap()

    with ExitStack() as ctx:
        def sb(name, shape):
            return ctx.enter_context(nc.sbuf_tensor(name, shape, F32))

        def sem(name):
            return ctx.enter_context(nc.semaphore(name))

        ring_lo = sb("ring_lo", [P, 4 * SLOT])
        hT = sb("hT", [P, KT, T])
        uT = sb("uT", [P, KT, T])
        oT = uT
        region_a = sb("region_a", [P, G * 2 * KT * T + 2 * G * D])
        scratch = sb("scratch", [P, 10752])
        ident = sb("ident", [P, P])
        ones = sb("ones", [P, P])
        blockones = sb("blockones", [P, P])
        epsc = sb("epsc", [P, 1])
        NVEC = 6 * KT + 2 * G
        vec_rows = sb("vec_rows", [NVEC, P])
        vecs = sb("vecs", [P, NVEC])
        gains = sb("gains", [P, 2])
        bucket_s = sb("bucket_s", [NB, G, P + 1])
        tab = sb("tab", [NB + 1, GH])
        tabrep = sb("tabrep", [NB, G, NS, H])
        same_batch = sb("same_batch", [BH, NS])
        rank = sb("rank", [P, NE])
        wr = sb("wr", [P, LAYERS, KT, NR])
        brow = sb("brow", [1, LAYERS, NR])
        rstd = sb("rstd", [P, 2, T])
        small = sb("small", [P, 64])
        tri = sb("tri", [P, P])
        slot_no = sb("slot_no", [P, CAP])
        rounds_f = sb("rounds_f", [P, LAYERS, NP + 1])
        rounds_i = ctx.enter_context(nc.sbuf_tensor("rounds_i", [1, LAYERS * (NP + 1)], I32))

        same_head = sb("same_head", [BH, H])

        def slot(s):
            if s < 4:
                return ring_lo[:, s * SLOT:(s + 1) * SLOT]
            return region_a[:, (s - 4) * SLOT:(s - 3) * SLOT]

        qk = region_a[:, 0:G * 2 * KT * T].rearrange("p (g w k t) -> p g w k t", g=G, w=2, k=KT)
        v_tok = region_a[:, G * 2 * KT * T:].rearrange("p (b g c) -> p b g c", b=2, g=G)

        def cut(start, shape, region=scratch):
            n = 1
            for s in shape:
                n *= s
            assert start + n <= region.shape[1], (start, n)
            names = "abcd"[:len(shape)]
            v = region[:, start:start + n]
            if len(shape) > 1:
                v = v.rearrange(f"p ({' '.join(names)}) -> p {' '.join(names)}",
                                **{c: s for c, s in zip(names, shape)})
            return v

        x_tok = cut(0, (3, D))
        sq = cut(4352, (KT, T))
        bucket_p = cut(6528, (G, BV))
        bias_rows = cut(7680, (G, BV))
        zn = cut(0, (4, T))
        zsq = cut(4 * T, (2, T))
        zr = cut(6 * T, (2, T))
        zri = cut(8 * T, (2, T))
        k_tok = cut(8192, (D,)), cut(3072, (D,))
        s_keys = cut(10240, (G, BH))
        q_rep = cut(7168, (D,)), cut(9216, (D,))
        qkv_s = cut(4096, (3, D))
        q_row = cut(4096, (3, D))
        v_new = cut(0, (G, D))
        o_own = cut(3072, (D,))
        s_rows = cut(4096, (G, P + 1))
        p_masked = cut(4608, (2, G, BH))
        qk_new = cut(9472, (2, G, HD))
        qk_prod = cut(5760, (G, HD))
        p_newm = cut(5952, (G, NS))
        p_newT = cut(5984, (G, BH))
        q_st = cut(6400, (2, G, SEQ))
        k_st = cut(7936, (2, G, SEQ))
        v_st = cut(0, (2, 2, G * P))
        probs = cut(1536, (2, 9 * P))
        probsT = cut(3840, (2, 9 * P))
        bias_t = ring_lo[:, 3 * SLOT:3 * SLOT + 4 * G * SEQ].rearrange("p (n g k) -> p n g k", n=4, g=G)
        u_tok = cut(0, (3, D))
        u_slots = cut(3072, (KT, P))
        silu = cut(4096, (FT * P,))
        hid = cut(4608, (FT, 2, CAP))
        y_pair = cut(5120, (D,))
        pick = cut(6144, (3, P))
        pick_gate = cut(6528, (3, P))
        place = cut(6912, (T,))
        logits = cut(7200, (3, NR))
        rt = cut(7264, (16, 3, NE))
        chosen = cut(8032, (3, NE))
        gates = cut(8080, (3, NE))
        position = cut(8128, (3, NE))
        pair_at = cut(8176, (2, 3, 2))
        hid_rows = cut(8208, (FT * P,))
        pair_max = cut(8192, (NP,))
        pair_rounds = cut(8200, (NP,))
        y_tok = cut(0, (3, D))
        PAD = POOL_WINDOWS[-1]
        A0 = 2 * SLOT
        pw = cut(A0, (KT, D // 4), region_a)
        inv_count = cut(A0 + 2048, (4, SEQ), region_a)
        state = cut(A0 + 3072, (D,), region_a)
        state_sum = cut(A0 + 4096, (4, NS), region_a)
        ext = cut(A0 + 4128, (2, 2, PAD + SEQ), region_a)
        pool_z = cut(A0 + 5216, (KT, T), region_a)
        pool_tok = cut(A0 + 7328, (D,), region_a)
        ybuf = cut(A0 + 8352, (2, T), region_a)
        zs_tmp = cut(A0 + 8880, (2, NS), region_a)

        bank = [ctx.enter_context(nc.psum_tensor(f"bank{n}", [P, 512], F32)) for n in range(8)]

        spread_bank = [bank[n] for n in (2, 3, 6, 7)]
        z_bank = [bank[n] for n in (0, 1, 6, 7)]

        x_landed, consts_landed, vecs_landed = sem("x_landed"), sem("consts_landed"), sem("vecs_landed")
        cache_copied = sem("cache_copied")
        ring_full = [sem(f"ring_full{n}") for n in range(6)]
        dve_own, pool_own = sem("dve_own"), sem("pool_own")
        setup_done, vecs_turned, bias_made = sem("setup_done"), sem("vecs_turned"), sem("bias_made")
        bias_copied, bias_stored = sem("bias_copied"), sem("bias_stored")
        x_turned, h_filled = sem("x_turned"), sem("h_filled")
        squares_ready, sums_ready = sem("squares_ready"), sem("sums_ready")
        root_ready, u_ready = sem("root_ready"), sem("u_ready")
        z_ready, zsq_ready, zsum_ready = sem("z_ready"), sem("zsq_ready"), sem("zsum_ready")
        zroot_ready, zn_ready, zn_kept = sem("zroot_ready"), sem("zn_ready"), sem("zn_kept")
        z_turned, z_stored, tokens_sent = sem("z_turned"), sem("z_stored"), sem("tokens_sent")
        q_rows_landed, q_spread = sem("q_rows_landed"), sem("q_spread")
        k_landed = [sem(f"k_landed{n}") for n in range(4)]
        q_sent, rows_sent, scored, o_own_ready, o_made = sem("q_sent"), sem("rows_sent"), sem("scored"), sem("o_own_ready"), sem("o_made")
        qk_new_landed, v_new_landed = sem("qk_new_landed"), sem("v_new_landed")
        s_turned = sem("s_turned")
        s_rows_ready, s_exp_ready, p_ready = sem("s_rows_ready"), sem("s_exp_ready"), sem("p_ready")
        p_turned, p_keys_ready = sem("p_turned"), sem("p_keys_ready")
        pv_s_ready, sample_done = sem("pv_s_ready"), sem("sample_done")
        qk_staged, v_staged = sem("qk_staged"), sem("v_staged")
        bias_landed = [sem(f"bias_landed{n}") for n in range(4)]
        scores_ready, biased, exps_ready = sem("scores_ready"), sem("biased"), sem("exps_ready")
        probs_ready, pt_ready = sem("probs_ready"), sem("pt_ready")
        pt_copied_dve, pt_copied_act = sem("pt_copied_dve"), sem("pt_copied_act")
        pv_ready, o_copied = sem("pv_ready"), sem("o_copied")
        wo_ready, wo_added = sem("wo_ready"), sem("wo_added")
        u_turned, u_tok_dve, u_tok_act = sem("u_turned"), sem("u_tok_dve"), sem("u_tok_act")
        rounds_ready, pick_ready, shifted = sem("rounds_ready"), sem("pick_ready"), sem("shifted")
        gathered, slots_dve, slots_act = sem("gathered"), sem("slots_dve"), sem("slots_act")
        place_made, place_ready, y_half, y_copied = sem("place_made"), sem("place_ready"), sem("y_half"), sem("y_copied")
        spread, spread_added, layer_added = sem("spread"), sem("spread_added"), sem("layer_added")
        logits_made, router_arg, router_exp = sem("logits_made"), sem("router_arg"), sem("router_exp")
        chosen_ready, positions_made = sem("chosen_ready"), sem("positions_made")
        up_ready = [sem("up_ready_even"), sem("up_ready_odd")]
        silu_ready, hid_rows_ready = sem("silu_ready"), sem("hid_rows_ready")
        hid_turned, hid_ready = sem("hid_turned"), sem("hid_ready")
        down_even_done = sem("down_even_done")
        pool_landed, state_summed, pooled = sem("pool_landed"), sem("state_summed"), sem("pooled")
        pool_y_ready, pool_y_added = sem("pool_y_ready"), sem("pool_y_added")
        pool_turned, pool_tok_ready, pool_sent = sem("pool_turned"), sem("pool_tok_ready"), sem("pool_sent")
        y_turned, y_ready, y_sent = sem("y_turned"), sem("y_ready"), sem("y_sent")
        block = ctx.enter_context(nc.Block())

        ATTN_G, POOL_G, FFN_G, POOL_B, POOL_S = 0, KT, (2 * KT, 3 * KT), 4 * KT, 5 * KT
        QK_G = 6 * KT
        N_CONSTS = 11 + 2 * LAYERS
        SENT_PER_G = 4
        RING_KV = CHUNKS // 3
        RING_WO = RING_KV + 2

        qkv_chunks = w_qkv[0].rearrange("(k p) (c n) -> c p k n", p=P, n=CW)
        k_strided = [c[0].rearrange("b (s d) w h e -> b w s d (h e)", d=d)[:, 0, :, 0, :] for c, d in zip(caches, DILATIONS)]
        v_strided = [c[0].rearrange("(x b) (s d) w h e -> x w s b d (h e)", b=HALF, d=d)[:, 1, :, :, 0, :]
                     for c, d in zip(caches, DILATIONS)]
        expert_w = (w_gate.rearrange("l e (k p) f -> (l e) p k f", p=P),
                    w_up.rearrange("l e (k p) f -> (l e) p k f", p=P),
                    w_down.rearrange("l e (k p) f -> (l e) p k f", p=P))
        SLOTS = ((2, 3, 4), (5, 0, 1))
        FIRST_USES = (RING_WO + 1, RING_WO + 1, RING_WO, 0, 0, 0)

        def norm_sums(pe, n):
            pe.wait_ge(squares_ready, n + 1)
            for k in range(KT):
                last = nc.tensor.matmul(bank[7][:, 0:T], ones[:], sq[:, k, :], start=(k == 0), stop=(k == KT - 1))
            last.then_inc(sums_ready, 1)

        def norm_root(act_e, n, h_done, count):
            act_e.wait_ge(h_done, count)
            nc.scalar.activation(sq[:, :, :], hT[:], ACT.Square).then_inc(squares_ready, 1)
            act_e.wait_ge(sums_ready, n + 1)
            nc.scalar.activation(rstd[:, 0, :], bank[7][:, 0:T], ACT.Sqrt, bias=epsc[:, 0:1], scale=1.0 / D).then_inc(root_ready, 1)

        def norm_apply(dve, chain, n, gain):
            dve.wait_ge(root_ready, n + 1)
            chain(nc.vector.reciprocal(rstd[:, 1, :], rstd[:, 0, :]))
            for k in range(KT):
                last = nc.vector.scalar_tensor_tensor(out=uT[:, k, :], in0=hT[:, k, :], scalar=vecs[:, gain + k:gain + k + 1],
                                                      in1=rstd[:, 1, :], op0=ALU.mult, op1=ALU.mult)
            last.then_inc(u_ready, 1)

        def all_rounds(eng, layer, one_round, pair_start=None, chain=None):
            eng.wait_ge(rounds_ready, layer + 1)
            with eng.Fori(0, NP) as p:
                first, end = (eng.value_load(rounds_i[0:1, ds(p + (layer * (NP + 1) + n), 1)], min_val=n, max_val=MAX_ROUNDS)
                              for n in range(2))
                if pair_start is not None:
                    chain.enter(p, 2)
                    pair_start(layer, p)
                with eng.Fori(first, end) as q:
                    one_round(q, p)
            if chain is not None:
                chain.leave(NP)

        @block.sync
        def _(sp):
            sp.dma_start(x_tok[:, 0:2, :], x_prompt[0].rearrange("(b p) c -> p b c", p=P)).then_inc(x_landed, 16)
            sp.dma_start(x_tok[0:NS, 2, :], x_sample[:, 0, :]).then_inc(x_landed, 16)

            PIECES = (1, 4, 16)
            moved = []
            for src, out, n in zip(caches, kv_s, PIECES):
                m = (src.shape[2] - 1) * 2 * D
                moved.append([v[0].rearrange("b l w h e -> b (l w h e)")[:, at:at + m].rearrange("b (n x y) -> b n x y", n=n, x=16)
                              for v, at in ((out, 0), (src, 2 * D))])

            def move(g, b, n):
                views = []
                for v in moved[g]:
                    v = v[b] if isinstance(b, int) else v[ds(b, 1)].rearrange("a n x y -> (a n) x y")
                    views.append(v[n] if isinstance(n, int) else v[ds(n, 1)].rearrange("a x y -> (a x) y"))
                sp.dma_start(views[0], views[1]).then_inc(cache_copied, 16)

            N_PIECES = NS * sum(PIECES)
            IN_QKV = 10
            for c in range(3):
                sp.dma_start(slot(c).rearrange("p (k n) -> p k n", k=KT), qkv_chunks[c]).then_inc(ring_full[c], 16)
            sp.wait_ge(consts_landed, 16 * N_CONSTS)
            for b in range(5):
                move(0, b, 0)
            sp.wait_ge(bias_stored, 16)
            for b in range(5, NS):
                move(0, b, 0)
            for n in range(PIECES[1]):
                move(1, 0, n)
            with sp.Fori(1, CHUNKS // 3) as r:
                for c in range(3):
                    sp.wait_ge(z_ready, r * (3 * TPC) + (c - 2) * TPC)
                    sp.dma_start(slot(c).rearrange("p (k n) -> p k n", k=KT),
                                 qkv_chunks[ds(r * 3 + c, 1)].rearrange("a p k n -> p (a k) n")).then_inc(ring_full[c], 16)
                    for n in range(3 * c, 3 * c + 3 + c // 2):
                        move(2, r, n)
            def bias_load(h, b):
                sp.dma_start(bias_t[:, b], bass.AP(tensor=bias_dram.tensor, offset=h * (G * BV),
                                                   ap=[[1, P], [BV, G], [1, SEQ]])).then_inc(bias_landed[b], 16)

            for half in range(2):
                for g in range(G):
                    if half:
                        sp.wait_ge(pv_s_ready, g + 1)
                    else:
                        sp.wait_ge(z_ready, G * NZ - (2 - g) * TPC)
                    sp.dma_start(slot(g).rearrange("p (b c) -> p b c", b=HALF), v_strided[g][half]).then_inc(ring_full[g], 16)
                    if half == 0 and g < 2:
                        move(2, 0, 13 + g)
                if not half:
                    sp.wait_ge(scored, G * NS)
                    sp.wait_ge(qk_new_landed, 16 * NS)
                    sp.wait_ge(v_new_landed, 16)
                    for b in range(4):
                        bias_load(b, b)
                for n in (range(0, 5) if half == 0 else range(5, 7)):
                    move(2, 0, n)
            for s in range(2):
                sp.wait_ge(pv_s_ready, G + s + 1)
                sp.dma_start(slot(s).rearrange("p (k n) -> p k n", k=KT // 2),
                             w_o[0].rearrange("(s k p) n -> s p k n", p=P, s=2)[s]).then_inc(ring_full[s], 16)
            sp.wait_ge(pv_s_ready, 2 * G)

            def expert(e, odd, what):
                s = SLOTS[odd][what]
                src = expert_w[what]
                src = src[e] if isinstance(e, int) else src[ds(e, 1)].rearrange("a p k f -> p (a k) f")
                sp.dma_start(slot(s).rearrange("p (k f) -> p k f", k=FT if what == 2 else KT), src).then_inc(ring_full[s], 16)

            expert(0, 0, 0)
            for n in range(7, 10):
                move(2, 0, n)
            with sp.Fori(1, H // 4) as r:
                for b in range(4):
                    sp.wait_ge(biased, r * 4 + b - 3)
                    bias_load(r * 4 + b, b)
                    move(2, 6, r * 4 + b - 4)
            for n in range(12, 16):
                move(2, 6, n)
            sp.wait_ge(biased, H)
            expert(0, 0, 1)
            sp.wait_ge(qk_staged, PAIRS)
            sp.wait_ge(v_staged, PAIRS)
            expert(0, 0, 2)
            expert(1, 1, 0)
            for n in range(PIECES[1]):
                move(1, 1, n)
            sp.wait_ge(wo_ready, KT)
            expert(1, 1, 1)
            expert(1, 1, 2)
            for n in range(10, 13):
                move(2, 0, n)
            for b in range(2, 7):
                for n in range(PIECES[1]):
                    move(1, b, n)

            def next_pair(r, rounds, moves):
                for odd in range(2):
                    for what in range(2):
                        sp.wait_ge(up_ready[odd], rounds)
                        expert(r * 2 + odd, odd, what)
                    for move_args in moves[odd::3]:
                        move(*move_args)
                for odd in range(2):
                    if odd:
                        sp.wait_ge(y_half, rounds * 2)
                        for move_args in moves[2::3]:
                            move(*move_args)
                    else:
                        sp.wait_ge(down_even_done, rounds)
                    expert(r * 2 + odd, odd, 2)

            def rounds_at(layer, p):
                return sp.value_load(rounds_i[0:1, ds(p + layer * (NP + 1), 1)], min_val=1, max_val=MAX_ROUNDS)

            sp.wait_ge(rounds_ready, 1)
            with sp.Fori(1, NP + 1) as p:
                next_pair(p, rounds_at(0, p), [(2, 7, p - 1)])
            for b in range(1, 6):
                for n in range(IN_QKV, 16):
                    move(2, b, n)
            sp.wait_ge(rounds_ready, 2)
            with sp.Fori(1, NP) as p:
                next_pair(p + NP, rounds_at(1, p), [(2, 7, p + 7)])
            for n in range(PIECES[1]):
                move(1, 7, n)
            move(2, 0, 15)
            move(2, 7, 15)
            for b in range(3):
                sp.wait_ge(y_ready, 2 * (b + 1))
                if b < 2:
                    sp.dma_start(y_prompt[0, b * P:(b + 1) * P, :], y_tok[:, b, :]).then_inc(y_sent, 16)
                else:
                    sp.dma_start(y_sample[:, 0, :], y_tok[0:NS, b, :]).then_inc(y_sent, 16)
            sp.wait_ge(y_sent, 48)
            sp.wait_ge(cache_copied, 16 * N_PIECES)

        @block.gpsimd
        def _(pool):
            pool.dma_start(pool_s[0, :, 0:STATE - 1, :].rearrange("b s c -> b (s c)"),
                           state_pool[0, :, 1:STATE, :].rearrange("b s c -> b (s c)")).then_inc(tokens_sent, 16)
            for g in range(G):
                def load_k(b):
                    pool.dma_start(slot(3)[:, b % 4 * D:(b % 4 + 1) * D], k_strided[g][b]).then_inc(k_landed[b % 4], 16)

                def spread_q(b):
                    at = 32 * (b // 3 + 1)
                    if b % 2 == 0 and b <= 2:
                        pool.wait_ge(zn_kept, g * NQK + (NQK - 2 + b))
                    if b >= 1:
                        pool.wait_ge(q_spread, g * NS + b)
                    pool.wait_ge(bias_stored, 16)
                    nc.gpsimd.partition_broadcast(q_rep[b % 2][:, :], q_row[at:at + 1, b % 3, :], channels=P).then_inc(q_spread, 1)

                for b in range(4):
                    load_k(b)
                for n in range(NQK):
                    pool.wait_ge(zn_ready, g * NZ + n + 1)
                    if n == KT + 6:
                        pool.wait_ge(q_spread, g * NS + 2)
                    nc.gpsimd.tensor_copy(qk[:, g, n // KT, n % KT, :], zn[:, n % 4, :]).then_inc(zn_kept, 1)
                    if n == KT + 3:
                        pool.wait_ge(z_stored, g * NZ + KT)
                        for at in range(0, NS, 3):
                            n_rows = min(3, NS - at)
                            pool.dma_start(q_row[32 * (at // 3 + 1):32 * (at // 3 + 1) + 1, 0:n_rows, :],
                                           qkv_s[at:at + n_rows, 0, :]).then_inc(q_rows_landed, 16)
                        pool.dma_start(qkvs_dram[:, 0, g], qkv_s[0:NS, 0, :]).then_inc(q_sent, 16)
                    if n == KT + 5:
                        pool.wait_ge(q_rows_landed, g * 48 + 48)
                        for b in range(2):
                            spread_q(b)
                for b in range(NS):
                    pool.wait_ge(scored, g * NS + b + 1)
                    if b + 2 < NS:
                        spread_q(b + 2)
                    if b + 4 < NS:
                        load_k(b + 4)
                pool.wait_ge(z_stored, (g + 1) * NZ)
                pool.dma_start(qkvs_dram[:, 1:3, g], qkv_s[0:NS, 1:3, :]).then_inc(rows_sent, 16)
                dst = kv_p[g][0, 0].rearrange("t w h e -> t w (h e)")
                if g == 0:
                    pool.dma_start(dst[:, 0, :], k_tok[1]).then_inc(tokens_sent, 16)
                    for a in range(2):
                        pool.dma_start(dst[a * HD:(a + 1) * HD, 1, :], v_tok[a * HD:(a + 1) * HD, 1, g, :]).then_inc(tokens_sent, 16)
                else:
                    for b in range(2):
                        pool.dma_start(dst[b * P:(b + 1) * P, 0, :], k_tok[b]).then_inc(tokens_sent, 16)
                    pool.dma_start(dst[:, 1, :].rearrange("(b p) c -> p b c", p=P), v_tok[:, :, g, :]).then_inc(tokens_sent, 16)
                pool.wait_ge(rows_sent, g * 16 + 16)
                pool.dma_start(kv_s[g][0, :, kv_s[g].shape[2] - 1].rearrange("b w h e -> b w (h e)"),
                               qkv_s[0:NS, 1:3, :]).then_inc(tokens_sent, 16)

            def stage_qk(pair, u):
                one = ds(pair, 1)
                for blk in range(2):
                    nc.gpsimd.tensor_copy(q_st[:, u, :, blk * P:(blk + 1) * P][:, :, ::-1],
                                          qk[:, :, 0, one, blk * P:(blk + 1) * P].rearrange("p g a t -> p (g a) t"))
                nc.gpsimd.tensor_copy(k_st[:, u], qk[:, :, 1, one, 0:SEQ].rearrange("p g a t -> p (g a) t")).then_inc(qk_staged, 1)

            def stage_v(pair, u):
                nc.gpsimd.tensor_copy(v_st[:, u].rearrange("p b (g c) -> p b g c", g=G),
                                      v_tok[:, :, :, ds(pair * P, P)]).then_inc(v_staged, 1)

            pool.wait_ge(tokens_sent, 16 * SENT_PER_G * G + 16)
            for pair in range(2):
                stage_qk(pair, pair)
            pool.wait_ge(sample_done, 1)
            for pair in range(2):
                stage_v(pair, pair)
            with pool.Fori(1, PAIRS // 2) as i:
                for u in range(2):
                    pool.wait_ge(scores_ready, i * 4 + (2 * u - 2))
                    stage_qk(i * 2 + u, u)
                    pool.wait_ge(pv_ready, i * 4 + (2 * u - 2))
                    stage_v(i * 2 + u, u)

            chain = Chain(pool, pool_own)

            def carry(place):
                return nc.gpsimd.tensor_tensor(small[:, place:place + 1], epsc[:, 0:1], epsc[:, 0:1], ALU.add)

            def pair_start(layer, p):
                e = p * 2
                chain(nc.gpsimd.tensor_copy(pair_at[:, 0], position[:, :, ds(e, 2)]))
                chain(nc.gpsimd.tensor_copy(pair_at[:, 1], gates[:, :, ds(e, 2)]))
                carry(56)

            def one_round(q, p):
                pool.wait_ge(place_made, q + 1)
                carry(57)
                for b in range(3):
                    n = P if b < 2 else NS
                    for e in range(2):
                        at = slice(e * CAP, (e + 1) * CAP)
                        nc.gpsimd.tensor_scalar(pick_gate[0:n, b, at], slot_no[0:n, :], pair_at[0:n, 0, b, e:e + 1],
                                                pair_at[0:n, 1, b, e:e + 1], ALU.is_equal, ALU.mult)
                        last = nc.gpsimd.tensor_scalar(pick[0:n, b, at], slot_no[0:n, :], pair_at[0:n, 0, b, e:e + 1], None, ALU.is_equal)
                last.then_inc(pick_ready, 1)
                pool.wait_ge(pick_ready, q + 1)
                carry(58)
                nc.gpsimd.tensor_scalar(pair_at[:, 0], pair_at[:, 0], -float(CAP), None, ALU.add).then_inc(shifted, 1)
                pool.wait_ge(shifted, q + 1)
                carry(59)

            carry(55).then_inc(place_made, 1)
            for layer in range(LAYERS):
                all_rounds(pool, layer, one_round, pair_start, chain)

        @block.scalar
        def _(ac):
            dma = ac.dma_start
            dma(ident[:], c_ident).then_inc(consts_landed, 16)
            dma(bucket_p[0:NB + 1, :, :], c_bucket_prompt).then_inc(consts_landed, 16)
            dma(bucket_s[:], c_bucket_sample.rearrange("g n k -> n g k")).then_inc(consts_landed, 16)
            dma(tab[0:NB, :], rel_bias).then_inc(consts_landed, 16)
            dma(same_batch[:], c_same_batch).then_inc(consts_landed, 16)
            dma(rank[:], c_rank[:, 0:NE]).then_inc(consts_landed, 16)
            dma(slot_no[:], c_rank[:, NE:NE + CAP]).then_inc(consts_landed, 16)
            dma(same_head[:], c_rank[:, NE + CAP:]).then_inc(consts_landed, 16)
            dma(tri[:], c_tri).then_inc(consts_landed, 16)
            for at, v in ((ATTN_G, attn_norm[0]), (POOL_G, pool_norm[0]), (POOL_B, pool_b[0]), (POOL_S, pool_scale[0])):
                dma(vec_rows[at:at + KT, :], v.rearrange("(k p) -> k p", p=P)).then_inc(vecs_landed, 16)
            dma(vec_rows[FFN_G[0]:FFN_G[0] + 2 * KT, :], ffn_norm.rearrange("l (k p) -> (l k) p", p=P)).then_inc(vecs_landed, 16)
            for w, v in enumerate((q_norm, k_norm)):
                for g in range(G):
                    for t in range(2):
                        dma(vec_rows[QK_G + 2 * g + w:QK_G + 2 * g + w + 1, t * HD:(t + 1) * HD], v[0, g:g + 1, :]).then_inc(vecs_landed, 16)
            for layer in range(LAYERS):
                dma(wr[:, layer, :, 0:NG], router_group_w[layer].rearrange("(k p) g -> p k g", p=P)).then_inc(consts_landed, 16)
                dma(wr[:, layer, :, NG:], router_expert_w[layer].rearrange("(k p) g -> p k g", p=P)).then_inc(consts_landed, 16)
            dma(brow[:, :, 0:NG], router_group_b.rearrange("(a l) g -> a l g", a=1)).then_inc(consts_landed, 16)
            dma(brow[:, :, NG:], router_expert_b.rearrange("(a l) g -> a l g", a=1)).then_inc(consts_landed, 16)

            ac.wait_ge(setup_done, 1)
            norm_root(ac, 0, h_filled, KT)
            ac.wait_ge(bias_copied, 1)
            dma(bias_dram.rearrange("h g d -> h g d"), bias_rows[0:H, :, :]).then_inc(bias_stored, 16)
            ac.wait_ge(bias_stored, 16)

            with ac.Fori(0, G) as g:
                for s in range(NZ + 4):
                    if s < NQK:
                        ac.wait_ge(z_ready, g * NZ + (s + 1))
                        nc.scalar.activation(zsq[:, s % 2, :], z_bank[s % 4][:, 0:T], ACT.Square).then_inc(zsq_ready, 1)
                    if 1 <= s <= NQK:
                        n = s - 1
                        ac.wait_ge(zsum_ready, g * NQK + (n + 1))
                        if n >= 2:
                            ac.wait_ge(zn_ready, g * NZ + (n - 1))
                        nc.scalar.activation(zr[:, n % 2, :], bank[2 + n % 2][:, 0:T], ACT.Sqrt, bias=epsc[:, 0:1],
                                             scale=1.0 / HD).then_inc(zroot_ready, 1)
                    if s >= 4:
                        n = s - 4
                        what, k = n // KT, n % KT
                        at = slice(k * P, (k + 1) * P)
                        src = bank[4 + n % 2]
                        if n == 0:
                            ac.wait_ge(tokens_sent, g * (16 * SENT_PER_G) + 16)
                        ac.wait_ge(z_turned, g * NZ + (n + 1))
                        if what == 1:
                            for b in range(2):
                                nc.scalar.activation(k_tok[b][:, at], src[:, b * P:(b + 1) * P], ACT.Copy)
                        if what == 2:
                            nc.scalar.activation(v_tok[:, :, ds(g, 1), at].rearrange("p b a c -> p (b a) c"),
                                                 src[:, 0:2 * P].rearrange("p (b c) -> p b c", b=2), ACT.Copy)
                        nc.scalar.activation(qkv_s[0:NS, what, at], src[0:NS, 2 * P:3 * P], ACT.Copy).then_inc(z_stored, 1)

            ac.wait_ge(rows_sent, 16 * G)
            ac.wait_ge(q_sent, 16 * G)
            ac.wait_ge(scored, G * NS)
            ac.wait_ge(zn_kept, G * NQK)
            ac.wait_ge(z_turned, G * NZ)
            for b in range(NS):
                dma(qk_new[b * H:(b + 1) * H].rearrange("p w g e -> p (w g) e"),
                    qkvs_dram[b, 0:2].rearrange("w g (h e) -> h (w g) e", e=HD)).then_inc(qk_new_landed, 16)
            dma(v_new[0:NS, :, :], qkvs_dram[:, 2, :, :]).then_inc(v_new_landed, 16)
            ac.wait_ge(s_rows_ready, 1)
            nc.scalar.activation(s_rows[:, :, :], s_rows[:, :, :], ACT.Exp, bias=small[:, 36:37],
                                 accum_out=small[:, 37:38]).then_inc(s_exp_ready, 1)

            def step(i, s, live, behind):
                h = i * 4 + s
                if live:
                    b = s % 2
                    ac.wait_ge(biased, h + 1)
                    nc.scalar.activation(probs[:, b, 0:G * P], probs[:, b, 0:G * P], ACT.Exp,
                                         bias=small[:, 8 * b + 3:8 * b + 4], accum_out=small[:, 8 * b + 5:8 * b + 6])
                    nc.scalar.activation(probs[:, b, G * P:], probs[:, b, G * P:], ACT.Exp,
                                         bias=small[:, 8 * b + 2:8 * b + 3], accum_out=small[:, 8 * b + 4:8 * b + 5]).then_inc(exps_ready, 1)
                if s % 2 == 0 and behind >= 4:
                    pair, u = i * 2 + (s // 2 - 2), s // 2 % 2
                    ac.wait_ge(pv_ready, h - 2)
                    for blk in range(2):
                        last = nc.scalar.activation(oT[:, ds(pair, 1), blk * P:(blk + 1) * P],
                                                    bank[6 + u][:, blk * P:(blk + 1) * P][:, ::-1].rearrange("p (a t) -> p a t", a=1), ACT.Copy)
                    last.then_inc(o_copied, 1)
                if 1 <= behind <= H:
                    b = (s - 1) % 2
                    ac.wait_ge(pt_ready, h)
                    nc.scalar.activation(probsT[:, b, 4 * P:8 * P], bank[4][:, :], ACT.Copy)
                    nc.scalar.activation(probsT[:, b, 8 * P:], bank[5][:, 0:P], ACT.Copy).then_inc(pt_copied_act, 1)

            for s in range(4):
                step(0, s, True, s)
            with ac.Fori(1, H // 4) as i:
                for s in range(4):
                    step(i, s, True, 4)
            step(H // 4, 0, False, H)
            step(H // 4, 2, False, H + 2)

            ac.wait_ge(qk_staged, PAIRS)
            ac.wait_ge(v_staged, PAIRS)
            dma(pw, pool_w[0].rearrange("g (k p) f -> p (g k) f", p=P)).then_inc(pool_landed, 16)
            for gi in range(4):
                dma(inv_count[:, gi, :], c_inv_count[gi:gi + 1, :].to_broadcast([P, SEQ])).then_inc(pool_landed, 16)
            dma(state[0:NS * STATE], state_pool[0].rearrange("b s c -> (b s) c")).then_inc(pool_landed, 16)
            dma(state_sum[0:NS * STATE], c_state_sum).then_inc(pool_landed, 16)

            for layer in range(LAYERS):
                if layer:
                    norm_root(ac, 2, layer_added, 1)
                    ac.wait_ge(pool_tok_ready, 1)
                    dma(pool_p[0, 0], pool_tok[0:STATE]).then_inc(pool_sent, 16)
                    dma(pool_s[0, :, STATE - 1, :], pool_tok[STATE:STATE + NS]).then_inc(pool_sent, 16)
                    norm_root(ac, 3, pool_y_added, KT)
                else:
                    norm_root(ac, 1, wo_added, KT)
                for b in range(3):
                    n = P if b < 2 else NS
                    ac.wait_ge(u_turned, 6 * layer + 2 * b + 2)
                    nc.scalar.activation(u_tok[0:n, b, D // 2:], bank[2 * b + 1][0:n, :], ACT.Copy).then_inc(u_tok_act, 1)
                for which in range(2):
                    ac.wait_ge(router_arg, 2 * layer + which + 1)
                    v = rt[:, 1, :, 0:NG] if which == 0 else rt[:, 12, :, 0:1]
                    nc.scalar.activation(v, v, ACT.Exp).then_inc(router_exp, 1)

                def one_round(q, p):
                    ac.wait_ge(gathered, q * 2 + 2)
                    nc.scalar.activation(u_slots[:, KT // 2:, :], bank[1].rearrange("p (k n) -> p k n", n=P), ACT.Copy).then_inc(slots_act, 1)
                    ac.wait_ge(place_made, q + 2)
                    nc.scalar.activation(place, bank[6][:, 0:T], ACT.Copy).then_inc(place_ready, 1)
                    for e in range(2):
                        rows = slice(e * CAP, (e + 1) * CAP)
                        ac.wait_ge(up_ready[e], q + 1)
                        nc.scalar.activation(silu[rows], bank[2][rows, :], ACT.Silu).then_inc(silu_ready, 1)
                    for a in range(2):
                        ac.wait_ge(y_half, q * 2 + (a + 1))
                        nc.scalar.activation(y_pair[:, a * 512:(a + 1) * 512], bank[4 + a][:, :], ACT.Copy).then_inc(y_copied, 1)

                all_rounds(ac, layer, one_round)
            ac.wait_ge(pool_sent, 32)

        @block.vector
        def _(dve):
            chain = Chain(dve, dve_own)
            vec = nc.vector
            vec.memset(ones[:], 1.0)
            vec.memset(epsc[:], RMS_EPS)
            vec.memset(small[:], 0.0)
            vec.memset(tab[NB:NB + 1, :], NEG)
            for a in range(2):
                for b in range(2):
                    last = vec.memset(blockones[a * HD:(a + 1) * HD, b * HD:(b + 1) * HD], float(a == b))
            last.then_inc(setup_done, 1)

            dve.wait_ge(vecs_turned, 1)
            chain(vec.tensor_copy(vecs[:], bank[7][:, 0:NVEC]))
            for g in range(G):
                c = QK_G + 2 * g
                last = vec.tensor_scalar(vecs[:, c:c + 1], vecs[:, c:c + 1], float(HD) ** -0.5, None, ALU.mult)
            chain(last)
            for k in range(KT):
                dve.wait_ge(x_turned, k + 1)
                vec.tensor_copy(hT[:, k, :], bank[k % 4][:, 0:T]).then_inc(h_filled, 1)
            dve.wait_ge(bias_made, 1)
            for g in range(G):
                last = vec.tensor_copy(bias_rows[0:H, g, :], bank[4 + g][0:H, 0:BV])
            last.then_inc(bias_copied, 1)
            dve.wait_ge(consts_landed, 16 * N_CONSTS)
            for g in range(G):
                chain(vec.tensor_copy(tabrep[:, g, :, :], tab[0:NB, g * H:(g + 1) * H].rearrange("p (a h) -> p a h", a=1).to_broadcast([NB, NS, H])))
            norm_apply(dve, chain, 0, ATTN_G)

            with dve.Fori(0, G) as g:
                chain.enter(g, NQK + 1 + NS)
                chain(vec.tensor_copy(gains[:], vecs[:, ds(g * 2 + QK_G, 2)]))
                for n in range(NZ):
                    if n >= 4:
                        dve.wait_ge(z_turned, g * NZ + (n - 3))
                        if n - 4 < NQK:
                            dve.wait_ge(zn_kept, g * NQK + (n - 3))
                    if n < NQK:
                        dve.wait_ge(zroot_ready, g * NQK + (n + 1))
                        chain(vec.reciprocal(zri[:, n % 2, :], zr[:, n % 2, :]))
                        vec.scalar_tensor_tensor(out=zn[:, n % 4, :], in0=z_bank[n % 4][:, 0:T], scalar=gains[:, n // KT:n // KT + 1],
                                                 in1=zri[:, n % 2, :], op0=ALU.mult, op1=ALU.mult).then_inc(zn_ready, 1)
                    else:
                        dve.wait_ge(z_ready, g * NZ + (n + 1))
                        vec.tensor_copy(zn[:, n % 4, :], z_bank[n % 4][:, 0:T]).then_inc(zn_ready, 1)
                    b = n - (NZ - 2 - NS)
                    if 0 <= b < NS:
                        dve.wait_ge(q_spread, g * NS + b + 1)
                        dve.wait_ge(k_landed[b % 4], g * 32 + 16 * (b // 4 + 1))
                        k_tile = slot(3)[:, b % 4 * D:(b % 4 + 1) * D]
                        chain(vec.tensor_tensor(k_tile, k_tile, q_rep[b % 2][:, :], ALU.mult))
                        vec.tensor_reduce(out=s_keys[:, ds(g, 1), b * H:(b + 1) * H].rearrange("p a h -> p (a h)"),
                                          in_=k_tile.rearrange("p (h e) -> p h e", e=HD), axis=AX_X, op=ALU.add).then_inc(scored, 1)
                dve.wait_ge(z_turned, g * NZ + NZ)
                dve.wait_ge(zn_kept, g * NQK + NQK)
            chain.leave(G)

            dve.wait_ge(tokens_sent, 16 * SENT_PER_G * G + 16)
            vec.memset(p_masked, 0.0)
            dve.wait_ge(qk_new_landed, 16 * NS)
            chain(vec.tensor_tensor(qk_prod, qk_new[:, 0], qk_new[:, 1], ALU.mult))
            chain(vec.tensor_reduce(out=small[:, 32:32 + G], in_=qk_prod, axis=AX_X, op=ALU.add))
            dve.wait_ge(s_turned, 1)
            chain(vec.tensor_copy(s_rows, bank[0][:, 0:G * (P + 1)].rearrange("p (g k) -> p g k", g=G)))
            chain(vec.tensor_tensor(s_rows[:, :, P], s_rows[:, :, P], small[:, 32:32 + G], ALU.add))
            chain(vec.tensor_reduce(out=small[:, 35:36], in_=s_rows.rearrange("p g k -> p (g k)"), axis=AX_X, op=ALU.max))
            vec.tensor_scalar(small[:, 36:37], small[:, 35:36], -1.0, None, ALU.mult).then_inc(s_rows_ready, 1)
            dve.wait_ge(s_exp_ready, 1)
            chain(vec.reciprocal(small[:, 38:39], small[:, 37:38]))
            chain(vec.tensor_scalar(s_rows, s_rows, small[:, 38:39], None, ALU.mult))
            for g in range(G):
                last = vec.tensor_scalar(p_newm[:, g, :], same_batch[:], s_rows[:, g, P:P + 1], None, ALU.mult)
            last.then_inc(p_ready, 1)
            dve.wait_ge(p_turned, 1)
            for t in range(2):
                src = bank[1][:, 0:G * BH].rearrange("p (x t h) -> p x t h", t=2, h=H)
                vec.tensor_copy(p_masked[:, t].rearrange("p g k -> p (g k)").rearrange("p (x t h) -> p x t h", t=2, h=H)[:, :, t, :], src[:, :, t, :])
            vec.tensor_copy(p_newT[0:NS], bank[2][0:NS, 0:G * BH].rearrange("p (g k) -> p g k", g=G)).then_inc(p_keys_ready, 1)
            dve.wait_ge(pv_s_ready, 2 * G)
            for a in range(2):
                last = vec.tensor_tensor(o_own[:, a * 512:(a + 1) * 512].rearrange("p (h e) -> p h e", e=HD),
                                         bank[3 + a].rearrange("p (h e) -> p h e", e=HD),
                                         same_head[:, a * 8:(a + 1) * 8].rearrange("p (h x) -> p h x", x=1).to_broadcast([P, 8, HD]), ALU.mult)
            last.then_inc(o_own_ready, 1)
            dve.wait_ge(o_made, 1)
            vec.tensor_copy(oT[:, :, SEQ:], bank[5][:, 0:KT * NS].rearrange("p (k b) -> p k b", k=KT)).then_inc(sample_done, 1)

            def step(i, s, live, behind):
                h = i * 4 + s
                b = s % 2
                if live:
                    dve.wait_ge(scores_ready, h + 1)
                    dve.wait_ge(bias_landed[s], i * 16 + 16)
                    c = 8 * b
                    vec.memset(small[:, 60:61], 0.0)
                    vec.tensor_tensor_reduce(out=probs[:, b, 0:G * P].rearrange("p (g k) -> p g k", g=G), in0=bank[0][:, 0:G * P].rearrange("p (g k) -> p g k", g=G),
                                             in1=bias_t[:, s, :, P:], scale=1.0, scalar=NEG, op0=ALU.add, op1=ALU.max,
                                             accum_out=small[:, 16 + c:17 + c])
                    vec.tensor_tensor_reduce(out=probs[:, b, 3 * P:7 * P], in0=bank[1][:, :], in1=bias_t[:, s, 0:2, :].rearrange("p g k -> p (g k)"),
                                             scale=1.0, scalar=NEG, op0=ALU.add, op1=ALU.max, accum_out=small[:, 17 + c:18 + c])
                    chain(vec.tensor_tensor_reduce(out=probs[:, b, 7 * P:], in0=bank[2][:, 0:SEQ], in1=bias_t[:, s, 2, :],
                                                   scale=1.0, scalar=NEG, op0=ALU.add, op1=ALU.max, accum_out=small[:, 18 + c:19 + c]))
                    vec.tensor_scalar(small[:, c + 3:c + 4], small[:, 16 + c:17 + c], -1.0, None, ALU.mult)
                    vec.tensor_scalar(small[:, c + 2:c + 3], small[:, 17 + c:18 + c], small[:, 18 + c:19 + c], -1.0,
                                      ALU.max, ALU.mult).then_inc(biased, 1)
                if 1 <= behind <= H:
                    dve.wait_ge(pt_ready, h)
                    vec.tensor_copy(probsT[:, 1 - b, 0:4 * P], bank[3][:, :]).then_inc(pt_copied_dve, 1)
                if live:
                    dve.wait_ge(exps_ready, h + 1)
                    chain(vec.reciprocal(small[:, 8 * b + 6:8 * b + 8], small[:, 8 * b + 4:8 * b + 6]))
                    vec.tensor_scalar(probs[:, b, 0:G * P], probs[:, b, 0:G * P], small[:, 8 * b + 7:8 * b + 8], None, ALU.mult)
                    vec.tensor_scalar(probs[:, b, G * P:], probs[:, b, G * P:], small[:, 8 * b + 6:8 * b + 7], None,
                                      ALU.mult).then_inc(probs_ready, 1)

            for s in range(4):
                step(0, s, True, s)
            with dve.Fori(1, H // 4) as i:
                chain.enter(i, 8, 1)
                for s in range(4):
                    step(i, s, True, 4)
            chain.leave(H // 4)
            step(H // 4, 0, False, H)

            for m in range(KT):
                dve.wait_ge(wo_ready, m + 1)
                vec.tensor_tensor(hT[:, m, :], bank[m % 2][:, 0:T], hT[:, m, :], ALU.add).then_inc(wo_added, 1)

            def wide(v, n):
                return v.to_broadcast([P, 3, n])

            def router(layer):
                lg, le = logits[:, :, 0:NG], logits[:, :, NG:]
                r = [rt[:, n] for n in range(16)]
                for b in range(3):
                    n = P if b < 2 else NS
                    dve.wait_ge(u_turned, 6 * layer + 2 * b + 1)
                    vec.tensor_copy(u_tok[0:n, b, 0:D // 2], bank[2 * b][0:n, :]).then_inc(u_tok_dve, 1)
                chain(vec.memset(logits[:, 2, :], 0.0))
                dve.wait_ge(logits_made, layer + 1)
                vec.tensor_copy(logits[:, 0:2, :], bank[6][:, 0:2 * NR].rearrange("p (t n) -> p t n", t=2))
                chain(vec.tensor_copy(logits[0:NS, 2, :], bank[6][0:NS, 2 * NR:3 * NR]))
                gmax = r[0][:, :, 0:1]
                chain(vec.tensor_reduce(out=gmax, in_=lg, axis=AX_X, op=ALU.max))
                vec.tensor_tensor(r[1][:, :, 0:NG], lg, wide(gmax, NG), ALU.subtract).then_inc(router_arg, 1)
                chain(vec.tensor_tensor(r[2][:, :, 0:NG], lg, wide(gmax, NG), ALU.is_equal))
                rk = rank[:, :].rearrange("p (a n) -> p a n", a=1)
                chain(vec.tensor_tensor(r[2][:, :, 0:NG], r[2][:, :, 0:NG], rk[:, :, 0:NG].to_broadcast([P, 3, NG]), ALU.mult))
                chain(vec.tensor_reduce(out=r[3][:, :, 0:1], in_=r[2][:, :, 0:NG], axis=AX_X, op=ALU.max))
                chain(vec.tensor_tensor(r[2][:, :, 0:NG], r[2][:, :, 0:NG], wide(r[3][:, :, 0:1], NG), ALU.is_equal))
                for g in range(NG):
                    last = vec.tensor_copy(r[4][:, :, g * EPG:(g + 1) * EPG], wide(r[2][:, :, g:g + 1], EPG))
                chain(last)
                chain(vec.tensor_tensor(r[5], le, r[4], ALU.mult))
                chain(vec.tensor_scalar(r[4], r[4], -1.0, -NEG, ALU.add, ALU.mult))
                chain(vec.tensor_tensor(r[5], r[5], r[4], ALU.add))

                def first_of_largest(src, top, out):
                    chain(vec.tensor_reduce(out=top, in_=src, axis=AX_X, op=ALU.max))
                    chain(vec.tensor_tensor(out, src, wide(top, NE), ALU.is_equal))
                    chain(vec.tensor_tensor(out, out, rk.to_broadcast([P, 3, NE]), ALU.mult))
                    chain(vec.tensor_reduce(out=r[3][:, :, 0:1], in_=out, axis=AX_X, op=ALU.max))
                    chain(vec.tensor_tensor(out, out, wide(r[3][:, :, 0:1], NE), ALU.is_equal))

                first_of_largest(r[5], r[6][:, :, 0:1], r[7])
                chain(vec.tensor_scalar(r[8], r[7], 2 * NEG, None, ALU.mult))
                chain(vec.tensor_tensor(r[8], r[8], r[5], ALU.add))
                first_of_largest(r[8], r[9][:, :, 0:1], r[10])
                vec.tensor_tensor(r[12][:, :, 0:1], r[9][:, :, 0:1], r[6][:, :, 0:1], ALU.subtract).then_inc(router_arg, 1)
                dve.wait_ge(router_exp, 2 * layer + 2)
                chain(vec.tensor_reduce(out=r[11][:, :, 0:1], in_=r[1][:, :, 0:NG], axis=AX_X, op=ALU.add))
                chain(vec.tensor_scalar(r[13][:, :, 0:1], r[12][:, :, 0:1], 1.0, None, ALU.add))
                chain(vec.tensor_tensor(r[13][:, :, 0:1], r[13][:, :, 0:1], r[11][:, :, 0:1], ALU.mult))
                chain(vec.reciprocal(r[14][:, :, 0:1], r[13][:, :, 0:1]))
                chain(vec.tensor_tensor(r[15][:, :, 0:1], r[14][:, :, 0:1], r[12][:, :, 0:1], ALU.mult))
                vec.tensor_tensor(chosen, r[7], r[10], ALU.add).then_inc(chosen_ready, 1)
                chain(vec.tensor_tensor(r[7], r[7], wide(r[14][:, :, 0:1], NE), ALU.mult))
                chain(vec.tensor_tensor(r[10], r[10], wide(r[15][:, :, 0:1], NE), ALU.mult))
                chain(vec.tensor_tensor(gates, r[7], r[10], ALU.add))
                dve.wait_ge(positions_made, layer + 1)
                chain(vec.memset(position[:, 2, :], 0.0))
                vec.tensor_tensor(position[:, 0:2, :], bank[6][:, 64:64 + 2 * NE].rearrange("p (b e) -> p b e", b=2), chosen[:, 0:2, :], ALU.mult)
                chain(vec.tensor_tensor(position[0:NS, 2, :], bank[6][0:NS, 64 + 2 * NE:64 + 3 * NE], chosen[0:NS, 2, :], ALU.mult))
                chain(vec.tensor_scalar(position, position, -1.0, None, ALU.add))
                chain(vec.tensor_reduce(out=pair_max, in_=bank[6][:, 128:128 + NE].rearrange("p (n a) -> p n a", a=2), axis=AX_X, op=ALU.max))
                chain(vec.tensor_scalar(pair_rounds, pair_max, float(CAP), 1.0, ALU.is_gt, ALU.add))
                for full in range(2 * CAP, T, CAP):
                    chain(vec.scalar_tensor_tensor(out=pair_rounds, in0=pair_max, scalar=float(full), in1=pair_rounds, op0=ALU.is_gt, op1=ALU.add))
                rf = rounds_f[:, layer, :]
                chain(vec.tensor_copy(rf[:, 0:1], rounds_f[:, 0, NP:]) if layer else vec.memset(rf[:, 0:1], 0.0))
                for p in range(NP):
                    chain(vec.tensor_tensor(rf[:, p + 1:p + 2], rf[:, p:p + 1], pair_rounds[:, p:p + 1], ALU.add))
                vec.tensor_copy(rounds_i[0:1, layer * (NP + 1):(layer + 1) * (NP + 1)], rounds_f[0:1, layer, :]).then_inc(rounds_ready, 1)

            def one_round(q, p):
                dve.wait_ge(gathered, q * 2 + 1)
                vec.tensor_copy(u_slots[:, 0:KT // 2, :], bank[0].rearrange("p (k n) -> p k n", n=P)).then_inc(slots_dve, 1)
                for e in range(2):
                    rows = slice(e * CAP, (e + 1) * CAP)
                    dve.wait_ge(silu_ready, q * 2 + (e + 1))
                    vec.tensor_tensor(hid_rows[rows], bank[3][rows, :], silu[rows], ALU.mult).then_inc(hid_rows_ready, 1)
                    dve.wait_ge(hid_turned, q * 2 + (e + 1))
                    vec.tensor_copy(hid[:, :, e, :], bank[0][:, e * FT * CAP:(e + 1) * FT * CAP].rearrange("p (f n) -> p f n", f=FT)).then_inc(hid_ready, 1)
                for m in range(KT):
                    dve.wait_ge(spread, q * KT + (m + 1))
                    vec.tensor_tensor(hT[:, m, :], spread_bank[m % 4][:, 0:T], hT[:, m, :], ALU.add).then_inc(spread_added, 1)

            def experts(layer):
                dve.wait_ge(rounds_ready, layer + 1)
                all_rounds(dve, layer, one_round)
                vec.memset(small[:, 62:63], 0.0).then_inc(layer_added, 1)

            norm_apply(dve, chain, 1, FFN_G[0])
            router(0)
            experts(0)

            norm_apply(dve, chain, 2, POOL_G)
            dve.wait_ge(u_ready, 3)
            dve.wait_ge(pool_landed, 16 * 7)
            chain(vec.memset(ext[:, :, :, 0:PAD], 0.0))
            for gi, win in enumerate(POOL_WINDOWS):
                u2 = uT[:, 2 * gi:2 * gi + 2, 0:SEQ]
                chain(vec.tensor_copy(ext[:, 0, :, PAD:], u2))
                at, sh = 0, 1
                while sh < win:
                    chain(vec.tensor_tensor(ext[:, 1 - at, :, PAD:], ext[:, at, :, PAD:], ext[:, at, :, PAD - sh:PAD + SEQ - sh], ALU.add))
                    at, sh = 1 - at, sh * 2
                chain(vec.tensor_tensor(ext[:, 1 - at, :, PAD:], ext[:, at, :, PAD:], inv_count[:, gi:gi + 1, :].to_broadcast([P, 2, SEQ]), ALU.mult))
                chain(vec.tensor_tensor(pool_z[:, 2 * gi:2 * gi + 2, 0:SEQ], ext[:, 1 - at, :, PAD:], u2, ALU.subtract))
                if gi == 0:
                    dve.wait_ge(state_summed, 1)
                us = uT[:, 2 * gi:2 * gi + 2, SEQ:]
                chain(vec.tensor_tensor(zs_tmp, bank[0][:, 2 * gi * NS:(2 * gi + 2) * NS].rearrange("p (k b) -> p k b", k=2), us, ALU.add))
                vec.scalar_tensor_tensor(out=pool_z[:, 2 * gi:2 * gi + 2, SEQ:], in0=zs_tmp, scalar=1.0 / win, in1=us,
                                         op0=ALU.mult, op1=ALU.subtract).then_inc(pooled, 1)
                dve.wait_ge(pooled, gi + 1)
            for a in range(2):
                dve.wait_ge(pool_turned, a + 1)
                last = vec.tensor_copy(pool_tok[0:STATE + NS, a * 512:(a + 1) * 512], bank[3 + a][0:STATE + NS, :])
            last.then_inc(pool_tok_ready, 1)
            for m in range(KT):
                dve.wait_ge(pool_y_ready, m + 1)
                chain(vec.tensor_scalar(ybuf[:, m % 2, :], bank[1 + m % 2][:, 0:T], vecs[:, POOL_B + m:POOL_B + m + 1],
                                        vecs[:, POOL_S + m:POOL_S + m + 1], ALU.add, ALU.mult))
                vec.tensor_tensor(hT[:, m, :], hT[:, m, :], ybuf[:, m % 2, :], ALU.add).then_inc(pool_y_added, 1)

            norm_apply(dve, chain, 3, FFN_G[1])
            router(1)
            experts(1)

            for b in range(3):
                n = P if b < 2 else NS
                for a in range(2):
                    dve.wait_ge(y_turned, 2 * b + a + 1)
                    vec.tensor_copy(y_tok[0:n, b, a * 512:(a + 1) * 512], bank[2 * b + a][0:n, :]).then_inc(y_ready, 1)

        @block.tensor
        def _(pe):
            mm = nc.tensor.matmul
            pe.wait_ge(consts_landed, 16 * N_CONSTS)
            pe.wait_ge(setup_done, 1)
            pe.wait_ge(vecs_landed, 16 * (5 + 4 * G))
            nc.tensor.transpose(bank[7][:, 0:NVEC], vec_rows[:], ident[0:NVEC, 0:NVEC]).then_inc(vecs_turned, 1)
            pe.wait_ge(x_landed, 32)
            for k in range(KT):
                if k >= 4:
                    pe.wait_ge(h_filled, k - 3)
                for b in range(2):
                    nc.tensor.transpose(bank[k % 4][:, b * P:(b + 1) * P], x_tok[:, b, k * P:(k + 1) * P], ident[:])
                nc.tensor.transpose(bank[k % 4][:, SEQ:T], x_tok[0:NS, 2, k * P:(k + 1) * P], ident[0:NS, 0:NS]).then_inc(x_turned, 1)
            for g in range(G):
                last = mm(bank[4 + g][0:H, 0:BV], tab[:, g * H:(g + 1) * H], bucket_p[0:NB + 1, g, :], start=True, stop=True)
            last.then_inc(bias_made, 1)
            norm_sums(pe, 0)
            pe.wait_ge(u_ready, 1)
            pe.wait_ge(bias_copied, 1)

            with pe.Fori(0, G) as g:
                for s in range(NZ + 3):
                    if s < NZ:
                        c = s // TPC
                        if s % TPC == 0:
                            pe.wait_ge(ring_full[c % 3], g * 32 + 16 * (c // 3 + 1))
                        if s >= 4:
                            pe.wait_ge(zn_ready, g * NZ + (s - 3))
                        w = slot(c % 3).rearrange("p (k n) -> p k n", k=KT)
                        at = s % TPC * P
                        for k in range(KT):
                            last = mm(z_bank[s % 4][:, 0:T], w[:, k, at:at + P], uT[:, k, :], start=(k == 0), stop=(k == KT - 1))
                        last.then_inc(z_ready, 1)
                    if 1 <= s <= NQK:
                        n = s - 1
                        pe.wait_ge(zsq_ready, g * NQK + (n + 1))
                        if n >= 2:
                            pe.wait_ge(zroot_ready, g * NQK + (n - 1))
                        mm(bank[2 + n % 2][:, 0:T], blockones[:], zsq[:, n % 2, :], start=True, stop=True).then_inc(zsum_ready, 1)
                    if s >= 3:
                        n = s - 3
                        pe.wait_ge(zn_ready, g * NZ + (n + 1))
                        if n >= 2:
                            pe.wait_ge(z_stored, g * NZ + (n - 1))
                        dst = bank[4 + n % 2]
                        if n >= KT:
                            for b in range(2):
                                nc.tensor.transpose(dst[:, b * P:(b + 1) * P], zn[:, n % 4, b * P:(b + 1) * P], ident[:])
                        nc.tensor.transpose(dst[0:NS, 2 * P:3 * P], zn[:, n % 4, SEQ:T], ident[:]).then_inc(z_turned, 1)
                pe.wait_ge(z_stored, g * NZ + NZ)

            pe.wait_ge(scored, G * NS)
            for g in range(G):
                at = g * (P + 1)
                mm(bank[0][:, at:at + P + 1], tabrep[:, g, :, :].rearrange("p b h -> p (b h)"), bucket_s[:, g, :], start=True, stop=False)
                last = mm(bank[0][:, at:at + P], s_keys[:, g, :], ident[:], start=False, stop=True)
            last.then_inc(s_turned, 1)
            pe.wait_ge(p_ready, 1)
            for g in range(G):
                nc.tensor.transpose(bank[1][:, g * BH:(g + 1) * BH], s_rows[:, g, 0:P], ident[:])
                last = nc.tensor.transpose(bank[2][0:NS, g * BH:(g + 1) * BH], p_newm[:, g, :], ident[:])
            last.then_inc(p_turned, 1)
            pe.wait_ge(p_keys_ready, 1)
            pe.wait_ge(v_new_landed, 16)
            for half in range(2):
                for g in range(G):
                    pe.wait_ge(ring_full[g], 16 * (RING_KV + half + 1))
                    for b4 in range(HALF):
                        b = half * HALF + b4
                        rows = slice(b // 2 * 2 * H, (b // 2 + 1) * 2 * H)
                        for a in range(2):
                            at = b4 * D + a * 512
                            last = mm(bank[3 + a][rows, :], p_masked[:, b % 2, g, rows], slot(g)[:, at:at + 512],
                                      start=(half == 0 and g == 0 and b % 2 == 0), stop=(half == 1 and g == G - 1 and b % 2 == 1))
                    last.then_inc(pv_s_ready, 1)
                if half == 0:
                    for rows, first in ((slice(0, BH // 2), False), (slice(BH // 2, BH), True)):
                        for a in range(2):
                            for g in range(G):
                                mm(bank[3 + a][rows, :], p_newT[0:NS, g, rows], v_new[0:NS, g, a * 512:(a + 1) * 512],
                                   start=(first and g == 0), stop=(not first and g == G - 1))
            pe.wait_ge(o_own_ready, 1)
            for j in range(KT):
                last = mm(bank[5][:, j * NS:(j + 1) * NS], o_own[:, j * P:(j + 1) * P], same_batch[:], start=True, stop=True)
            last.then_inc(o_made, 1)

            def step(i, s, live, behind):
                h = i * 4 + s
                if live:
                    u, t = s // 2 % 2, s % 2
                    rows = slice(t * HD, (t + 1) * HD)
                    pe.wait_ge(qk_staged, i * 2 + (s // 2 + 1))
                    if behind:
                        pe.wait_ge(biased, h)
                    for g in range(G):
                        mm(bank[0][:, g * P:(g + 1) * P], q_st[rows, u, g, 0:P], k_st[rows, u, g, 0:P], start=True, stop=True)
                    for g in range(G):
                        at = g % 2 * SEQ
                        last = mm(bank[1 + g // 2][:, at:at + SEQ], q_st[rows, u, g, P:], k_st[rows, u, g, :], start=True, stop=True)
                    last.then_inc(scores_ready, 1)
                if behind >= 2:
                    pe.wait_ge(pt_copied_dve, h - 1)
                    pe.wait_ge(pt_copied_act, h - 1)
                if 1 <= behind <= H:
                    pe.wait_ge(probs_ready, h)
                    for n in range(3 * G):
                        last = nc.tensor.transpose(bank[3 + n // 4][:, n % 4 * P:(n % 4 + 1) * P], probs[:, (s - 1) % 2, n * P:(n + 1) * P], ident[:])
                    last.then_inc(pt_ready, 1)
                if behind >= 2:
                    u, t = (s - 2) // 2 % 2, s % 2
                    rows = slice(t * HD, (t + 1) * HD)
                    pe.wait_ge(v_staged, i * 2 + ((s - 2) // 2 + 1))
                    for g in range(G):
                        mm(bank[6 + u][rows, 0:P], v_st[:, u, 0, g * P + t * HD:g * P + (t + 1) * HD],
                           probsT[:, t, g * P:(g + 1) * P], start=(g == 0), stop=(g == G - 1))
                    for g in range(G):
                        for kb in range(2):
                            n = G + 2 * g + kb
                            last = mm(bank[6 + u][rows, P:2 * P], v_st[:, u, kb, g * P + t * HD:g * P + (t + 1) * HD],
                                      probsT[:, t, n * P:(n + 1) * P], start=(n == G), stop=(n == 3 * G - 1))
                    last.then_inc(pv_ready, 1)

            pe.wait_ge(sample_done, 1)
            for s in range(4):
                step(0, s, True, s)
            with pe.Fori(1, H // 4) as i:
                for s in range(4):
                    step(i, s, True, 4)
            step(H // 4, 0, False, H)
            step(H // 4, 1, False, H + 1)

            pe.wait_ge(o_copied, PAIRS)
            for s in range(2):
                pe.wait_ge(ring_full[s], 16 * (RING_WO + 1))
            for m in range(KT):
                if m >= 2:
                    pe.wait_ge(wo_added, m - 1)
                for f in range(KT):
                    w = slot(f // 4).rearrange("p (k n) -> p k n", k=4)
                    last = mm(bank[m % 2][:, 0:T], w[:, f % 4, m * P:(m + 1) * P], oT[:, f, :], start=(f == 0), stop=(f == KT - 1))
                last.then_inc(wo_ready, 1)

            def router(layer, n_norm):
                pe.wait_ge(u_ready, n_norm + 1)
                for b in range(3):
                    n = P if b < 2 else NS
                    out = bank[6][0:n, b * NR:(b + 1) * NR]
                    for k in range(KT):
                        mm(out, uT[:, k, b * P:b * P + n], wr[:, layer, k, :], start=(k == 0), stop=False)
                    last = mm(out, ones[0:1, 0:n], brow[:, layer, :], start=False, stop=True)
                last.then_inc(logits_made, 1)
                for b in range(3):
                    n = P if b < 2 else NS
                    for k in range(KT):
                        last = nc.tensor.transpose(bank[2 * b + k // 4][0:n, k % 4 * P:(k % 4 + 1) * P], uT[:, k, b * P:b * P + n], ident[:])
                        if k % 4 == 3:
                            last.then_inc(u_turned, 1)
                pe.wait_ge(chosen_ready, layer + 1)
                sizes = (P, P, NS)
                for b in range(3):
                    out = bank[6][0:sizes[b], 64 + b * NE:64 + (b + 1) * NE]
                    for a in range(b + 1):
                        w = tri if a == b else ones
                        mm(out, w[0:sizes[a], 0:sizes[b]], chosen[0:sizes[a], a, :], start=(a == 0), stop=(a == b))
                for a in range(3):
                    last = mm(bank[6][:, 128:128 + NE], ones[0:sizes[a], :], chosen[0:sizes[a], a, :], start=(a == 0), stop=(a == 2))
                last.then_inc(positions_made, 1)
                pe.wait_ge(u_tok_dve, 3 * layer + 3)
                pe.wait_ge(u_tok_act, 3 * layer + 3)

            weights = [(slot(a).rearrange("p (k f) -> p k f", k=KT), slot(b).rearrange("p (k f) -> p k f", k=KT),
                        slot(c).rearrange("p (k f) -> p k f", k=FT)) for a, b, c in SLOTS]

            def one_round(q, p, layer):
                def weights_there(s):
                    pe.wait_ge(ring_full[s], p * 16 + 16 * (layer * NP + FIRST_USES[s] + 1))

                pe.wait_ge(pick_ready, q + 1)
                sizes = (P, P, NS)
                for m in range(KT):
                    for b in range(3):
                        last = mm(bank[m // 4][:, m % 4 * P:(m % 4 + 1) * P], u_tok[0:sizes[b], b, m * P:(m + 1) * P],
                                  pick[0:sizes[b], b, :], start=(b == 0), stop=(b == 2))
                    if m % 4 == 3:
                        last.then_inc(gathered, 1)
                pe.wait_ge(slots_dve, q + 1)
                pe.wait_ge(slots_act, q + 1)
                for b in range(3):
                    last = mm(bank[6][:, b * P:b * P + sizes[b]], pick_gate[0:sizes[b], b, :], ident[0:sizes[b], 0:sizes[b]],
                              start=True, stop=True)
                last.then_inc(place_made, 1)

                def turn_hidden(e):
                    rows = slice(e * CAP, (e + 1) * CAP)
                    pe.wait_ge(hid_rows_ready, q * 2 + (e + 1))
                    for f in range(FT):
                        at = (e * FT + f) * CAP
                        if f == 0:
                            mm(bank[0][:, at:at + CAP], hid_rows[rows, f * P:(f + 1) * P], ident[rows, rows], start=True, stop=True)
                        else:
                            last = nc.tensor.transpose(bank[0][:, at:at + CAP], hid_rows[rows, f * P:(f + 1) * P], ident[rows, rows])
                    last.then_inc(hid_turned, 1)

                def down(e, a):
                    weights_there(SLOTS[e][2])
                    pe.wait_ge(hid_ready, q * 2 + (e + 1))
                    for f in range(FT):
                        last = mm(bank[4 + a][e * CAP:(e + 1) * CAP, :], hid[:, f, e, :], weights[e][2][:, f, a * 512:(a + 1) * 512],
                                  start=(f == 0), stop=(f == FT - 1))
                    return last

                for e in range(2):
                    rows = slice(e * CAP, (e + 1) * CAP)
                    for w in range(2):
                        weights_there(SLOTS[e][w])
                        for k in range(KT):
                            last = mm(bank[2 + w][rows, :], u_slots[:, k, rows], weights[e][w][:, k, :], start=(k == 0), stop=(k == KT - 1))
                        if e == 1 and w == 0:
                            turn_hidden(0)
                    last.then_inc(up_ready[e], 1)
                down(0, 0)
                turn_hidden(1)
                down(0, 1).then_inc(down_even_done, 1)
                down(1, 0).then_inc(y_half, 1)
                down(1, 1).then_inc(y_half, 1)
                pe.wait_ge(place_ready, q + 1)
                for m in range(KT):
                    if m % 4 == 0:
                        pe.wait_ge(y_copied, q * 2 + (m // 4 + 1))
                    if m >= 4:
                        pe.wait_ge(spread_added, q * KT + (m - 3))
                    mm(spread_bank[m % 4][:, 0:T], y_pair[:, m * P:(m + 1) * P], place, start=True, stop=True).then_inc(spread, 1)

            def experts(layer):
                all_rounds(pe, layer, lambda q, p: one_round(q, p, layer))

            norm_sums(pe, 1)
            router(0, 1)
            experts(0)

            norm_sums(pe, 2)
            pe.wait_ge(pool_landed, 16 * 7)
            for k in range(KT):
                last = mm(bank[0][:, k * NS:(k + 1) * NS], state[0:NS * STATE, k * P:(k + 1) * P], state_sum[0:NS * STATE, k // 2, :], start=True, stop=True)
            last.then_inc(state_summed, 1)
            pe.wait_ge(u_ready, 3)
            for k in range(KT):
                last = nc.tensor.transpose(bank[3 + k // 4][0:STATE + NS, k % 4 * P:(k % 4 + 1) * P], uT[:, k, SEQ - STATE:T], ident[:])
                if k % 4 == 3:
                    last.then_inc(pool_turned, 1)
            for m in range(KT):
                gi, ft = m // 2, m % 2
                pe.wait_ge(pooled, gi + 1)
                if m >= 2:
                    pe.wait_ge(pool_y_added, m - 1)
                for ct in range(2):
                    last = mm(bank[1 + m % 2][:, 0:T], pw[:, 2 * gi + ct, ft * P:(ft + 1) * P], pool_z[:, 2 * gi + ct, :], start=(ct == 0), stop=(ct == 1))
                last.then_inc(pool_y_ready, 1)

            norm_sums(pe, 3)
            router(1, 3)
            experts(1)

            pe.wait_ge(layer_added, LAYERS)
            for b in range(3):
                n = P if b < 2 else NS
                for k in range(KT):
                    last = nc.tensor.transpose(bank[2 * b + k // 4][0:n, k % 4 * P:(k % 4 + 1) * P], hT[:, k, b * P:b * P + n], ident[:])
                    if k % 4 == 3:
                        last.then_inc(y_turned, 1)


def constants():
    import math

    import numpy as np

    n_buckets, max_distance, seq, ns = 32, 2048, 256, 8
    exact = n_buckets // 2

    def bucket(dist):
        df = np.maximum(dist, exact).astype(np.float32)
        large = exact + (np.log(df / np.float32(exact)) / np.float32(math.log(max_distance / exact))
                         * np.float32(n_buckets - exact)).astype(np.int32)
        return np.where(dist < exact, dist, np.minimum(large, n_buckets - 1))

    one = np.float32(1)
    dist = 2 * P - 1 - np.arange(3 * P)
    bp = np.zeros((n_buckets + 1, 3, 3 * P), np.float32)
    for g, (w, d) in enumerate(zip(WINDOWS, DILATIONS)):
        ok = (dist >= 0) & (dist <= w) & (dist % d == 0)
        bp[bucket(np.maximum(dist, 0))[ok], g, np.nonzero(ok)[0]] = one
        bp[n_buckets, g, ~ok] = one
    bs = np.zeros((3, n_buckets, P + 1), np.float32)
    for g, d in enumerate(DILATIONS):
        bs[g, bucket((P - np.arange(P + 1)) * d), np.arange(P + 1)] = one
    same = np.repeat(np.eye(ns, dtype=np.float32), P // ns, axis=0)
    rank = np.tile(np.concatenate([16 - np.arange(16), np.arange(64)]).astype(np.float32), (P, 1))
    rank = np.concatenate([rank, np.tile(np.eye(16, dtype=np.float32), (ns, 1))], 1)
    inv = np.stack([one / np.minimum(w, np.arange(seq) + 1).astype(np.float32) for w in POOL_WINDOWS]).astype(np.float32)
    n_state = POOL_WINDOWS[-1] - 1
    ssum = np.zeros((ns, n_state, 4, ns), np.float32)
    for gi, w in enumerate(POOL_WINDOWS):
        for b in range(ns):
            ssum[b, n_state - (w - 1):, gi, b] = one
    return {"c_ident": np.eye(P, dtype=np.float32), "c_bucket_prompt": bp, "c_bucket_sample": bs, "c_same_batch": same,
            "c_rank": rank, "c_inv_count": inv, "c_state_sum": ssum.reshape(ns * n_state, 4, ns),
            "c_tri": np.triu(np.ones((P, P), np.float32))}


_INS = ['x_prompt', 'x_sample', 'cache_kv_w128', 'cache_kv_w512', 'cache_kv_w2048', 'state_pool', 'w_qkv', 'q_norm',
        'k_norm', 'w_o', 'rel_bias', 'attn_norm', 'pool_norm', 'pool_w', 'pool_b', 'pool_scale', 'ffn_norm',
        'router_group_w', 'router_group_b', 'router_expert_w', 'router_expert_b', 'w_gate', 'w_up', 'w_down']
_OUTS = [(1, 256, 1024), (8, 1, 1024), (1, 1, 128, 2, 16, 64), (1, 1, 256, 2, 16, 64), (1, 1, 256, 2, 16, 64),
         (1, 1, 15, 1024), (1, 8, 128, 2, 16, 64), (1, 8, 512, 2, 16, 64), (1, 8, 2048, 2, 16, 64), (1, 8, 15, 1024)]


def kernel(**inputs):
    import numpy as _np
    import concourse.bacc as _bacc
    from concourse import mybir as _mybir
    from concourse.bass_utils import run_bass_kernel_spmd as _run

    nc = _bacc.Bacc("TRN2", target_bir_lowering=False, num_devices=1)
    arrays, args = {}, []
    given = [(n, _np.ascontiguousarray(inputs[n])) for n in _INS] + list(constants().items())
    for name, a in given:
        arrays[f"in_{name}_dram"] = a
        args.append(nc.dram_tensor(f"in_{name}_dram", a.shape, _mybir.dt.from_np(a.dtype), kind="ExternalInput").ap())
    for i, shape in enumerate(_OUTS):
        args.append(nc.dram_tensor(f"out_{i}_dram", shape, _mybir.dt.float32, kind="ExternalOutput").ap())
    build(nc, *args)
    r = _run(nc, [arrays], core_ids=[0])
    return tuple(r.results[0][f"out_{i}_dram"] for i in range(len(_OUTS)))
```
